# Optimizing a Trainium2 kernel written in Bass

```python
import math
import jax, jax.numpy as jnp
from jax import lax
import numpy as np
import jax
import jax.numpy as jnp

D_MODEL = 1024
BATCH = 1
SEQ = 256
DEPTH = 1

N_FOX_HEADS = 8
FOX_HEAD_DIM = 64
FOX_WIDTH = N_FOX_HEADS * FOX_HEAD_DIM
N_DIFF_HEADS = 4
DIFF_QK_DIM = 64
DIFF_V_DIM = 2 * DIFF_QK_DIM
DIFF_QK_WIDTH = N_DIFF_HEADS * 2 * DIFF_QK_DIM
DIFF_WIDTH = N_DIFF_HEADS * DIFF_V_DIM
MIX_WIDTH = FOX_WIDTH + DIFF_WIDTH
IN_SIZES = (FOX_WIDTH, FOX_WIDTH, FOX_WIDTH, N_FOX_HEADS,
            DIFF_QK_WIDTH, DIFF_QK_WIDTH, DIFF_WIDTH)
IN_WIDTH = sum(IN_SIZES)
IN_SPLITS = tuple(int(v) for v in np.cumsum(IN_SIZES)[:-1])
ROPE_THETA = 500000.0
ROPE_DIM = DIFF_QK_DIM // 4
D_FF = 2816
FFN_RESIDUAL_WEIGHT = 0.5
Q_BLOCK = 128
RMS_EPS = 1e-6


def rms_norm(x, g):
    xf = x.astype(jnp.float32)
    y = xf * lax.rsqrt(jnp.mean(xf * xf, axis=-1, keepdims=True) + RMS_EPS)
    return (y * g.astype(jnp.float32)).astype(x.dtype)

def swiglu(x, w_gate, w_up, w_down):
    return (jax.nn.silu(x @ w_gate) * (x @ w_up)) @ w_down

def to_heads(t, n_heads):
    b, s, _ = t.shape
    return t.reshape(b, s, n_heads, -1).transpose(0, 2, 1, 3)

def from_heads(t):
    b, h, s, d = t.shape
    return t.transpose(0, 2, 1, 3).reshape(b, s, h * d)

def partial_rope(t, pos):
    half = ROPE_DIM // 2
    inv_freq = ROPE_THETA ** (-jnp.arange(0, ROPE_DIM, 2, dtype=jnp.float32) / ROPE_DIM)
    ang = pos.astype(jnp.float32)[:, None] * inv_freq[None, :]
    cos, sin = jnp.cos(ang), jnp.sin(ang)
    tf = t.astype(jnp.float32)
    x1, x2, rest = tf[..., :half], tf[..., half:ROPE_DIM], tf[..., ROPE_DIM:]
    out = jnp.concatenate([x1 * cos - x2 * sin, x2 * cos + x1 * sin, rest], axis=-1)
    return out.astype(t.dtype)

def causal_block_attention(q, k, v, log_decay_cum=None):
    seq = q.shape[2]
    scale = q.shape[-1] ** -0.5
    outs = []
    for i in range(seq // Q_BLOCK):
        q0, q1 = i * Q_BLOCK, (i + 1) * Q_BLOCK
        s = jnp.einsum('bhqd,bhkd->bhqk', q[:, :, q0:q1], k[:, :, :q1]).astype(jnp.float32) * scale
        if log_decay_cum is not None:
            s = s + log_decay_cum[:, :, q0:q1, None] - log_decay_cum[:, :, None, :q1]
        mask = jnp.arange(q1)[None, :] <= jnp.arange(q0, q1)[:, None]
        s = jnp.where(mask, s, jnp.finfo(jnp.float32).min)
        p = jax.nn.softmax(s, axis=-1).astype(v.dtype)
        outs.append(jnp.einsum('bhqk,bhkd->bhqd', p, v[:, :, :q1]))
    return jnp.concatenate(outs, axis=2)

def token_mixer(h, w_in, fox_forget_b, lam_q1, lam_k1, lam_q2, lam_k2, subln_g, w_out, layer):
    b, s, _ = h.shape
    pos = jnp.arange(s)
    proj = h @ w_in
    fq, fk, fv, fgate, dq, dk, dv = jnp.split(proj, IN_SPLITS, axis=-1)

    log_f = jax.nn.log_sigmoid(fgate.astype(jnp.float32) + fox_forget_b.astype(jnp.float32))
    c = jnp.cumsum(log_f, axis=1).transpose(0, 2, 1)
    fox_o = causal_block_attention(to_heads(fq, N_FOX_HEADS), to_heads(fk, N_FOX_HEADS),
                                   to_heads(fv, N_FOX_HEADS), c)
    fox_o = from_heads(fox_o)

    dq = dq.reshape(b, s, N_DIFF_HEADS, 2, DIFF_QK_DIM)
    dk = dk.reshape(b, s, N_DIFF_HEADS, 2, DIFF_QK_DIM)
    hd = lambda t: partial_rope(t.transpose(0, 2, 1, 3), pos)
    q1, q2 = hd(dq[..., 0, :]), hd(dq[..., 1, :])
    k1, k2 = hd(dk[..., 0, :]), hd(dk[..., 1, :])
    v = to_heads(dv, N_DIFF_HEADS)
    lam_init = 0.8 - 0.6 * math.exp(-0.3 * layer)
    lam = (jnp.exp(jnp.sum(lam_q1.astype(jnp.float32) * lam_k1.astype(jnp.float32)))
           - jnp.exp(jnp.sum(lam_q2.astype(jnp.float32) * lam_k2.astype(jnp.float32)))
           + lam_init)
    a1 = causal_block_attention(q1, k1, v)
    a2 = causal_block_attention(q2, k2, v)
    diff_o = a1 - lam.astype(a1.dtype) * a2
    diff_o = rms_norm(diff_o, subln_g) * (1.0 - lam_init)
    diff_o = from_heads(diff_o)

    return jnp.concatenate([fox_o, diff_o], axis=-1) @ w_out

def first_inputs(seed: int = 0) -> dict:
    key = jax.random.key(seed)
    ks = jax.random.split(key, 24)
    L = DEPTH
    nrm = lambda k, shape, scale: jax.random.normal(k, shape, jnp.float32) * scale
    gain = lambda k, n: 1.0 + 0.02 * jax.random.normal(k, (L, n), jnp.float32)
    return {
        "x": jax.random.normal(ks[0], (BATCH, SEQ, D_MODEL), jnp.float32),
        "ffn1_pre_g": gain(ks[1], D_MODEL),
        "ffn1_post_g": gain(ks[2], D_MODEL),
        "ffn1_w_gate": nrm(ks[3], (L, D_MODEL, D_FF), D_MODEL ** -0.5),
        "ffn1_w_up": nrm(ks[4], (L, D_MODEL, D_FF), D_MODEL ** -0.5),
        "ffn1_w_down": nrm(ks[5], (L, D_FF, D_MODEL), D_FF ** -0.5),
        "mix_pre_g": gain(ks[6], D_MODEL),
        "mix_post_g": gain(ks[7], D_MODEL),
        "w_in": nrm(ks[8], (L, D_MODEL, IN_WIDTH), D_MODEL ** -0.5),
        "fox_forget_b": nrm(ks[9], (L, N_FOX_HEADS), 0.02),
        "diff_lambda_q1": nrm(ks[10], (L, DIFF_QK_DIM), 0.1),
        "diff_lambda_k1": nrm(ks[11], (L, DIFF_QK_DIM), 0.1),
        "diff_lambda_q2": nrm(ks[12], (L, DIFF_QK_DIM), 0.1),
        "diff_lambda_k2": nrm(ks[13], (L, DIFF_QK_DIM), 0.1),
        "diff_subln_g": gain(ks[14], DIFF_V_DIM),
        "w_out": nrm(ks[15], (L, MIX_WIDTH, D_MODEL), MIX_WIDTH ** -0.5),
        "ffn2_pre_g": gain(ks[16], D_MODEL),
        "ffn2_post_g": gain(ks[17], D_MODEL),
        "ffn2_w_gate": nrm(ks[18], (L, D_MODEL, D_FF), D_MODEL ** -0.5),
        "ffn2_w_up": nrm(ks[19], (L, D_MODEL, D_FF), D_MODEL ** -0.5),
        "ffn2_w_down": nrm(ks[20], (L, D_FF, D_MODEL), D_FF ** -0.5),
    }

def first_block(x, ffn1_pre_g, ffn1_post_g, ffn1_w_gate, ffn1_w_up, ffn1_w_down,
              mix_pre_g, mix_post_g, w_in, fox_forget_b,
              diff_lambda_q1, diff_lambda_k1, diff_lambda_q2, diff_lambda_k2, diff_subln_g,
              w_out, ffn2_pre_g, ffn2_post_g, ffn2_w_gate, ffn2_w_up, ffn2_w_down):
    for l in range(DEPTH):
        f1 = swiglu(rms_norm(x, ffn1_pre_g[l]), ffn1_w_gate[l], ffn1_w_up[l], ffn1_w_down[l])
        x = x + FFN_RESIDUAL_WEIGHT * rms_norm(f1, ffn1_post_g[l])
        m = token_mixer(rms_norm(x, mix_pre_g[l]), w_in[l], fox_forget_b[l],
                        diff_lambda_q1[l], diff_lambda_k1[l], diff_lambda_q2[l], diff_lambda_k2[l],
                        diff_subln_g[l], w_out[l], l)
        x = x + rms_norm(m, mix_post_g[l])
        f2 = swiglu(rms_norm(x, ffn2_pre_g[l]), ffn2_w_gate[l], ffn2_w_up[l], ffn2_w_down[l])
        x = x + FFN_RESIDUAL_WEIGHT * rms_norm(f2, ffn2_post_g[l])
    return x


DEPTH_2 = 2

HEAD_DIM = 64
ROT_DIM = HEAD_DIM // 4
NORM_EPS = 1e-6

SB_HEADS = 4
NSA_HEADS = 8
NSA_GROUPS = 2
NSA_HPG = NSA_HEADS // NSA_GROUPS
NSA_CMP_LEN = 32
NSA_CMP_STRIDE = 16
NSA_CMP_HIDDEN = 2 * HEAD_DIM
NSA_SEL_LEN = 64
NSA_SEL_N = 16
NSA_WINDOW = 512
NSA_FORCED_SCORE = 1.0e4
DSA_HEADS = 4
DSA_IDX_HEADS = 8
DSA_IDX_DIM = 32
DSA_IDX_ROT = DSA_IDX_DIM // 4
DSA_TOPK = 256

SB_W = SB_HEADS * HEAD_DIM
NSA_QW = NSA_HEADS * HEAD_DIM
NSA_KVW = NSA_GROUPS * HEAD_DIM
DSA_QW = DSA_HEADS * HEAD_DIM
IN_WIDTHS = (SB_W, SB_W, SB_W,
             NSA_QW, NSA_KVW, NSA_KVW, NSA_KVW, NSA_KVW, NSA_KVW, NSA_KVW, 3 * NSA_HEADS,
             DSA_QW, HEAD_DIM, HEAD_DIM, DSA_IDX_HEADS * DSA_IDX_DIM, DSA_IDX_DIM, DSA_IDX_HEADS)
D_IN = sum(IN_WIDTHS)


def rms_norm_2(x, g):
    xf = x.astype(jnp.float32)
    y = xf * lax.rsqrt(jnp.mean(xf * xf, axis=-1, keepdims=True) + NORM_EPS)
    return (y * g.astype(jnp.float32)).astype(x.dtype)

def rope_tables(pos, rot_dim):
    inv = ROPE_THETA ** (-jnp.arange(0, rot_dim, 2, dtype=jnp.float32) / rot_dim)
    ang = pos.astype(jnp.float32)[:, None] * inv[None, :]
    return jnp.cos(ang), jnp.sin(ang)

def apply_rope(x, cos, sin):
    half = cos.shape[-1]
    xf = x[..., :2 * half].astype(jnp.float32)
    x1, x2 = xf[..., :half], xf[..., half:]
    c, s = cos[:, None, :], sin[:, None, :]
    rot = jnp.concatenate([x1 * c - x2 * s, x2 * c + x1 * s], axis=-1).astype(x.dtype)
    return jnp.concatenate([rot, x[..., 2 * half:]], axis=-1)

def masked_softmax(s, mask):
    s = jnp.where(mask, s.astype(jnp.float32), -jnp.inf)
    m = jnp.max(s, axis=-1, keepdims=True)
    m = jnp.where(jnp.isfinite(m), m, 0.0)
    p = jnp.exp(s - m)
    den = jnp.sum(p, axis=-1, keepdims=True)
    return p / jnp.where(den > 0, den, 1.0)

def unblock(y):
    n, b, t = y.shape[:3]
    return jnp.moveaxis(y, 0, 1).reshape((b, n * t) + y.shape[3:])

def swiglu_ffn(x, g, w_gu, w_down):
    h = rms_norm_2(x, g)
    gate, up = jnp.split(h @ w_gu, 2, axis=-1)
    return (jax.nn.silu(gate) * up) @ w_down

def stick_breaking_attention(q, k, v):
    B, S, H, d = q.shape
    scale = d ** -0.5
    kh = k.transpose(0, 2, 1, 3)
    vh = v.transpose(0, 2, 1, 3)
    s_pos = jnp.arange(S)

    def block(i):
        q0 = i * Q_BLOCK
        qb = lax.dynamic_slice_in_dim(q, q0, Q_BLOCK, axis=1)
        z = jnp.einsum('bthd,bhsd->bhts', qb, kh).astype(jnp.float32) * scale
        t_pos = q0 + jnp.arange(Q_BLOCK)
        past = s_pos[None, :] < t_pos[:, None]
        log_1m = jnp.where(past, jax.nn.log_sigmoid(-z), 0.0)
        tail = lax.cumsum(log_1m, axis=3, reverse=True) - log_1m
        w = jnp.where(past, jnp.exp(jax.nn.log_sigmoid(z) + tail), 0.0)
        return jnp.einsum('bhts,bhsd->bthd', w.astype(v.dtype), vh)

    return unblock(lax.map(block, jnp.arange(S // Q_BLOCK)))

def nsa_compress(x, pe, w1, w2):
    B, S, G, d = x.shape
    nchunk = S // NSA_CMP_STRIDE
    r = NSA_CMP_LEN // NSA_CMP_STRIDE
    nc = nchunk - r + 1
    chunks = x.reshape(B, nchunk, NSA_CMP_STRIDE, G, d)
    blocks = jnp.concatenate([chunks[:, m:m + nc] for m in range(r)], axis=2)
    blocks = blocks + pe[None, None, :, None, :]
    flat = blocks.transpose(0, 1, 3, 2, 4).reshape(B, nc, G, NSA_CMP_LEN * d)
    return jax.nn.silu(flat @ w1) @ w2

def nsa_attention(q, k_cmp, v_cmp, k_sel, v_sel, k_win, v_win, gate_logits,
                  q_norm, k_norm, pe, w1, w2, cos, sin):
    B, S, _, d = q.shape
    G, hpg, T = NSA_GROUPS, NSA_HPG, Q_BLOCK
    scale = d ** -0.5
    dt = v_sel.dtype
    qg = apply_rope(rms_norm_2(q, q_norm), cos, sin).reshape(B, S, G, hpg, d)
    k_sel = apply_rope(rms_norm_2(k_sel, k_norm[1]), cos, sin)
    k_win = apply_rope(rms_norm_2(k_win, k_norm[2]), cos, sin)
    gates = jax.nn.sigmoid(gate_logits).reshape(B, S, G, hpg, 3)

    kc = rms_norm_2(nsa_compress(k_cmp, pe[0], w1[0], w2[0]), k_norm[0])
    nc = kc.shape[1]
    cmp_start = jnp.arange(nc) * NSA_CMP_STRIDE
    cmp_end = cmp_start + NSA_CMP_LEN - 1
    cos_c, sin_c = rope_tables(cmp_end, ROT_DIM)
    kc = apply_rope(kc, cos_c, sin_c).transpose(0, 2, 1, 3)
    vc = nsa_compress(v_cmp, pe[1], w1[1], w2[1]).transpose(0, 2, 1, 3)

    ns = S // NSA_SEL_LEN
    n_sel = min(NSA_SEL_N, ns)
    ks_blocks = k_sel.reshape(B, ns, NSA_SEL_LEN, G, d).transpose(0, 3, 1, 2, 4)
    vs_blocks = v_sel.reshape(B, ns, NSA_SEL_LEN, G, d).transpose(0, 3, 1, 2, 4)
    sel_start = jnp.arange(ns) * NSA_SEL_LEN
    overlap = ((cmp_start[:, None] < sel_start[None, :] + NSA_SEL_LEN)
               & (cmp_end[:, None] >= sel_start[None, :])).astype(jnp.float32)
    gather_blocks = jax.vmap(jax.vmap(lambda src, ix: src[ix]))

    pad = ((0, 0), (NSA_WINDOW, 0), (0, 0), (0, 0))
    kw_pad = jnp.pad(k_win, pad)
    vw_pad = jnp.pad(v_win, pad)

    def block(i):
        q0 = i * T
        t_pos = q0 + jnp.arange(T)
        qb = lax.dynamic_slice_in_dim(qg, q0, T, axis=1)

        sc = jnp.einsum('btghd,bgcd->bghtc', qb, kc) * scale
        pc = masked_softmax(sc, cmp_end[None, :] <= t_pos[:, None])
        o_cmp = jnp.einsum('bghtc,bgcd->btghd', pc.astype(dt), vc)

        imp = jnp.einsum('bghtc,cn->bgtn', pc, overlap)
        j = jnp.arange(ns)[None, :]
        cur = (t_pos // NSA_SEL_LEN)[:, None]
        visible = j * NSA_SEL_LEN <= t_pos[:, None]
        forced = (j == 0) | (j == cur) | (j == cur - 1)
        score = jnp.where(visible, jnp.where(forced, NSA_FORCED_SCORE, imp), -jnp.inf)
        _, sel = lax.top_k(score, n_sel)
        k_g = gather_blocks(ks_blocks, sel)
        v_g = gather_blocks(vs_blocks, sel).reshape(B, G, T, n_sel * NSA_SEL_LEN, d)
        tok = sel[..., None] * NSA_SEL_LEN + jnp.arange(NSA_SEL_LEN)
        smask = (tok <= t_pos[:, None, None]).reshape(B, G, 1, T, n_sel * NSA_SEL_LEN)
        ss = jnp.einsum('btghd,bgtnld->bghtnl', qb, k_g) * scale
        ps = masked_softmax(ss.reshape(B, G, hpg, T, n_sel * NSA_SEL_LEN), smask)
        o_sel = jnp.einsum('bghtm,bgtmd->btghd', ps.astype(dt), v_g)

        kwb = lax.dynamic_slice_in_dim(kw_pad, q0, T + NSA_WINDOW, axis=1)
        vwb = lax.dynamic_slice_in_dim(vw_pad, q0, T + NSA_WINDOW, axis=1)
        s_abs = q0 - NSA_WINDOW + jnp.arange(T + NSA_WINDOW)
        wmask = ((s_abs[None, :] <= t_pos[:, None]) & (s_abs[None, :] > t_pos[:, None] - NSA_WINDOW)
                 & (s_abs[None, :] >= 0))
        sw = jnp.einsum('btghd,bsgd->bghts', qb, kwb) * scale
        pw = masked_softmax(sw, wmask)
        o_win = jnp.einsum('bghts,bsgd->btghd', pw.astype(dt), vwb)

        g = lax.dynamic_slice_in_dim(gates, q0, T, axis=1)
        return g[..., 0:1] * o_cmp + g[..., 1:2] * o_sel + g[..., 2:3] * o_win

    out = unblock(lax.map(block, jnp.arange(S // T)))
    return out.reshape(B, S, NSA_HEADS * d)

def dsa_attention(q, k, v, iq, ik, iw, q_norm, k_norm, cos, sin, cos_i, sin_i):
    B, S, _, d = q.shape
    T = Q_BLOCK
    scale = d ** -0.5
    dt = v.dtype
    top_k = min(DSA_TOPK, S // 4)
    q = apply_rope(rms_norm_2(q, q_norm), cos, sin)
    k = apply_rope(rms_norm_2(k[:, :, None, :], k_norm), cos, sin)[:, :, 0, :]
    iq = apply_rope(iq, cos_i, sin_i)
    ik = apply_rope(ik[:, :, None, :], cos_i, sin_i)[:, :, 0, :]
    iw = iw.astype(jnp.float32) * (DSA_IDX_HEADS ** -0.5) * (DSA_IDX_DIM ** -0.5)
    s_pos = jnp.arange(S)
    gather_rows = jax.vmap(lambda src, ix: src[ix])

    def block(i):
        q0 = i * T
        t_pos = q0 + jnp.arange(T)
        qi = lax.dynamic_slice_in_dim(iq, q0, T, axis=1)
        wi = lax.dynamic_slice_in_dim(iw, q0, T, axis=1)
        logits = jax.nn.relu(jnp.einsum('bthd,bsd->bths', qi, ik).astype(jnp.float32))
        score = jnp.einsum('bths,bth->bts', logits, wi)
        score = jnp.where(s_pos[None, None, :] <= t_pos[None, :, None], score, -jnp.inf)
        _, idx = lax.top_k(score, top_k)
        kg = gather_rows(k, idx)
        vg = gather_rows(v, idx)
        qb = lax.dynamic_slice_in_dim(q, q0, T, axis=1)
        sc = jnp.einsum('bthd,btkd->bhtk', qb, kg) * scale
        p = masked_softmax(sc, (idx <= t_pos[None, :, None])[:, None])
        return jnp.einsum('bhtk,btkd->bthd', p.astype(dt), vg)

    out = unblock(lax.map(block, jnp.arange(S // T)))
    return out.reshape(B, S, DSA_HEADS * d)

def hybrid_mixer(h, w_in, w_gate, nsa_q_norm, nsa_k_norm, nsa_cmp_pe, nsa_cmp_w1, nsa_cmp_w2,
                 dsa_q_norm, dsa_k_norm, w_br_a, w_br_b, w_br_c, w_out, cos, sin, cos_i, sin_i):
    B, S, _ = h.shape
    offs = np.cumsum(IN_WIDTHS)[:-1].tolist()
    (sb_q, sb_k, sb_v, nq, nkc, nvc, nks, nvs, nkw, nvw, ngate,
     dq, dk, dv, iq, ik, iw) = jnp.split(h @ w_in, offs, axis=-1)

    def heads(t, n, d):
        return t.reshape(B, S, n, d)

    o_a = stick_breaking_attention(heads(sb_q, SB_HEADS, HEAD_DIM), heads(sb_k, SB_HEADS, HEAD_DIM),
                                   heads(sb_v, SB_HEADS, HEAD_DIM)).reshape(B, S, SB_W)
    kv = lambda t: heads(t, NSA_GROUPS, HEAD_DIM)
    o_b = nsa_attention(heads(nq, NSA_HEADS, HEAD_DIM), kv(nkc), kv(nvc), kv(nks), kv(nvs), kv(nkw), kv(nvw),
                        heads(ngate, NSA_HEADS, 3), nsa_q_norm, nsa_k_norm, nsa_cmp_pe, nsa_cmp_w1, nsa_cmp_w2,
                        cos, sin)
    o_c = dsa_attention(heads(dq, DSA_HEADS, HEAD_DIM), dk, dv, heads(iq, DSA_IDX_HEADS, DSA_IDX_DIM), ik, iw,
                        dsa_q_norm, dsa_k_norm, cos, sin, cos_i, sin_i)

    g_a, g_b, g_c = jnp.split(jax.nn.sigmoid(h @ w_gate), 3, axis=-1)
    merged = g_a * (o_a @ w_br_a) + g_b * (o_b @ w_br_b) + g_c * (o_c @ w_br_c)
    return merged @ w_out

def second_inputs(seed: int = 0) -> dict:
    key = jax.random.key(seed)
    ks = jax.random.split(key, 21)
    f32 = jnp.float32

    def normal(k, shape, scale):
        return jax.random.normal(k, shape, f32) * scale

    def gain(k, shape):
        return 1.0 + 0.02 * jax.random.normal(k, shape, f32)

    D, L = D_MODEL, DEPTH_2
    cmp_in = NSA_CMP_LEN * HEAD_DIM
    return {
        "x": jax.random.normal(ks[0], (BATCH, SEQ, D), f32),
        "ffn1_norm": gain(ks[1], (L, D)),
        "ffn1_w_gu": normal(ks[2], (L, D, 2 * D_FF), D ** -0.5),
        "ffn1_w_down": normal(ks[3], (L, D_FF, D), D_FF ** -0.5),
        "mix_norm": gain(ks[4], (L, D)),
        "w_in": normal(ks[5], (L, D, D_IN), D ** -0.5),
        "w_gate": normal(ks[6], (L, D, 3 * D), D ** -0.5),
        "nsa_q_norm": gain(ks[7], (L, HEAD_DIM)),
        "nsa_k_norm": gain(ks[8], (L, 3, HEAD_DIM)),
        "nsa_cmp_pe": normal(ks[9], (L, 2, NSA_CMP_LEN, HEAD_DIM), 0.1),
        "nsa_cmp_w1": normal(ks[10], (L, 2, cmp_in, NSA_CMP_HIDDEN), cmp_in ** -0.5),
        "nsa_cmp_w2": normal(ks[11], (L, 2, NSA_CMP_HIDDEN, HEAD_DIM), NSA_CMP_HIDDEN ** -0.5),
        "dsa_q_norm": gain(ks[12], (L, HEAD_DIM)),
        "dsa_k_norm": gain(ks[13], (L, HEAD_DIM)),
        "w_br_a": normal(ks[14], (L, SB_W, D), SB_W ** -0.5),
        "w_br_b": normal(ks[15], (L, NSA_QW, D), NSA_QW ** -0.5),
        "w_br_c": normal(ks[16], (L, DSA_QW, D), DSA_QW ** -0.5),
        "w_out": normal(ks[17], (L, D, D), D ** -0.5),
        "ffn2_norm": gain(ks[18], (L, D)),
        "ffn2_w_gu": normal(ks[19], (L, D, 2 * D_FF), D ** -0.5),
        "ffn2_w_down": normal(ks[20], (L, D_FF, D), D_FF ** -0.5),
    }

def second_block(x, ffn1_norm, ffn1_w_gu, ffn1_w_down, mix_norm, w_in, w_gate, nsa_q_norm, nsa_k_norm,
              nsa_cmp_pe, nsa_cmp_w1, nsa_cmp_w2, dsa_q_norm, dsa_k_norm, w_br_a, w_br_b, w_br_c, w_out,
              ffn2_norm, ffn2_w_gu, ffn2_w_down):
    S = x.shape[1]
    pos = jnp.arange(S)
    cos, sin = rope_tables(pos, ROT_DIM)
    cos_i, sin_i = rope_tables(pos, DSA_IDX_ROT)
    for l in range(DEPTH_2):
        x = x + 0.5 * swiglu_ffn(x, ffn1_norm[l], ffn1_w_gu[l], ffn1_w_down[l])
        h = rms_norm_2(x, mix_norm[l])
        x = x + hybrid_mixer(h, w_in[l], w_gate[l], nsa_q_norm[l], nsa_k_norm[l], nsa_cmp_pe[l],
                             nsa_cmp_w1[l], nsa_cmp_w2[l], dsa_q_norm[l], dsa_k_norm[l],
                             w_br_a[l], w_br_b[l], w_br_c[l], w_out[l], cos, sin, cos_i, sin_i)
        x = x + 0.5 * swiglu_ffn(x, ffn2_norm[l], ffn2_w_gu[l], ffn2_w_down[l])
    return x


def setup_inputs(seed=0):
    out = dict(first_inputs(seed))
    for name, value in second_inputs(seed + 1).items():
        if name != "x":
            out[name + "_2"] = value
    return out


def reference(
    x, ffn1_pre_g, ffn1_post_g, ffn1_w_gate, ffn1_w_up, ffn1_w_down, mix_pre_g, mix_post_g,
    w_in, fox_forget_b, diff_lambda_q1, diff_lambda_k1, diff_lambda_q2, diff_lambda_k2,
    diff_subln_g, w_out, ffn2_pre_g, ffn2_post_g, ffn2_w_gate, ffn2_w_up, ffn2_w_down,
    ffn1_norm_2, ffn1_w_gu_2, ffn1_w_down_2, mix_norm_2, w_in_2, w_gate_2, nsa_q_norm_2,
    nsa_k_norm_2, nsa_cmp_pe_2, nsa_cmp_w1_2, nsa_cmp_w2_2, dsa_q_norm_2, dsa_k_norm_2,
    w_br_a_2, w_br_b_2, w_br_c_2, w_out_2, ffn2_norm_2, ffn2_w_gu_2, ffn2_w_down_2,
):
    x = first_block(
        x, ffn1_pre_g, ffn1_post_g, ffn1_w_gate, ffn1_w_up, ffn1_w_down, mix_pre_g, mix_post_g,
        w_in, fox_forget_b, diff_lambda_q1, diff_lambda_k1, diff_lambda_q2, diff_lambda_k2,
        diff_subln_g, w_out, ffn2_pre_g, ffn2_post_g, ffn2_w_gate, ffn2_w_up, ffn2_w_down,
    )
    return second_block(
        x, ffn1_norm_2, ffn1_w_gu_2, ffn1_w_down_2, mix_norm_2, w_in_2, w_gate_2, nsa_q_norm_2,
        nsa_k_norm_2, nsa_cmp_pe_2, nsa_cmp_w1_2, nsa_cmp_w2_2, dsa_q_norm_2, dsa_k_norm_2,
        w_br_a_2, w_br_b_2, w_br_c_2, w_out_2, ffn2_norm_2, ffn2_w_gu_2, ffn2_w_down_2,
    )


_drawn_inputs = setup_inputs


def setup_inputs(seed=0):
    import zlib

    import numpy as np

    out = dict(_drawn_inputs(seed))
    spreads = {}
    factors = {'ffn1_post_g': 3.334,
     'mix_post_g': 3.116,
     'fox_forget_b': 8.0,
     'diff_lambda_q1': 8.0,
     'diff_subln_g': 3.782,
     'ffn2_pre_g': 4.312,
     'ffn2_post_g': 5.721,
     'ffn1_norm_2': 5.329,
     'mix_norm_2': 3.568,
     'nsa_q_norm_2': 8.0,
     'nsa_k_norm_2': 8.0,
     'nsa_cmp_pe_2': 3.966,
     'dsa_q_norm_2': 8.0,
     'dsa_k_norm_2': 8.0,
     'ffn2_norm_2': 6.838}
    for name, (base, spread) in spreads.items():
        noise = np.random.default_rng([zlib.crc32(name.encode()), seed]).standard_normal(out[name].shape)
        drawn = base * np.exp(spread * noise) if base else spread * noise
        out[name] = jnp.asarray(drawn.astype(out[name].dtype))
    for name, factor in factors.items():
        out[name] = (out[name] * factor).astype(out[name].dtype)
    return out
```

```python
from contextlib import ExitStack

import numpy as np

import concourse.bass as bass
from concourse import mybir

F32 = mybir.dt.float32
F32R = mybir.dt.float32r
BF16 = mybir.dt.bfloat16
ALU = mybir.AluOpType
ACT = mybir.ActivationFunctionType
AX = mybir.AxisListType

P = 128
S = 256
NT = S // P
D = 1024
KC = D // P
DFF = 2816
STEP_F = 256
STEPS = DFF // STEP_F
UNIT = 2048
SLOTS = 3
EPS = 1e-6
NEG = -1.0e30
TAKEN = -3.0e38
HD = 64
SCALE = HD ** -0.5
STAGES = 9
FIRST_STAGE = 0


class Chain:

    def __init__(self, eng, sem):
        self.eng, self.sem, self.n = eng, sem, 0

    def __call__(self, ins):
        ins.then_inc(self.sem, 1)
        self.n += 1

    def wait(self):
        self.eng.wait_ge(self.sem, self.n)


def const_arrays():
    j = np.arange(P)[:, None]
    t = np.arange(P)[None, :]
    cols = {}
    cols["ident"] = np.eye(P)
    cols["cumsum"] = (j <= t) * 1.0
    cols["ones"] = np.ones((P, P))
    cols["ones_neg"] = -np.ones((P, P))
    cols["tail_neg"] = (j >= t) * -1.0
    cols["past"] = (j < t) * 1.0
    cols["causal"] = (t > j) * NEG

    def rope(pos, dim):
        inv = np.float32(500000.0) ** (-np.arange(0, dim, 2, dtype=np.float32) / np.float32(dim))
        ang = pos.astype(np.float32)[:, None] * inv.astype(np.float32)[None, :]
        return np.cos(ang.astype(np.float32)), np.sin(ang.astype(np.float32))

    pos = np.arange(S)
    for name, dim in (("16", 16), ("8", 8)):
        c, s = rope(pos, dim)
        for nm, v in (("cos", c), ("sin", s)):
            cols[nm + name] = v.reshape(NT, P, dim // 2).transpose(1, 0, 2).reshape(P, -1)
    nc_blocks = S // 16 - 1
    c, s = rope(np.arange(nc_blocks) * 16 + 31, 16)
    for nm, v in (("coscmp", c), ("sincmp", s)):
        full = np.zeros((P, 8))
        full[:2 * nc_blocks] = np.tile(v, (2, 1))
        cols[nm] = full
    end = np.arange(nc_blocks) * 16 + 31
    vis = (end[None, None, :] <= (np.arange(NT)[None, :, None] * P + np.arange(P)[:, None, None]))
    cols["cmpvis"] = (vis * 1.0).reshape(P, -1)
    cols["cmpbias"] = ((~vis) * NEG).reshape(P, -1)
    bd = np.zeros((P, 8))
    for h in range(8):
        bd[h * nc_blocks:(h + 1) * nc_blocks, h] = 1.0
    cols["headdiag"] = bd
    place, at = {}, 0
    for name, v in cols.items():
        place[name] = (at, v.shape[1])
        at += v.shape[1]
    table = np.concatenate([v for v in cols.values()] + [(j >= t) * NEG], axis=1).astype(np.float32)
    return table, place


def build(nc, A, place, out):
    with ExitStack() as ctx:
        sems = {}

        def sem(name):
            if name not in sems:
                sems[name] = ctx.enter_context(nc.semaphore(name))
            return sems[name]

        def sb(name, shape, dt=F32):
            return ctx.enter_context(nc.sbuf_tensor(name, shape, dt))

        raw = [sb(f"raw{i}", [P, UNIT]) for i in range(SLOTS)]
        w_hi = [sb(f"w_hi{i}", [P, UNIT], F32R) for i in range(SLOTS)]
        w_lo = [sb(f"w_lo{i}", [P, UNIT], F32R) for i in range(SLOTS)]
        aT_hi = sb("aT_hi", [P, KC, S], F32R)
        aT_lo = sb("aT_lo", [P, KC, S], F32R)
        act_hi = [sb(f"act_hi{i}", [P, 2, S], F32R) for i in range(2)]
        act_lo = [sb(f"act_lo{i}", [P, 2, S], F32R) for i in range(2)]
        x = sb("x", [P, NT, D])
        tmp = sb("tmp", [P, 2304])
        qk_t = sb("qk_t", [P, 17, S])
        consts = sb("consts", [P, max(a + w for a, w in place.values())])
        cbf = sb("cbf", [P, 3 * P], BF16)
        gains = sb("gains", [P, NGAIN, KC])
        stats = sb("stats", [P, 96])
        gate_or_gain = sb("gate_or_gain", [P, NT, 3 * D])
        proj = sb("proj", [P, NT, 3080])
        o_all = sb("o_all", [P, NT, D])
        p_buf = sb("p_buf", [P, 2, 2, 384])
        pt_buf = sb("pt_buf", [P, 2, 2, 384])
        sb_mask = sb("sel_mask", [P, 3 * P], BF16)
        small = sb("small", [P, 700])
        ps = ctx.enter_context(nc.psum_tensor("ps", [P, 8, 512], F32))

        xn = qk_t[:, 0:8, :].rearrange("p a b -> p (a b)").rearrange("p (t d) -> p t d", t=NT)
        post_gain = gate_or_gain[:, 1, 0:D]
        sg = [tmp[:, i * 512:(i + 1) * 512].rearrange("p (f s) -> p f s", f=2) for i in range(2)]
        minus_half = stats[:, 95:96]

        def const(name, rows=P):
            a, w = place[name]
            return consts[0:rows, a:a + w]

        ident = const("ident")
        ident_bf = cbf[:, 0:P]
        causal_bf = cbf[:, P:2 * P]
        notpast_bf = cbf[:, 2 * P:3 * P]

        def acc(t):
            return ps[:, 2 * t:2 * t + 2, :].rearrange("p b n -> p (b n)")

        def gu(par):
            return ps[:, 4 + 2 * par:6 + 2 * par, :].rearrange("p f (g s) -> p f g s", g=2)

        def tp(b):
            return ps[:, 4 + b, :].rearrange("p (c s) -> p c s", c=2)

        raw_loaded = [sem(f"raw_loaded{i}") for i in range(SLOTS)]
        hi_ready, lo_ready, unit_used = sem("hi_ready"), sem("lo_ready"), sem("unit_used")
        silu_ready, act_ready = sem("silu_ready"), sem("act_ready")
        act_hi_ready, act_lo_ready = sem("act_hi_ready"), sem("act_lo_ready")
        ss_ready, rstd_ready, x_ready = sem("ss_ready"), sem("rstd_ready"), sem("x_ready")
        xn_ready, tp_done, tmp_ready = sem("xn_ready"), sem("tp_done"), sem("tmp_ready")
        aT_hi_ready, aT_ready = sem("aT_hi_ready"), sem("aT_ready")
        const_loaded, x_loaded, gain_loaded, stored = (sem("const_loaded"), sem("x_loaded"),
                                                       sem("gain_loaded"), sem("stored"))

        phases = PLAN[FIRST_STAGE:STAGES]
        n_units = 0
        n_b = n_item = n_proj = n_mix2 = 0
        n_x = n_t = n_ss = n_post = steps = 0
        info = []
        for ph in phases:
            ph = dict(ph)
            ph["u0"], ph["t0"], ph["x0"], ph["ss0"], ph["s0"], ph["post0"] = n_units, n_t, n_x, n_ss, steps, n_post
            ph["B0"], ph["item0"], ph["proj0"], ph["mix2_before"] = n_b, n_item, n_proj, n_mix2
            kind = ph["kind"]
            n_b += {"ffn": 0, "mix1": 8, "mix2": 10}[kind]
            n_item += {"ffn": 0, "mix1": 16, "mix2": 18}[kind]
            n_proj += {"ffn": 0, "mix1": 13, "mix2": 23}[kind]
            n_mix2 += kind == "mix2"
            n_units += {"ffn": 3 * STEPS, "mix1": UNITS1, "mix2": UNITS2}[kind]
            n_t += {"ffn": 1, "mix1": 2, "mix2": 3}[kind]
            n_x += 2
            n_ss += 2 + (2 if ph["post"] else 0)
            n_post += 1 if ph["post"] else 0
            steps += STEPS if kind == "ffn" else 0
            info.append(ph)

        def raw_count(n):
            return 16 * (n // SLOTS + 1)

        def load(sp, n, src, slot=None):
            k = n % SLOTS if slot is None else slot
            if slot is not None or n >= SLOTS:
                sp.wait_ge(lo_ready, n - (SLOTS - 1))
            width = 1
            for w in src.shape[1:]:
                width *= w
            dst = raw[k][:, 0:width]
            if len(src.shape) == 3:
                dst = dst.rearrange("p (a b) -> p a b", a=src.shape[1])
            sp.dma_start(dst, src).then_inc(raw_loaded[k], 16)

        def split_hi(act, n, width=UNIT, slot=None, loads=None):
            k = n % SLOTS if slot is None else slot
            if slot is None and n >= n_units:
                return
            act.wait_ge(raw_loaded[k], raw_count(n) if loads is None else 16 * loads)
            if slot is not None or n >= SLOTS:
                act.wait_ge(unit_used, n - (SLOTS - 1))
            nc.scalar.activation(w_hi[k][:, 0:width], raw[k][:, 0:width], ACT.Copy).then_inc(hi_ready, 1)

        def split_lo(dve, n, width=UNIT, slot=None):
            k = n % SLOTS if slot is None else slot
            if slot is None and n >= n_units:
                return
            dve.wait_ge(hi_ready, n + 1)
            nc.vector.tensor_tensor(w_lo[k][:, 0:width], raw[k][:, 0:width],
                                    w_hi[k][:, 0:width].bitcast(F32), ALU.subtract).then_inc(lo_ready, 1)

        def act_prenorm(act, ph):
            for t in range(NT):
                act.wait_ge(x_ready, ph["x0"] + t + 1)
                c = ph["ss0"] + t
                nc.scalar.activation(xn[:, t, :], x[:, t, :], ACT.Square,
                                     accum_out=stats[:, c:c + 1]).then_inc(ss_ready, 1)

        def pool_rstd(pool, chain, first, n=2, width=D):
            for c in range(first, first + n):
                pool.wait_ge(ss_ready, c + 1)
                chain(nc.gpsimd.tensor_scalar(stats[:, c:c + 1], stats[:, c:c + 1], 1.0 / width, EPS,
                                              ALU.mult, ALU.add))
                chain.wait()
                nc.gpsimd.tensor_tensor(stats[:, c:c + 1], stats[:, c:c + 1], minus_half, ALU.pow)\
                    .then_inc(rstd_ready, 1)

        def dve_prenorm(dve, ph):
            for t in range(NT):
                c = ph["ss0"] + t
                dve.wait_ge(rstd_ready, c + 1)
                nc.vector.tensor_scalar(xn[:, t, :], x[:, t, :], stats[:, c:c + 1], None, ALU.mult)\
                    .then_inc(xn_ready, 1)

        def pe_transpose(pe, inst, src):
            for t in range(NT):
                pe.wait_ge(xn_ready, 2 * inst + t + 1)
                for b in range(4):
                    for c in (b, b + 4):
                        last = nc.tensor.transpose(tp(b)[:, c // 4, t * P:(t + 1) * P],
                                                   src[:, t, c * P:(c + 1) * P], ident)
                    if t == NT - 1:
                        last.then_inc(tp_done, 1)

        def dve_transposed(dve, inst, gain=None):
            for b in range(4):
                dve.wait_ge(tp_done, 4 * inst + b + 1)
                dst = tmp[:, b * 512:(b + 1) * 512].rearrange("p (c s) -> p c s", c=2)
                if gain is None:
                    nc.vector.tensor_copy(dst, tp(b)).then_inc(tmp_ready, 1)
                else:
                    nc.vector.tensor_tensor(dst, tp(b), gains[:, gain, b:KC:4].unsqueeze(2)
                                            .broadcast_to([P, 2, S]), ALU.mult).then_inc(tmp_ready, 1)
            for b in range(4):
                dve.wait_ge(aT_hi_ready, 4 * inst + b + 1)
                nc.vector.tensor_tensor(aT_lo[:, b:KC:4, :],
                                        tmp[:, b * 512:(b + 1) * 512].rearrange("p (c s) -> p c s", c=2),
                                        aT_hi[:, b:KC:4, :].bitcast(F32), ALU.subtract).then_inc(aT_ready, 1)

        def act_transposed(act, inst):
            for b in range(4):
                act.wait_ge(tmp_ready, 4 * inst + b + 1)
                nc.scalar.activation(aT_hi[:, b:KC:4, :],
                                     tmp[:, b * 512:(b + 1) * 512].rearrange("p (c s) -> p c s", c=2),
                                     ACT.Copy).then_inc(aT_hi_ready, 1)

        def act_post(act, ph, last_unit):
            act.wait_ge(unit_used, last_unit + 1)
            for t in range(NT):
                c = ph["ss0"] + 2 + t
                nc.scalar.activation(xn[:, t, :], acc(t), ACT.Square,
                                     accum_out=stats[:, c:c + 1]).then_inc(ss_ready, 1)

        def dve_post(dve, chain, ph, last_unit):
            dve.wait_ge(unit_used, last_unit + 1)
            if ph["post"]:
                dve.wait_ge(gain_loaded, 16 * (ph["post0"] + 1))
            for t in range(NT):
                src, weight = acc(t), ph["weight"]
                if ph["post"]:
                    c = ph["ss0"] + 2 + t
                    dve.wait_ge(rstd_ready, c + 1)
                    chain(nc.vector.scalar_tensor_tensor(xn[:, t, :], acc(t), stats[:, c:c + 1], post_gain,
                                                         ALU.mult, ALU.mult))
                    chain.wait()
                    src = xn[:, t, :]
                nc.vector.scalar_tensor_tensor(x[:, t, :], src, weight, x[:, t, :], ALU.mult, ALU.add)\
                    .then_inc(x_ready, 1)

        def ffn_src(ph):
            if ph["gu"] is None:
                wg, wu = A[ph["gate"]][ph["l"]], A[ph["up"]][ph["l"]]
            else:
                both = A[ph["gu"]][ph["l"]]
                wg, wu = both[:, 0:DFF], both[:, DFF:2 * DFF]
            return (wg.rearrange("(k p) f -> p k f", p=P), wu.rearrange("(k p) f -> p k f", p=P),
                    A[ph["down"]][ph["l"]].rearrange("(c p) n -> p c n", p=P))

        def sp_ffn(sp, ph):
            wg, wu, wd = ffn_src(ph)
            u0 = ph["u0"]
            load(sp, u0, wg[:, :, 0:STEP_F])
            load(sp, u0 + 1, wu[:, :, 0:STEP_F])
            first = 1
            if u0 == 0:
                load(sp, 2, wg[:, :, STEP_F:2 * STEP_F])
                load(sp, 3, wu[:, :, STEP_F:2 * STEP_F])
                load(sp, 4, wd[:, 0:2, :])
                first = 2
            with sp.Fori(first, STEPS) as s:
                load(sp, 3 * s + (u0 - 1), wg[:, :, bass.ds(s * STEP_F, STEP_F)], slot=(u0 - 1) % SLOTS)
                load(sp, 3 * s + u0, wu[:, :, bass.ds(s * STEP_F, STEP_F)], slot=u0 % SLOTS)
                load(sp, 3 * s + (u0 + 1), wd[:, bass.ds(2 * s - 2, 2), :], slot=(u0 + 1) % SLOTS)
            load(sp, u0 + 3 * STEPS - 1, wd[:, 2 * STEPS - 2:2 * STEPS, :])

        def pe_gate_up(pe, ph, s, par, in_loop=False):
            u0 = ph["u0"]
            if in_loop or ph["s0"] + s >= 2:
                pe.wait_ge(act_ready, s + (ph["s0"] - 1))
            for g in range(2):
                n = 3 * s + (u0 - 1 + g) if in_loop or s > 0 else u0 + g
                slot = (u0 - 1 + g) % SLOTS if in_loop or s > 0 else (u0 + g) % SLOTS
                pe.wait_ge(lo_ready, n + 1)
                hi = w_hi[slot][:, :].rearrange("p (k f) -> p k f", k=KC)
                lo = w_lo[slot][:, :].rearrange("p (k f) -> p k f", k=KC)
                for f in range(2):
                    dst = gu(par)[:, f, g, :]
                    for k in range(KC):
                        cols = slice(f * P, (f + 1) * P)
                        nc.tensor.matmul(dst, hi[:, k, cols], aT_hi[:, k, :], start=k == 0, stop=False)
                        nc.tensor.matmul(dst, hi[:, k, cols], aT_lo[:, k, :], start=False, stop=False)
                        last = nc.tensor.matmul(dst, lo[:, k, cols], aT_hi[:, k, :], start=False,
                                                stop=k == KC - 1)
                last.then_inc(unit_used, 1)

        def pe_rows(pe, n, slot, hi_a, lo_a, banks, first, last):
            pe.wait_ge(lo_ready, n + 1)
            hi = w_hi[slot][:, :].rearrange("p (c n) -> p c n", c=2)
            lo = w_lo[slot][:, :].rearrange("p (c n) -> p c n", c=2)
            for c in range(2):
                for t in range(NT):
                    toks = slice(t * P, (t + 1) * P)
                    for h in range(2):
                        dst = ps[:, banks + 2 * t + h, :]
                        cols = slice(h * 512, (h + 1) * 512)
                        nc.tensor.matmul(dst, hi_a[:, c, toks], hi[:, c, cols], start=first and c == 0, stop=False)
                        nc.tensor.matmul(dst, hi_a[:, c, toks], lo[:, c, cols], start=False, stop=False)
                        mm = nc.tensor.matmul(dst, lo_a[:, c, toks], hi[:, c, cols], start=False,
                                              stop=last and c == 1)
            mm.then_inc(unit_used, 1)

        def pe_down(pe, ph, s, par, in_loop=False, first=False, last=False):
            u0 = ph["u0"]
            n = 3 * s + (u0 + 1) if not last else u0 + 3 * STEPS - 1
            pe.wait_ge(act_lo_ready, s + ph["s0"])
            pe_rows(pe, n, (u0 + 1) % SLOTS if not last else n % SLOTS, act_hi[par], act_lo[par], 0, first, last)

        def pe_ffn(pe, ph):
            pe_transpose(pe, ph["t0"], xn)
            pe.wait_ge(aT_ready, 4 * (ph["t0"] + 1))
            pe_gate_up(pe, ph, 0, 0)
            pe_gate_up(pe, ph, 1, 1)
            pe_down(pe, ph, 1, 0, first=True)
            with pe.Fori(2, STEPS - 1, 2) as s:
                for j in range(2):
                    pe_gate_up(pe, ph, s + j, j, in_loop=True)
                    pe_down(pe, ph, s + j, 1 - j, in_loop=True)
            pe_gate_up(pe, ph, STEPS - 1, 0)
            pe_down(pe, ph, STEPS - 1, 1)
            pe_down(pe, ph, STEPS, 0, last=True)

        def act_step(act, ph, s, par, in_loop=False):
            u0, s0 = ph["u0"], ph["s0"]

            def split(d):
                n = 3 * s + (u0 + d)
                if in_loop:
                    slot = (u0 + d) % SLOTS
                    split_hi(act, n, slot=slot, loads=s + (u0 + d - slot) // SLOTS + 1)
                else:
                    split_hi(act, n, width=width_of(n))
            split(2)
            act.wait_ge(unit_used, (3 * s + u0 + 1) if in_loop or s > 0 else u0 + 2)
            if in_loop or s0 + s >= 2:
                act.wait_ge(act_lo_ready, s + (s0 - 1))
            nc.scalar.activation(sg[par], gu(par)[:, :, 0, :], ACT.Silu).then_inc(silu_ready, 1)
            split(3)
            act.wait_ge(act_ready, s + (s0 + 1))
            nc.scalar.activation(act_hi[par][:, :, :], sg[par], ACT.Copy).then_inc(act_hi_ready, 1)
            split(4)

        def dve_step(dve, ph, s, par, in_loop=False):
            u0, s0 = ph["u0"], ph["s0"]

            def split(d):
                n = 3 * s + (u0 + d)
                if in_loop:
                    split_lo(dve, n, slot=(u0 + d) % SLOTS)
                else:
                    split_lo(dve, n, width=width_of(n))
            split(2)
            dve.wait_ge(silu_ready, s + (s0 + 1))
            nc.vector.tensor_tensor(sg[par], sg[par], gu(par)[:, :, 1, :], ALU.mult).then_inc(act_ready, 1)
            dve.wait_ge(act_hi_ready, s + (s0 + 1))
            nc.vector.tensor_tensor(act_lo[par][:, :, :], sg[par], act_hi[par][:, :, :].bitcast(F32),
                                    ALU.subtract).then_inc(act_lo_ready, 1)
            split(3)
            split(4)

        def run_steps(eng, ph, step):
            step(eng, ph, 0, 0)
            step(eng, ph, 1, 1)
            with eng.Fori(2, STEPS - 1, 2) as s:
                for j in range(2):
                    step(eng, ph, s + j, j, in_loop=True)
            step(eng, ph, STEPS - 1, 0)

        def act_ffn(act, ph):
            act_prenorm(act, ph)
            act_transposed(act, ph["t0"])
            run_steps(act, ph, act_step)
            if ph["post"]:
                act_post(act, ph, ph["u0"] + 3 * STEPS - 1)

        def dve_ffn(dve, chain, ph):
            dve_prenorm(dve, ph)
            dve_transposed(dve, ph["t0"], ph["gain"])
            run_steps(dve, ph, dve_step)
            dve_post(dve, chain, ph, ph["u0"] + 3 * STEPS - 1)

        widths = {}

        for ph in info:
            if ph["kind"] == "mix1":
                widths[ph["u0"]] = KC * 8
            elif ph["kind"] == "mix2":
                widths[ph["u0"] + 10] = KC * 192

        def width_of(n):
            return widths.get(n, UNIT)

        proj_evac, items_done = sem("proj_evac"), sem("items_done")
        item_act, item_dve = sem("item_act"), sem("item_dve")
        att_scores, att_max, att_exp, att_pt = sem("att_scores"), sem("att_max"), sem("att_exp"), sem("att_pt")
        att_pt_act, att_pt_dve, att_pv, att_out = (sem("att_pt_act"), sem("att_pt_dve"), sem("att_pv"),
                                                   sem("att_out"))
        FILL_BANK, O_BANK = 7, 6

        def proj_psum(bank, w):
            return ps[:, bank, 0:2 * w].rearrange("p (t n) -> p t n", t=NT)

        def sp_cols(sp, n, w_ap, c0, w):
            load(sp, n, w_ap.rearrange("(k p) f -> p k f", p=P)[:, :, c0:c0 + w])

        def sp_rows(sp, n, w_ap, i):
            load(sp, n, w_ap.rearrange("(c p) n -> p c n", p=P)[:, 2 * i:2 * i + 2, :])

        def pe_cols(pe, st, n, w, bank, evacuated):
            if evacuated > 0:
                pe.wait_ge(proj_evac, evacuated)
            pe.wait_ge(lo_ready, n + 1)
            hi = w_hi[n % SLOTS][:, 0:KC * w].rearrange("p (k f) -> p k f", k=KC)
            lo = w_lo[n % SLOTS][:, 0:KC * w].rearrange("p (k f) -> p k f", k=KC)
            for t in range(NT):
                dst, toks = proj_psum(bank, w)[:, t, :], slice(t * P, (t + 1) * P)
                for k in range(KC):
                    nc.tensor.matmul(dst, aT_hi[:, k, toks], hi[:, k, :], start=k == 0, stop=False)
                    nc.tensor.matmul(dst, aT_hi[:, k, toks], lo[:, k, :], start=False, stop=False)
                    last = nc.tensor.matmul(dst, aT_lo[:, k, toks], hi[:, k, :], start=False, stop=k == KC - 1)
            last.then_inc(unit_used, 1)
            st["proj"] += 1

        def act_evac(act, st, n, dst, w, bank, scale=1.0):
            act.wait_ge(unit_used, n + 1)
            src = proj_psum(bank, w)
            if len(dst.shape) == 4:
                src = src.rearrange("p t (h d) -> p t h d", d=dst.shape[3])
            nc.scalar.activation(dst, src, ACT.Copy, scale=scale).then_inc(proj_evac, 1)
            st["proj"] += 1

        def pe_items(pe, st, items):
            first = st["item"]
            for i, (srcs, dst, _) in enumerate(items):
                m = first + i - 3
                if i >= 4:
                    pe.wait_ge(item_act, (m + 1) // 2)
                    pe.wait_ge(item_dve, m // 2)
                rows = dst.shape[0]
                for j, src in enumerate(srcs):
                    for t in range(NT):
                        c = (j * NT + t) * P
                        last = nc.tensor.transpose(ps[0:rows, i % 4, c:c + P], src[t], ident)
                last.then_inc(items_done, 1)
            st["item"] += len(items)

        def pe_items_left(pe, st):
            pe.wait_ge(item_act, (st["item"] + 1) // 2)
            pe.wait_ge(item_dve, st["item"] // 2)

        def evac_items(eng, st, items, parity):
            for i, (srcs, dst, scale) in enumerate(items):
                m = st["item"] + i
                if m % 2 != parity:
                    continue
                eng.wait_ge(items_done, m + 1)
                rows, n = dst.shape[0], len(srcs)
                src = ps[0:rows, i % 4, 0:n * S].rearrange("p (h s) -> p h s", h=n)
                if parity == 0:
                    nc.scalar.activation(dst, src, ACT.Copy, scale=scale).then_inc(item_act, 1)
                else:
                    nc.vector.tensor_scalar(dst, src, scale, None, ALU.mult).then_inc(item_dve, 1)
            st["item"] += len(items)

        def score_banks(B):
            return ps[:, 2 * (B % 2):2 * (B % 2) + 2, :]

        neg_max = [small[:, 0 + 4 * i:4 + 4 * i] for i in range(2)]
        row_sum = [small[:, 8 + 4 * i:12 + 4 * i] for i in range(2)]
        row_inv = small[:, 16:20]

        def pe_scores(pe, att, b):
            B = att["B0"] + b
            if B >= 2:
                pe.wait_ge(att_exp, 4 * (B - 1))
            for hh in range(2):
                q, k, dst = att["q"](b, hh), att["k"](b, hh), score_banks(B)[:, hh, :]
                mask = att.get("mask")
                nc.tensor.matmul(dst[:, 0:P], q[:, 0:P], k[:, 0:P], start=True, stop=False)
                nc.tensor.matmul(dst[:, 0:P], ident_bf, causal_bf if mask is None else mask[:, 0:P],
                                 start=False, stop=True)
                nc.tensor.matmul(dst[:, P:3 * P], q[:, P:S], k, start=True, stop=False)
                if mask is None:
                    last = nc.tensor.matmul(dst[:, 2 * P:3 * P], ident_bf, causal_bf, start=False, stop=True)
                else:
                    last = nc.tensor.matmul(dst[:, P:3 * P], ident_bf, mask[:, P:3 * P], start=False, stop=True)
            last.then_inc(att_scores, 1)

        def dve_max(dve, att, b):
            B = att["B0"] + b
            dve.wait_ge(att_scores, B + 1)
            nm = neg_max[B % 2]
            nc.vector.tensor_reduce(nm[:, 0:2], score_banks(B)[:, :, 0:P], AX.X, ALU.max, negate=True)
            nc.vector.tensor_reduce(nm[:, 2:4], score_banks(B)[:, :, P:3 * P], AX.X, ALU.max, negate=True)\
                .then_inc(att_max, 1)

        def act_exp(act, att, b):
            B = att["B0"] + b
            act.wait_ge(att_max, B + 1)
            if B >= 2:
                act.wait_ge(att_pt, 2 * (B - 1))
                act.wait_ge(att_out, B - 1)
            for t in range(NT):
                cols = slice(0, P) if t == 0 else slice(P, 3 * P)
                for hh in range(2):
                    j = 2 * t + hh
                    nc.scalar.activation(p_buf[:, B % 2, hh, cols], score_banks(B)[:, hh, cols], ACT.Exp,
                                         bias=neg_max[B % 2][:, j:j + 1],
                                         accum_out=row_sum[B % 2][:, j:j + 1]).then_inc(att_exp, 1)

        def pe_pt(pe, att, b):
            B = att["B0"] + b
            pe.wait_ge(att_exp, 4 * (B + 1))
            for hh in range(2):
                if B >= 1:
                    pe.wait_ge(att_pt_dve if hh else att_pt_act, B)
                for i in range(3):
                    last = nc.tensor.transpose(ps[:, 4 + hh, i * P:(i + 1) * P],
                                               p_buf[:, B % 2, hh, i * P:(i + 1) * P], ident)
                last.then_inc(att_pt, 1)

        def evac_pt(eng, att, b, hh):
            B = att["B0"] + b
            eng.wait_ge(att_pt, 2 * B + 1 + hh)
            if B >= 2:
                eng.wait_ge(att_pv, B - 1)
            src, dst = ps[:, 4 + hh, 0:3 * P], pt_buf[:, B % 2, hh, :]
            if hh == 0:
                nc.scalar.activation(dst, src, ACT.Copy).then_inc(att_pt_act, 1)
            else:
                nc.vector.tensor_copy(dst, src).then_inc(att_pt_dve, 1)

        def att_psum(dv):
            return ps[:, O_BANK, 0:4 * dv].rearrange("p (t h d) -> p t h d", t=NT, h=2)

        def pe_pv(pe, att, b):
            B = att["B0"] + b
            pe.wait_ge(att_pt_act, B + 1)
            pe.wait_ge(att_pt_dve, B + 1)
            if B >= 1:
                pe.wait_ge(att_out, B)
            for hh in range(2):
                pt = pt_buf[:, B % 2, hh, :]
                dst = att_psum(att["dv"])
                nc.tensor.matmul(dst[:, 0, hh, :], pt[:, 0:P], att["v"](b, hh, 0), start=True, stop=True)
                nc.tensor.matmul(dst[:, 1, hh, :], pt[:, P:2 * P], att["v"](b, hh, 0), start=True, stop=False)
                last = nc.tensor.matmul(dst[:, 1, hh, :], pt[:, 2 * P:3 * P], att["v"](b, hh, 1), start=False,
                                        stop=True)
            last.then_inc(att_pv, 1)

        def dve_norm(dve, chain, att, b):
            B = att["B0"] + b
            dve.wait_ge(att_pv, B + 1)
            chain(nc.vector.reciprocal(row_inv, row_sum[B % 2]))
            chain.wait()
            att["finish"](dve, chain, b)

        def pe_attention(pe, att, fill=None):
            pe_scores(pe, att, 0)
            pe_scores(pe, att, 1)
            for b in range(att["n"]):
                pe_pt(pe, att, b)
                if b + 2 < att["n"]:
                    pe_scores(pe, att, b + 2)
                if fill:
                    fill(b)
                pe_pv(pe, att, b)

        def act_attention(act, att, fill=None):
            act_exp(act, att, 0)
            for b in range(att["n"]):
                if b + 1 < att["n"]:
                    act_exp(act, att, b + 1)
                evac_pt(act, att, b, 0)
                if fill:
                    fill(b)

        def dve_attention(dve, chain, att, fill=None):
            dve_max(dve, att, 0)
            for b in range(att["n"]):
                if b + 1 < att["n"]:
                    dve_max(dve, att, b + 1)
                evac_pt(dve, att, b, 1)
                if fill:
                    fill(b)
                dve_norm(dve, chain, att, b)

        def inv_bc(dv):
            return row_inv.rearrange("p (t h) -> p t h", t=NT).unsqueeze(3).broadcast_to([P, NT, 2, dv])

        def rope(dve, chain, view, n, half, cos, sin, scratch, ready):
            shape = [P, NT, n, half]
            c = cos.rearrange("p (t i) -> p t i", t=NT).unsqueeze(2).broadcast_to(shape)
            s = sin.rearrange("p (t i) -> p t i", t=NT).unsqueeze(2).broadcast_to(shape)
            x1, x2 = view[:, :, :, 0:half], view[:, :, :, half:2 * half]
            size = NT * n * half
            a, b, e, f = (scratch[:, i * size:(i + 1) * size].rearrange("p (t h i) -> p t h i", t=NT, h=n)
                          for i in range(4))
            chain(nc.vector.tensor_tensor(a, x1, c, ALU.mult))
            chain(nc.vector.tensor_tensor(b, x2, s, ALU.mult))
            chain(nc.vector.tensor_tensor(e, x2, c, ALU.mult))
            chain(nc.vector.tensor_tensor(f, x1, s, ALU.mult))
            chain.wait()
            nc.vector.tensor_tensor(x1, a, b, ALU.subtract)
            nc.vector.tensor_tensor(x2, e, f, ALU.add).then_inc(ready, 1)

        FH, DH, DV = 8, 4, 128
        GATE0, DIFF0 = 3 * FH * HD, 3 * FH * HD + FH
        cols1 = [(GATE0, FH)] + [(i * 256, 256) for i in range(6)] + [(DIFF0 + i * 256, 256) for i in range(6)]
        LAM_INIT = 0.8 - 0.6 * float(np.exp(-0.3 * 0))
        AUG = HD + 2
        q_aug = tmp[:, 0:NT * FH * AUG].rearrange("p (t h d) -> p t h d", t=NT, h=FH)
        k_aug = tmp[:, NT * FH * AUG:2 * NT * FH * AUG].rearrange("p (t h d) -> p t h d", t=NT, h=FH)

        def tiny(at, shape):
            n = 1
            for w in shape:
                n *= w
            v = small[:, at:at + n]
            return v if len(shape) == 1 else v.rearrange("p (a b) -> p a b", a=shape[0])

        gate_z, gate_e = tiny(20, [NT, FH]), tiny(36, [NT, FH])
        log_f, forget_b = tiny(52, [NT, FH]), tiny(68, [FH])
        lam_in, lam_prod = tiny(76, [4, HD]), tiny(332, [2, HD])
        lam_sum, neg_lam = tiny(460, [2]), tiny(462, [1])
        sub_gain, diff_ss = tiny(463, [DV]), tiny(591, [NT, DH])
        diff_nat = o_all[:, :, FH * HD:D]
        c_psum = ps[:, FILL_BANK, 0:NT * FH].rearrange("p (t h) -> p t h", t=NT)

        def fox_finish(dve, chain, b):
            dst = o_all[:, :, 2 * b * HD:2 * (b + 1) * HD].rearrange("p t (h d) -> p t h d", h=2)
            nc.vector.tensor_tensor(dst, att_psum(HD), inv_bc(HD), ALU.mult).then_inc(att_out, 1)

        def diff_finish(dve, chain, b):
            both = tmp[:, 1024:1536].rearrange("p (t h d) -> p t h d", t=NT, h=2)
            nc.vector.tensor_tensor(both, att_psum(DV), inv_bc(DV), ALU.mult).then_inc(att_out, 1)
            dve.wait_ge(att_out, fox["n"] + b + 1)
            chain(nc.vector.scalar_tensor_tensor(diff_nat[:, :, b * DV:(b + 1) * DV], both[:, :, 1, :], neg_lam,
                                                 both[:, :, 0, :], ALU.mult, ALU.add))
            chain.wait()

        fox = {"B0": 0, "n": FH // 2, "dv": HD, "finish": fox_finish,
               "q": lambda b, hh: qk_t[0:AUG, 2 * b + hh, :], "k": lambda b, hh: qk_t[0:AUG, 8 + 2 * b + hh, :],
               "v": lambda b, hh, kt: proj[:, kt, 1024 + (2 * b + hh) * HD:1024 + (2 * b + hh + 1) * HD]}
        diff = {"B0": FH // 2, "n": DH, "dv": DV, "finish": diff_finish,
                "q": lambda b, hh: qk_t[0:HD, 2 * b + hh, :], "k": lambda b, hh: qk_t[0:HD, 8 + 2 * b + hh, :],
                "v": lambda b, hh, kt: proj[:, kt, DIFF0 + 1024 + b * DV:DIFF0 + 1024 + (b + 1) * DV]}
        diff_qk = proj[:, :, DIFF0:DIFF0 + 1024].rearrange("p t (h d) -> p t h d", d=HD)
        fox_items, diff_items = [], []
        for _b in range(4):
            for _k, _aug in ((0, q_aug), (1, k_aug)):
                fox_items.append(([[_aug[:, t, h, :] for t in range(NT)] for h in (2 * _b, 2 * _b + 1)],
                                  qk_t[0:AUG, 8 * _k + 2 * _b:8 * _k + 2 * _b + 2, :], 1.0))
                diff_items.append(([[diff_qk[:, t, 8 * _k + h, :] for t in range(NT)]
                                    for h in (2 * _b, 2 * _b + 1)],
                                   qk_t[0:HD, 8 * _k + 2 * _b:8 * _k + 2 * _b + 2, :], 1.0))

        def evac1(act, st, u0, i, bank):
            if i == 0:
                dst, scale = gate_z, 1.0
            elif i <= 2:
                dst, scale = q_aug[:, :, 4 * (i - 1):4 * i, 0:HD], SCALE
            elif i <= 4:
                dst, scale = k_aug[:, :, 4 * (i - 3):4 * (i - 2), 0:HD], 1.0
            else:
                c0 = cols1[i][0]
                dst, scale = proj[:, :, c0:c0 + 256], SCALE if i in (7, 8) else 1.0
            act_evac(act, st, u0 + i, dst, cols1[i][1], bank, scale)

        def sp_mix1(sp, ph):
            w_in, w_out = A["w_in"][0], A["w_out"][0]
            for i, (c0, w) in enumerate(cols1):
                sp_cols(sp, ph["u0"] + i, w_in, c0, w)
            for i in range(4):
                sp_rows(sp, ph["u0"] + 13 + i, w_out, i)

        def pool_mix1(pool, chain, ph):
            pool.dma_start(forget_b, A["fox_forget_b"][0].partition_broadcast(P)).then_inc(sem("mix1_loaded"), 16)
            for i, nm in enumerate(("q1", "q2", "k1", "k2")):
                pool.dma_start(lam_in[:, i, :], A["diff_lambda_" + nm][0].partition_broadcast(P))\
                    .then_inc(sem("mix1_loaded"), 16)
            pool.dma_start(sub_gain, A["diff_subln_g"][0].partition_broadcast(P)).then_inc(sem("mix1_loaded"), 16)
            pool.wait_ge(aT_ready, 4 * (ph["t0"] + 1))
            nc.gpsimd.memset(q_aug[:, :, :, HD + 1:HD + 2], 1.0).then_inc(sem("aug_ones"), 1)
            nc.gpsimd.memset(k_aug[:, :, :, HD:HD + 1], 1.0).then_inc(sem("aug_ones"), 1)
            pool.wait_ge(sem("diff_ss_ready"), 1)
            chain(nc.gpsimd.tensor_scalar(diff_ss, diff_ss, 1.0 / DV, EPS, ALU.mult, ALU.add))
            chain.wait()
            nc.gpsimd.tensor_tensor(diff_ss, diff_ss, minus_half.unsqueeze(2).broadcast_to([P, NT, DH]), ALU.pow)\
                .then_inc(sem("diff_rstd_ready"), 1)

        def pe_mix1(pe, ph):
            st, u0 = {"item": 0, "proj": 0}, ph["u0"]
            pe_transpose(pe, ph["t0"], xn)
            pe.wait_ge(aT_ready, 4 * (ph["t0"] + 1))
            for i in range(7):
                pe_cols(pe, st, u0 + i, cols1[i][1], i % 4, i - 3)
            pe_cols(pe, st, u0 + 7, 256, FILL_BANK, 0)
            pe.wait_ge(sem("logf_ready"), 1)
            pe.wait_ge(proj_evac, 8)
            nc.tensor.matmul(c_psum[:, 0, :], const("cumsum"), log_f[:, 0, :], start=True, stop=True)
            nc.tensor.matmul(c_psum[:, 1, :], const("cumsum"), log_f[:, 1, :], start=True, stop=False)
            nc.tensor.matmul(c_psum[:, 1, :], const("ones"), log_f[:, 0, :], start=False, stop=True)\
                .then_inc(sem("decay_ready"), 1)
            pe.wait_ge(sem("aug_ready"), 2)
            pe.wait_ge(sem("aug_ones"), 2)
            pe_items(pe, st, fox_items)
            pe_cols(pe, st, u0 + 8, 256, FILL_BANK, 0)
            pe_items_left(pe, st)
            pe_attention(pe, fox, lambda b: pe_cols(pe, st, u0 + 9 + b, 256, FILL_BANK, 9 + b))
            pe.wait_ge(proj_evac, 13)
            pe.wait_ge(sem("diff_rope_ready"), 1)
            pe.wait_ge(att_exp, 4 * fox["n"])
            pe_items(pe, st, diff_items)
            pe_items_left(pe, st)
            pe_attention(pe, diff)
            pe_transpose(pe, ph["t0"] + 1, o_all)
            pe.wait_ge(aT_ready, 4 * (ph["t0"] + 2))
            for i in range(4):
                n = u0 + 13 + i
                pe_rows(pe, n, n % SLOTS, aT_hi[:, 2 * i:2 * i + 2, :], aT_lo[:, 2 * i:2 * i + 2, :], 0,
                        i == 0, i == 3)

        def act_mix1(act, chain, ph):
            st, u0 = {"item": 0, "proj": 0}, ph["u0"]

            def ahead(i):
                split_hi(act, u0 + i + 2, width=width_of(u0 + i + 2))
            act_prenorm(act, ph)
            act_transposed(act, ph["t0"])
            for i in range(7):
                ahead(i)
                evac1(act, st, u0, i, i % 4)
                if i == 1:
                    act.wait_ge(sem("gate_abs_ready"), 1)
                    chain(nc.scalar.activation(gate_e, gate_e, ACT.Exp))
                    chain.wait()
                    nc.scalar.activation(gate_e, gate_e, ACT.Ln, bias=1.0).then_inc(sem("gate_ln_ready"), 1)
            ahead(7)
            evac1(act, st, u0, 7, FILL_BANK)
            ahead(8)
            evac_items(act, st, fox_items, 0)
            evac1(act, st, u0, 8, FILL_BANK)
            act.wait_ge(sem("lam_sum_ready"), 1)
            nc.scalar.activation(lam_sum, lam_sum, ACT.Exp).then_inc(sem("lam_exp_ready"), 1)

            def fill(b):
                ahead(9 + b)
                evac1(act, st, u0, 9 + b, FILL_BANK)
            act_attention(act, fox, fill)
            ahead(13)
            evac_items(act, st, diff_items, 0)
            act_attention(act, diff)
            act_transposed(act, ph["t0"] + 1)
            for i in range(14, 17):
                ahead(i)
            act_post(act, ph, u0 + 16)

        def dve_mix1(dve, chain, ph):
            st, u0 = {"item": 0, "proj": 0}, ph["u0"]

            def ahead(i):
                split_lo(dve, u0 + i + 2, width=width_of(u0 + i + 2))
            dve_prenorm(dve, ph)
            dve_transposed(dve, ph["t0"], ph["gain"])
            ahead(0)
            dve.wait_ge(sem("mix1_loaded"), 16 * 6)
            dve.wait_ge(proj_evac, 1)
            chain(nc.vector.tensor_tensor(gate_z, gate_z, forget_b.unsqueeze(1).broadcast_to([P, NT, FH]), ALU.add))
            chain.wait()
            nc.vector.scalar_tensor_tensor(gate_e, gate_z, -1.0, gate_z, ALU.mult, ALU.min)\
                .then_inc(sem("gate_abs_ready"), 1)
            ahead(1)
            dve.wait_ge(sem("gate_ln_ready"), 1)
            nc.vector.scalar_tensor_tensor(log_f, gate_z, 0.0, gate_e, ALU.min, ALU.subtract)\
                .then_inc(sem("logf_ready"), 1)
            chain(nc.vector.tensor_tensor(lam_prod, lam_in[:, 0:2, :], lam_in[:, 2:4, :], ALU.mult))
            chain(nc.vector.tensor_scalar(sub_gain, sub_gain, 1.0 - LAM_INIT, None, ALU.mult))
            chain.wait()
            nc.vector.tensor_reduce(lam_sum, lam_prod, AX.X, ALU.add).then_inc(sem("lam_sum_ready"), 1)
            for i in range(2, 9):
                ahead(i)
            dve.wait_ge(sem("decay_ready"), 1)
            nc.vector.tensor_copy(q_aug[:, :, :, HD:HD + 1], c_psum.unsqueeze(3)).then_inc(sem("aug_ready"), 1)
            nc.vector.tensor_scalar(k_aug[:, :, :, HD + 1:HD + 2], c_psum.unsqueeze(3), -1.0, None, ALU.mult)\
                .then_inc(sem("aug_ready"), 1)
            evac_items(dve, st, fox_items, 1)
            dve.wait_ge(sem("lam_exp_ready"), 1)
            chain(nc.vector.tensor_tensor(neg_lam, lam_sum[:, 1:2], lam_sum[:, 0:1], ALU.subtract))
            chain.wait()
            chain(nc.vector.tensor_scalar(neg_lam, neg_lam, -LAM_INIT, None, ALU.add))
            chain.wait()
            dve_attention(dve, chain, fox, lambda b: ahead(9 + b))
            ahead(13)
            dve.wait_ge(proj_evac, 13)
            rope(dve, chain, diff_qk, 16, 8, const("cos16"), const("sin16"), tmp, sem("diff_rope_ready"))
            evac_items(dve, st, diff_items, 1)
            dve_attention(dve, chain, diff)
            square = tmp[:, 0:1024].rearrange("p (t h d) -> p t h d", t=NT, h=DH)
            heads = diff_nat.rearrange("p t (h d) -> p t h d", h=DH)
            chain(nc.vector.tensor_tensor(square, heads, heads, ALU.mult))
            chain.wait()
            nc.vector.tensor_reduce(diff_ss, square, AX.X, ALU.add).then_inc(sem("diff_ss_ready"), 1)
            dve.wait_ge(sem("diff_rstd_ready"), 1)
            for t in range(NT):
                chain(nc.vector.tensor_tensor(heads[:, t], heads[:, t],
                                              diff_ss[:, t, :].unsqueeze(2).broadcast_to([P, DH, DV]), ALU.mult))
                chain.wait()
                nc.vector.tensor_tensor(heads[:, t], heads[:, t],
                                        sub_gain.unsqueeze(1).broadcast_to([P, DH, DV]), ALU.mult)\
                    .then_inc(xn_ready, 1)
            dve_transposed(dve, ph["t0"] + 1)
            for i in range(14, 17):
                ahead(i)
            dve_post(dve, chain, ph, u0 + 16)

        DIN = 2752
        cols2 = [(i * 256, 256) for i in range(10)] + [(2560, DIN - 2560)]
        N_IN, N_GATE = len(cols2), 3 * D // 256
        SBH, NH, NG, DSH, IXH, IXD = 4, 8, 2, 4, 8, 32
        NQ, NKC, NKS, NVS, NKW, NVW, GATES, DQ, DV0, IQ, IW = (768, 1280, 1536, 1664, 1792, 1920, 2048, 2072,
                                                               2392, 2456, 2744)
        NB = S // 16 - 1
        TOPK = min(256, S // 4)
        NQK = NH + 2 * NG + DSH + 1
        qk_nat = tmp[:, 0:NT * NQK * HD].rearrange("p (t h d) -> p t h d", t=NT, h=NQK)
        qk_groups = [(0, NH, NQ, 0), (NH, NG, NKS, 1), (NH + NG, NG, NKW, 2), (NH + 2 * NG, DSH, DQ, 3),
                     (NH + 2 * NG + DSH, 1, DQ + DSH * HD, 4)]
        qk_load = [qk_groups[0], qk_groups[1], qk_groups[2], (NH + 2 * NG, DSH + 1, DQ, 3)]
        head_gain = proj[:, 0, DIN:DIN + 5 * HD].rearrange("p (g d) -> p g d", g=5)
        cmp_gain = proj[:, 1, DIN:DIN + HD]
        cmp_w2 = proj[:, 1, DIN + HD:DIN + 3 * HD].rearrange("p (a d) -> p a d", a=2)
        cmp_pe = proj[:, 1, DIN + 3 * HD:DIN + 3 * HD + 32].rearrange("p (a j) -> p a j", a=2)
        cmp_w1 = qk_t[:, 0:16, :].rearrange("p a b -> p (a b)").rearrange("p (a j n) -> p a j n", a=2, j=16)
        pb = p_buf[:, :, :, :].rearrange("p a b c -> p (a b c)")
        ptb = pt_buf[:, :, :, :].rearrange("p a b c -> p (a b c)")
        cmp_in = pb[:, 0:960].rearrange("p (a j c) -> p a j c", a=2, j=16)
        sb_t = o_all[:, :, :].rearrange("p t d -> p (t d)").rearrange("p (h s) -> p h s", h=8)
        cmp_hid, cmp_sig = tiny(20, [2, 2 * NB]), tiny(80, [2, 2 * NB])
        vc_in = small[:, 140:140 + NH * NB]
        kc = small[0:2 * NB, 260:324]
        kc_sq = small[0:2 * NB, 324:388]
        kc_ss = small[0:2 * NB, 388:389]
        kc_t = small[0:HD, 390:390 + 2 * NB]
        kc_rot = small[0:2 * NB, 420:452]
        nsa_gate = tiny(452, [NT, 3 * NH])
        gates = nsa_gate.rearrange("p t (h c) -> p t h c", c=3)
        qk_ss = tiny(500, [NT, NQK])
        cmp_max, cmp_den, cmp_zero = tiny(534, [NT, NH]), tiny(550, [NT, NH]), tiny(566, [NT, NH])
        row_gate = small[:, 582:586]
        top8 = [small[:, 586 + 8 * i:594 + 8 * i] for i in range(2)]
        ix_w = tiny(602, [NT, IXH])
        v_diag = ptb[0:NH * NB, 0:512].rearrange("p (h d) -> p h d", h=NH)
        cmp_s = pb[:, 0:NT * NH * NB].rearrange("p (t h c) -> p t h c", t=NT, h=NH)
        cmp_p_t = pb[0:NH * NB, 240:240 + S]
        ix_relu = [pb[:, 500:884], ptb[:, 512:896]]
        ix_score, ix_val = pb[:, 884:1268], ptb[:, 896:1280]
        sel_mask = sb_mask
        CMP_BANK = 4

        def ev(name, ph):
            return sem(name), ph["mix2_before"] + 1

        def wait(eng, name, ph, times=1):
            s_, v_ = ev(name, ph)
            eng.wait_ge(s_, v_ * times)

        def nsa_finish(branch):
            def finish(dve, chain, b):
                chain(nc.vector.tensor_tensor(row_gate.rearrange("p (t h) -> p t h", t=NT),
                                              row_inv.rearrange("p (t h) -> p t h", t=NT),
                                              gates[:, :, 2 * b:2 * b + 2, branch], ALU.mult))
                chain.wait()
                part = tmp[:, 0:256].rearrange("p (t h d) -> p t h d", t=NT, h=2)
                nc.vector.tensor_tensor(part, att_psum(HD), row_gate.rearrange("p (t h) -> p t h", t=NT)
                                        .unsqueeze(3).broadcast_to([P, NT, 2, HD]), ALU.mult).then_inc(att_out, 1)
                dve.wait_ge(att_out, finish.B0 + b + 1)
                dst = o_all[:, :, 256 + 2 * b * HD:256 + 2 * (b + 1) * HD].rearrange("p t (h d) -> p t h d", h=2)
                chain(nc.vector.tensor_tensor(dst, dst, part, ALU.add))
                chain.wait()
            return finish

        def dsa_finish(dve, chain, b):
            dst = o_all[:, :, 768 + 2 * b * HD:768 + 2 * (b + 1) * HD].rearrange("p t (h d) -> p t h d", h=2)
            nc.vector.tensor_tensor(dst, att_psum(HD), inv_bc(HD), ALU.mult).then_inc(att_out, 1)

        def attentions(ph):
            B0 = ph["B0"]
            out_ = []
            for i, (k0, v0) in enumerate(((NH, NVS), (NH + NG, NVW))):
                fin = nsa_finish(i + 1)
                fin.B0 = B0 + 4 * i
                out_.append({"B0": B0 + 4 * i, "n": 4, "dv": HD, "finish": fin,
                             "q": lambda b, hh: qk_t[0:HD, 2 * b + hh, :],
                             "k": lambda b, hh, k0=k0: qk_t[0:HD, k0 + b // 2, :],
                             "v": lambda b, hh, kt, v0=v0: proj[:, kt, v0 + (b // 2) * HD:v0 + (b // 2 + 1) * HD]})
            out_.append({"B0": B0 + 8, "n": 2, "dv": HD, "finish": dsa_finish, "mask": sel_mask,
                         "q": lambda b, hh: qk_t[0:HD, NH + 2 * NG + 2 * b + hh, :],
                         "k": lambda b, hh: qk_t[0:HD, NQK - 1, :],
                         "v": lambda b, hh, kt: proj[:, kt, DV0:DV0 + HD]})
            return out_

        def nat(src, c0, w):
            return [src[:, t, c0:c0 + w] for t in range(NT)]

        sb_items, qk_items, ix_items = [], [], []
        for _i in range(2):
            for _k in range(2):
                sb_items.append(([nat(proj, 256 * _k + (2 * _i + j) * HD, HD) for j in range(2)],
                                 sb_t[0:HD, 4 * _k + 2 * _i:4 * _k + 2 * _i + 2, :], 1.0))
        for _i in range(0, NQK, 2):
            _n = min(2, NQK - _i)
            is_q = _i < NH or NH + 2 * NG <= _i < NQK - 1
            qk_items.append(([[qk_nat[:, t, _i + j, :] for t in range(NT)] for j in range(_n)],
                             qk_t[0:HD, _i:_i + _n, :], SCALE if is_q else 1.0))
        ix_t = tmp[0:IXD, 0:(IXH + 1) * S].rearrange("p (h s) -> p h s", h=IXH + 1)
        for _i in range(0, IXH + 1, 2):
            _n = min(2, IXH + 1 - _i)
            ix_items.append(([nat(proj, IQ + (_i + j) * IXD, IXD) for j in range(_n)],
                             ix_t[:, _i:_i + _n, :], 1.0))

        def sb_bank(h):
            return ps[:, h, 0:3 * P]

        def sb_view(buf, half):
            return buf[:, half * 768:(half + 1) * 768].rearrange("p (h c) -> p h c", h=2)

        def sb_diag(buf, half):
            v = sb_view(buf, half).rearrange("p h (b c) -> p h b c", b=3)
            return [v[:, h, 0:3:2, :] for h in range(2)]

        def pe_sb_z(pe, h, start, stop):
            q, k, dst = sb_t[0:HD, h, :], sb_t[0:HD, 4 + h, :], sb_bank(h)
            nc.tensor.matmul(dst[:, 0:S], k[:, 0:P], q, start=start, stop=stop)
            return dst, q, k

        def pe_sb_scores(pe, half, ph):
            for h in (2 * half, 2 * half + 1):
                dst, q, k = pe_sb_z(pe, h, True, True)
                last = nc.tensor.matmul(dst[:, S:3 * P], k[:, P:S], q[:, P:S], start=True, stop=True)
            last.then_inc(ev("sb_z_ready", ph)[0], 1)

        def pe_sb_logw(pe, half, ph):
            sp_ = sb_view(ptb, half)
            for h in (2 * half, 2 * half + 1):
                dst, q, k = pe_sb_z(pe, h, True, False)
                own = sp_[:, h % 2, :]
                nc.tensor.matmul(dst[:, 0:S], const("tail_neg"), own[:, 0:S], start=False, stop=False)
                nc.tensor.matmul(dst[:, P:S], const("ones_neg"), own[:, S:3 * P], start=False, stop=False)
                nc.tensor.matmul(dst[:, 0:P], ident_bf, notpast_bf, start=False, stop=True)
                nc.tensor.matmul(dst[:, S:3 * P], k[:, P:S], q[:, P:S], start=True, stop=False)
                nc.tensor.matmul(dst[:, S:3 * P], const("tail_neg"), own[:, S:3 * P], start=False, stop=False)
                last = nc.tensor.matmul(dst[:, S:3 * P], ident_bf, notpast_bf, start=False, stop=True)
            last.then_inc(ev("sb_logw_ready", ph)[0], 1)

        def sp_mix2(sp, ph):
            l, u0 = ph["l"], ph["u0"]
            for i, (c0, w) in enumerate(cols2):
                sp_cols(sp, u0 + i, A["w_in_2"][l], c0, w)
            for i in range(N_GATE):
                sp_cols(sp, u0 + N_IN + i, A["w_gate_2"][l], i * 256, 256)
            sp_rows(sp, u0 + 23, A["w_br_a_2"][l], 0)
            sp_rows(sp, u0 + 24, A["w_br_b_2"][l], 0)
            sp_rows(sp, u0 + 25, A["w_br_b_2"][l], 1)
            sp_rows(sp, u0 + 26, A["w_br_c_2"][l], 0)
            for i in range(4):
                sp_rows(sp, u0 + 27 + i, A["w_out_2"][l], i)

        def pool_mix2(pool, chain, ph):
            l = ph["l"]
            loaded = ev("mix2_loaded", ph)[0]
            pool.wait_ge(tp_done, 4 * (ph["t0"] + 1))
            for a in range(2):
                pool.dma_start(cmp_w1[:, a], A["nsa_cmp_w1_2"][l, a].rearrange("(j p) n -> p j n", p=P))\
                    .then_inc(loaded, 16)
                pool.dma_start(cmp_w2[:, a, :], A["nsa_cmp_w2_2"][l, a]).then_inc(loaded, 16)
                pool.dma_start(cmp_pe[:, a, :], A["cmp_pe"][l, a]).then_inc(loaded, 16)
            for i, src in enumerate((A["nsa_q_norm_2"][l], A["nsa_k_norm_2"][l, 1], A["nsa_k_norm_2"][l, 2],
                                     A["dsa_q_norm_2"][l], A["dsa_k_norm_2"][l])):
                pool.dma_start(head_gain[:, i, :], src.partition_broadcast(P)).then_inc(loaded, 16)
            pool.dma_start(cmp_gain, A["nsa_k_norm_2"][l, 0].partition_broadcast(P)).then_inc(loaded, 16)
            wait(pool, "qk_ss_ready", ph)
            chain(nc.gpsimd.tensor_scalar(qk_ss, qk_ss, 1.0 / HD, EPS, ALU.mult, ALU.add))
            chain.wait()
            nc.gpsimd.tensor_tensor(qk_ss, qk_ss, minus_half.unsqueeze(2).broadcast_to([P, NT, NQK]), ALU.pow)\
                .then_inc(ev("qk_rstd_ready", ph)[0], 1)
            wait(pool, "kc_ss_ready", ph)
            chain(nc.gpsimd.tensor_scalar(kc_ss, kc_ss, 1.0 / HD, EPS, ALU.mult, ALU.add))
            chain.wait()
            nc.gpsimd.tensor_tensor(kc_ss, kc_ss, minus_half[0:2 * NB], ALU.pow)\
                .then_inc(ev("kc_rstd_ready", ph)[0], 1)
            for t in range(NT):
                wait(pool, "gated_ready", ph, 1)
                nc.gpsimd.tensor_tensor(xn[:, t, :], gate_or_gain[:, t, 0:D], gate_or_gain[:, t, D:2 * D], ALU.add)\
                    .then_inc(ev("merged_ab", ph)[0], 1)

        def pe_mix2(pe, ph):
            st, u0 = {"item": ph["item0"], "proj": 0}, ph["u0"]
            pj0 = ph["proj0"]

            def fill(k):
                pe_cols(pe, st, u0 + N_IN + k, 256, FILL_BANK, pj0 + N_IN + k)
            pe_transpose(pe, ph["t0"], xn)
            pe.wait_ge(aT_ready, 4 * (ph["t0"] + 1))
            for i, (_, w) in enumerate(cols2):
                pe_cols(pe, st, u0 + i, w, i % 4, pj0 + i - 3 if i > 3 else 0)
            pe.wait_ge(proj_evac, pj0 + N_IN)
            pe_items(pe, st, sb_items)
            for a in range(2):
                for g in range(NG):
                    for t in range(NT):
                        for par in range(2):
                            c = (a * NG + g) * P + t * HD
                            last = nc.tensor.matmul(ps[par * HD:(par + 1) * HD, O_BANK, c:c + HD],
                                                    proj[:, t, NKC + (a * NG + g) * HD:NKC + (a * NG + g + 1) * HD],
                                                    ident[:, par::2], start=True, stop=True)
            last.then_inc(ev("pairs_ready", ph)[0], 1)
            fill(0)
            wait(pe, "cmp_in_ready", ph)
            for a in range(2):
                for j in range(16):
                    last = nc.tensor.matmul(ps[:, CMP_BANK, a * 2 * NB:(a + 1) * 2 * NB], cmp_w1[:, a, j, :],
                                            cmp_in[:, a, j, :], start=j == 0, stop=j == 15)
            last.then_inc(ev("hidden_ready", ph)[0], 1)
            pe_items_left(pe, st)
            pe_sb_scores(pe, 0, ph)
            pe_sb_scores(pe, 1, ph)
            fill(1)
            for half in range(2):
                pe.wait_ge(ev("sb_sp_ready", ph)[0], 2 * (ev("", ph)[1] - 1) + half + 1)
                pe_sb_logw(pe, half, ph)
            fill(2)
            for half in range(2):
                pe.wait_ge(ev("sb_w_ready", ph)[0], 2 * (ev("", ph)[1] - 1) + half + 1)
            o_sb = ps[:, O_BANK, :].rearrange("p (t h d) -> p t h d", t=NT, h=SBH)
            for h in range(SBH):
                w = sb_view(pb, h // 2)[:, h % 2, :]
                v = [proj[:, t, 512 + h * HD:512 + (h + 1) * HD] for t in range(NT)]
                nc.tensor.matmul(o_sb[:, 0, h, :], w[:, 0:P], v[0], start=True, stop=True)
                nc.tensor.matmul(o_sb[:, 1, h, :], w[:, P:S], v[0], start=True, stop=False)
                last = nc.tensor.matmul(o_sb[:, 1, h, :], w[:, S:3 * P], v[1], start=False, stop=True)
            last.then_inc(ev("sb_out_ready", ph)[0], 1)
            wait(pe, "hid_ready", ph)
            nc.tensor.matmul(ps[0:2 * NB, CMP_BANK, 128:128 + HD], cmp_hid[:, 0, :], cmp_w2[:, 0, :],
                             start=True, stop=True)
            nc.tensor.matmul(ps[0:NH * NB, CMP_BANK + 1, 0:HD], vc_in, cmp_w2[:, 1, :], start=True, stop=True)\
                .then_inc(ev("kcvc_ready", ph)[0], 1)
            fill(3)
            wait(pe, "qk_ready", ph)
            pe_items(pe, st, qk_items)
            wait(pe, "kc_ready", ph)
            nc.tensor.transpose(ps[0:HD, CMP_BANK, 256:256 + 2 * NB], kc, ident[0:2 * NB, 0:2 * NB])\
                .then_inc(ev("kcT_psum", ph)[0], 1)
            pe_items_left(pe, st)
            wait(pe, "kcT_ready", ph)
            for t in range(NT):
                for h in range(NH):
                    g = h // (NH // NG)
                    c = (t * NH + h) * NB
                    last = nc.tensor.matmul(ps[:, CMP_BANK, c:c + NB], qk_t[0:HD, h, t * P:(t + 1) * P],
                                            kc_t[:, g * NB:(g + 1) * NB], start=True, stop=True)
            last.then_inc(ev("cmp_scores", ph)[0], 1)
            fill(4)
            wait(pe, "ix_rope_ready", ph)
            pe_items(pe, st, ix_items)
            wait(pe, "cmp_p_ready", ph)
            for t in range(NT):
                last = nc.tensor.transpose(ps[0:NH * NB, CMP_BANK + 1, t * P:(t + 1) * P],
                                           cmp_s[:, t].rearrange("p h c -> p (h c)"), ident)
            last.then_inc(ev("cmp_pt", ph)[0], 1)
            wait(pe, "cmp_pt_ready", ph)
            for t in range(NT):
                last = nc.tensor.matmul(ps[:, CMP_BANK + t, :], cmp_p_t[:, t * P:(t + 1) * P],
                                        v_diag.rearrange("p h d -> p (h d)"), start=True, stop=True)
            last.then_inc(ev("cmp_out_ready", ph)[0], 1)
            fill(5)
            pe_items_left(pe, st)
            r0 = IXH * (ev("", ph)[1] - 1)
            for h in range(IXH):
                if h >= 4:
                    pe.wait_ge(sem("ix_relu_ready"), r0 + h - 3)
                nc.tensor.matmul(ps[:, h % 4, 0:P], ix_t[:, h, 0:P], ix_t[:, IXH, 0:P], start=True, stop=True)
                nc.tensor.matmul(ps[:, h % 4, P:3 * P], ix_t[:, h, P:S], ix_t[:, IXH, :], start=True, stop=True)\
                    .then_inc(sem("ix_logits"), 1)
            for k in (6, 7, 8):
                fill(k)
            wait(pe, "mask_ready", ph)
            sel, win, dsa = attentions(ph)
            pe_attention(pe, sel, lambda b: fill(9 + b) if b < 3 else None)
            pe_attention(pe, win)
            pe_attention(pe, dsa)
            pe_transpose(pe, ph["t0"] + 1, o_all)
            pe.wait_ge(aT_ready, 4 * (ph["t0"] + 2))
            for i, (bank, first, last) in enumerate(((0, True, True), (4, True, False), (4, False, True),
                                                     (0, True, True))):
                if i == 3:
                    pe.wait_ge(sem("gated"), 5 * (ev("", ph)[1] - 1) + 2)
                n = u0 + 23 + i
                pe_rows(pe, n, n % SLOTS, aT_hi[:, 2 * i:2 * i + 2, :], aT_lo[:, 2 * i:2 * i + 2, :], bank,
                        first, last)
            pe_transpose(pe, ph["t0"] + 2, xn)
            pe.wait_ge(aT_ready, 4 * (ph["t0"] + 3))
            for i in range(4):
                n = u0 + 27 + i
                pe_rows(pe, n, n % SLOTS, aT_hi[:, 2 * i:2 * i + 2, :], aT_lo[:, 2 * i:2 * i + 2, :], 0,
                        i == 0, i == 3)

        def act_mix2(act, chain, ph):
            st, u0 = {"item": ph["item0"], "proj": 0}, ph["u0"]
            li = ev("", ph)[1] - 1

            def ahead(i):
                split_hi(act, u0 + i + 2, width=width_of(u0 + i + 2))

            def fill(k):
                ahead(N_IN + k)
                act_evac(act, st, u0 + N_IN + k, gate_or_gain[:, :, k * 256:(k + 1) * 256], 256, FILL_BANK)
            act_prenorm(act, ph)
            act_transposed(act, ph["t0"])
            for i, (c0, w) in enumerate(cols2):
                ahead(i)
                act_evac(act, st, u0 + i, proj[:, :, c0:c0 + w], w, i % 4, SCALE if i == 0 else 1.0)
            act.wait_ge(proj_evac, ph["proj0"] + N_IN)
            act.wait_ge(aT_ready, 4 * (ph["t0"] + 1))
            for h0, n, c0, _ in qk_load:
                last = nc.scalar.activation(qk_nat[:, :, h0:h0 + n, :].rearrange("p t h d -> p t (h d)"),
                                            proj[:, :, c0:c0 + n * HD], ACT.Square)
            last.then_inc(ev("qk_sq_ready", ph)[0], 1)
            evac_items(act, st, sb_items, 0)
            fill(0)
            wait(act, "gates_clamped", ph)
            nc.scalar.activation(nsa_gate, nsa_gate, ACT.Exp, scale=-1.0).then_inc(ev("gates_exp", ph)[0], 1)
            wait(act, "hid_clamped", ph)
            nc.scalar.activation(cmp_sig, cmp_sig, ACT.Exp, scale=-1.0).then_inc(ev("hid_exp", ph)[0], 1)
            for half in range(2):
                act.wait_ge(sem("sb_z_ready"), 2 * li + half + 1)
                z, buf = ps[:, 2 * half:2 * half + 2, 0:3 * P], sb_view(pb, half)
                chain(nc.scalar.activation(buf, z, ACT.Abs))
                chain.wait()
                chain(nc.scalar.activation(buf, buf, ACT.Exp, scale=-1.0))
                chain.wait()
                nc.scalar.activation(buf, buf, ACT.Ln, bias=1.0).then_inc(sem("sb_ln_ready"), 1)
            fill(1)
            for half in range(2):
                act.wait_ge(sem("sb_logw_ready"), 2 * li + half + 1)
                nc.scalar.activation(sb_view(pb, half), ps[:, 2 * half:2 * half + 2, 0:3 * P], ACT.Exp)\
                    .then_inc(sem("sb_w_ready"), 1)
            fill(2)
            fill(3)
            evac_items(act, st, qk_items, 0)
            wait(act, "kcT_psum", ph)
            nc.scalar.activation(kc_t, ps[0:HD, CMP_BANK, 256:256 + 2 * NB], ACT.Copy)\
                .then_inc(ev("kcT_ready", ph)[0], 1)
            wait(act, "cmp_shifted", ph)
            nc.scalar.activation(cmp_s, cmp_s, ACT.Exp).then_inc(ev("cmp_exp", ph)[0], 1)
            fill(4)
            evac_items(act, st, ix_items, 0)
            wait(act, "cmp_pt", ph)
            nc.scalar.activation(cmp_p_t, ps[0:NH * NB, CMP_BANK + 1, 0:S], ACT.Copy)\
                .then_inc(ev("cmp_pt_ready", ph)[0], 1)
            fill(5)
            for h in range(IXH):
                act.wait_ge(sem("ix_logits"), IXH * li + h + 1)
                if h >= 2:
                    act.wait_ge(sem("ix_added"), IXH * li + h - 1)
                nc.scalar.activation(ix_relu[h % 2], ps[:, h % 4, 0:3 * P], ACT.Relu)\
                    .then_inc(sem("ix_relu_ready"), 1)
            for k in (6, 7, 8):
                fill(k)
            sel, win, dsa = attentions(ph)
            act_attention(act, sel, lambda b: fill(9 + b) if b < 3 else None)
            act_attention(act, win)
            act_attention(act, dsa)
            ahead(23)
            for br in range(3):
                g_ = gate_or_gain[:, :, br * D:(br + 1) * D]
                nc.scalar.activation(g_, g_, ACT.Sigmoid).then_inc(sem("gate_sigmoid"), 1)
            act_transposed(act, ph["t0"] + 1)
            ahead(24)
            ahead(25)
            ahead(26)
            act_transposed(act, ph["t0"] + 2)
            for i in range(27, 31):
                ahead(i)

        def dve_mix2(dve, chain, ph):
            st, u0 = {"item": ph["item0"], "proj": 0}, ph["u0"]
            li = ev("", ph)[1] - 1

            def ahead(i):
                split_lo(dve, u0 + i + 2, width=width_of(u0 + i + 2))

            def fill(k):
                ahead(N_IN + k)
            dve_prenorm(dve, ph)
            dve_transposed(dve, ph["t0"], ph["gain"])
            for i in range(N_IN):
                ahead(i)
            dve.wait_ge(proj_evac, ph["proj0"] + N_IN)
            evac_items(dve, st, sb_items, 1)
            dve.wait_ge(sem("mix2_loaded"), 16 * 12 * (li + 1))
            wait(dve, "pairs_ready", ph)
            for a in range(2):
                for g in range(NG):
                    c = (a * NG + g) * P
                    pairs = ps[:, O_BANK, c:c + P].rearrange("p (m j) -> p m j", j=8)
                    for jh in range(2):
                        last = nc.vector.tensor_tensor(
                            cmp_in[:, a, 8 * jh:8 * jh + 8, g * NB:(g + 1) * NB].rearrange("p j c -> p c j"),
                            pairs[:, jh:jh + NB, :],
                            cmp_pe[:, a, 8 * jh:8 * jh + 8].unsqueeze(1).broadcast_to([P, NB, 8]), ALU.add)
            last.then_inc(ev("cmp_in_ready", ph)[0], 1)
            fill(0)
            nc.vector.tensor_scalar(nsa_gate, proj[:, :, GATES:GATES + 3 * NH], -80.0, None, ALU.max)\
                .then_inc(ev("gates_clamped", ph)[0], 1)
            wait(dve, "qk_sq_ready", ph)
            nc.vector.tensor_reduce(qk_ss, qk_nat, AX.X, ALU.add).then_inc(ev("qk_ss_ready", ph)[0], 1)
            wait(dve, "hidden_ready", ph)
            hid = ps[:, CMP_BANK, 0:4 * NB].rearrange("p (a c) -> p a c", a=2)
            nc.vector.tensor_scalar(cmp_sig, hid, -80.0, None, ALU.max).then_inc(ev("hid_clamped", ph)[0], 1)
            wait(dve, "gates_exp", ph)
            chain(nc.vector.tensor_scalar(nsa_gate, nsa_gate, 1.0, None, ALU.add))
            wait(dve, "hid_exp", ph)
            chain(nc.vector.tensor_scalar(cmp_sig, cmp_sig, 1.0, None, ALU.add))
            chain.wait()
            chain(nc.vector.reciprocal(nsa_gate, nsa_gate))
            chain(nc.vector.reciprocal(cmp_sig, cmp_sig))
            chain.wait()
            chain(nc.vector.tensor_tensor(cmp_hid, hid, cmp_sig, ALU.mult))
            chain.wait()
            nc.vector.tensor_copy(vc_in.rearrange("p (g r c) -> p g r c", g=NG, c=NB),
                                  cmp_hid[:, 1, :].rearrange("p (g c) -> p g c", g=NG).unsqueeze(2)
                                  .broadcast_to([P, NG, NH // NG, NB])).then_inc(ev("hid_ready", ph)[0], 1)
            for half in range(2):
                dve.wait_ge(sem("sb_ln_ready"), 2 * li + half + 1)
                out_ = sb_view(ptb, half)
                for h in range(2):
                    chain(nc.vector.scalar_tensor_tensor(out_[:, h], ps[:, 2 * half + h, 0:3 * P], 0.0,
                                                         sb_view(pb, half)[:, h], ALU.max, ALU.add))
                chain.wait()
                for h in range(2):
                    d_ = sb_diag(ptb, half)[h]
                    last = nc.vector.tensor_tensor(d_, d_, const("past").unsqueeze(1).broadcast_to([P, 2, P]),
                                                   ALU.mult)
                last.then_inc(sem("sb_sp_ready"), 1)
            fill(1)
            wait(dve, "qk_rstd_ready", ph)
            for h0, n, c0, _ in qk_load:
                chain(nc.vector.tensor_tensor(qk_nat[:, :, h0:h0 + n, :],
                                              proj[:, :, c0:c0 + n * HD].rearrange("p t (h d) -> p t h d", d=HD),
                                              qk_ss[:, :, h0:h0 + n].unsqueeze(3).broadcast_to([P, NT, n, HD]),
                                              ALU.mult))
            chain.wait()
            for h0, n, _, g in qk_groups:
                v = qk_nat[:, :, h0:h0 + n, :]
                chain(nc.vector.tensor_tensor(v, v, head_gain[:, g, :].unsqueeze(1).unsqueeze(1)
                                              .broadcast_to([P, NT, n, HD]), ALU.mult))
            chain.wait()
            fill(2)
            wait(dve, "sb_out_ready", ph)
            chain(nc.vector.tensor_copy(o_all[:, :, 0:256],
                                        ps[:, O_BANK, :].rearrange("p (t n) -> p t n", t=NT)))
            rope(dve, chain, qk_nat, NQK, 8, const("cos16"), const("sin16"), pb, ev("qk_ready", ph)[0])
            wait(dve, "qk_ready", ph)
            wait(dve, "kcvc_ready", ph)
            chain(nc.vector.tensor_copy(kc, ps[0:2 * NB, CMP_BANK, 128:128 + HD]))
            chain(nc.vector.tensor_tensor(v_diag, ps[0:NH * NB, CMP_BANK + 1, 0:HD].unsqueeze(1)
                                          .broadcast_to([NH * NB, NH, HD]),
                                          const("headdiag", NH * NB).unsqueeze(2)
                                          .broadcast_to([NH * NB, NH, HD]), ALU.mult))
            chain.wait()
            chain(nc.vector.tensor_tensor(kc_sq, kc, kc, ALU.mult))
            chain.wait()
            nc.vector.tensor_reduce(kc_ss, kc_sq, AX.X, ALU.add).then_inc(ev("kc_ss_ready", ph)[0], 1)
            fill(3)
            wait(dve, "kc_rstd_ready", ph)
            chain(nc.vector.scalar_tensor_tensor(kc, kc, kc_ss, cmp_gain[0:2 * NB], ALU.mult, ALU.mult))
            chain.wait()
            cs, sn = const("coscmp", 2 * NB), const("sincmp", 2 * NB)
            for i, (half_, tab) in enumerate(((0, cs), (1, sn), (1, cs), (0, sn))):
                chain(nc.vector.tensor_tensor(kc_rot[:, 8 * i:8 * i + 8], kc[:, 8 * half_:8 * half_ + 8], tab,
                                              ALU.mult))
            chain.wait()
            nc.vector.tensor_tensor(kc[:, 0:8], kc_rot[:, 0:8], kc_rot[:, 8:16], ALU.subtract)
            nc.vector.tensor_tensor(kc[:, 8:16], kc_rot[:, 16:24], kc_rot[:, 24:32], ALU.add)\
                .then_inc(ev("kc_ready", ph)[0], 1)
            evac_items(dve, st, qk_items, 1)
            rope(dve, chain, proj[:, :, IQ:IW].rearrange("p t (h d) -> p t h d", d=IXD), IXH + 1, 4,
                 const("cos8"), const("sin8"), pb[:, 884:1268],
                 ev("ix_rope_ready", ph)[0])
            chain(nc.vector.tensor_scalar(ix_w, proj[:, :, IW:IW + IXH], IXH ** -0.5, IXD ** -0.5,
                                          ALU.mult, ALU.mult))
            wait(dve, "cmp_scores", ph)
            shape = [P, NT, NH, NB]
            vis = const("cmpvis").rearrange("p (t c) -> p t c", t=NT).unsqueeze(2).broadcast_to(shape)
            bias = const("cmpbias").rearrange("p (t c) -> p t c", t=NT).unsqueeze(2).broadcast_to(shape)
            sc = ps[:, CMP_BANK, 0:NT * NH * NB].rearrange("p (t h c) -> p t h c", t=NT, h=NH)
            chain(nc.vector.tensor_tensor(cmp_s, sc, bias, ALU.add))
            chain.wait()
            chain(nc.vector.tensor_reduce(cmp_max, cmp_s, AX.X, ALU.max))
            chain.wait()
            nc.vector.tensor_tensor(cmp_s, cmp_s, cmp_max.unsqueeze(3).broadcast_to(shape), ALU.subtract)\
                .then_inc(ev("cmp_shifted", ph)[0], 1)
            wait(dve, "cmp_exp", ph)
            chain(nc.vector.tensor_tensor(cmp_s, cmp_s, vis, ALU.mult))
            chain.wait()
            chain(nc.vector.tensor_reduce(cmp_den, cmp_s, AX.X, ALU.add))
            chain.wait()
            chain(nc.vector.tensor_scalar(cmp_zero, cmp_den, 0.0, None, ALU.is_equal))
            chain.wait()
            chain(nc.vector.tensor_tensor(cmp_den, cmp_den, cmp_zero, ALU.add))
            chain.wait()
            chain(nc.vector.reciprocal(cmp_den, cmp_den))
            chain.wait()
            nc.vector.tensor_tensor(cmp_s, cmp_s, cmp_den.unsqueeze(3).broadcast_to(shape), ALU.mult)\
                .then_inc(ev("cmp_p_ready", ph)[0], 1)
            fill(4)
            evac_items(dve, st, ix_items, 1)
            wait(dve, "cmp_out_ready", ph)
            for t in range(NT):
                chain(nc.vector.tensor_tensor(o_all[:, t, 256:768].rearrange("p (h d) -> p h d", h=NH),
                                              ps[:, CMP_BANK + t, :].rearrange("p (h d) -> p h d", h=NH),
                                              gates[:, t, :, 0].unsqueeze(2).broadcast_to([P, NH, HD]), ALU.mult))
            fill(5)
            tiles = (slice(0, P), slice(P, 3 * P))
            for h in range(IXH):
                dve.wait_ge(sem("ix_relu_ready"), IXH * li + h + 1)
                for t in range(NT):
                    r, w_ = ix_relu[h % 2][:, tiles[t]], ix_w[:, t, h:h + 1]
                    dst = ix_score[:, tiles[t]]
                    if h == 0:
                        last = nc.vector.tensor_scalar(dst, r, w_, None, ALU.mult)
                    else:
                        last = nc.vector.scalar_tensor_tensor(dst, r, w_, dst, ALU.mult, ALU.add)
                last.then_inc(sem("ix_added"), 1)
                dve.wait_ge(sem("ix_added"), IXH * li + h + 1)
            for c in (0, 2 * P):
                chain(nc.vector.tensor_tensor(ix_score[:, c:c + P], ix_score[:, c:c + P], const("causal"), ALU.add))
            chain.wait()
            for r in range(TOPK // 8):
                if r in (1, 3, 5):
                    fill(6 + r // 2)
                for t in range(NT):
                    src = ix_score if r == 0 else ix_val
                    chain(nc.vector.max(top8[t], src[:, tiles[t]]))
                chain.wait()
                for t in range(NT):
                    src = ix_score if r == 0 else ix_val
                    chain(nc.vector.match_replace(ix_val[:, tiles[t]], top8[t], src[:, tiles[t]], TAKEN))
                chain.wait()
            chain(nc.vector.tensor_scalar(ix_val, ix_val, TAKEN, -1.0, ALU.is_equal, ALU.add))
            chain.wait()
            chain(nc.vector.tensor_scalar(ix_val, ix_val, -NEG, None, ALU.mult))
            chain.wait()
            for c in (0, 2 * P):
                chain(nc.vector.tensor_tensor(sel_mask[:, c:c + P], ix_val[:, c:c + P], const("causal"), ALU.add))
            nc.vector.tensor_copy(sel_mask[:, P:2 * P], ix_val[:, P:2 * P]).then_inc(ev("mask_ready", ph)[0], 1)
            sel, win, dsa = attentions(ph)
            dve_attention(dve, chain, sel, lambda b: fill(9 + b) if b < 3 else None)
            dve_attention(dve, chain, win)
            dve_attention(dve, chain, dsa)
            dve.wait_ge(att_out, ph["B0"] + 10)
            for t in range(NT):
                nc.vector.tensor_copy(stats[:, 91 + t:92 + t], o_all[:, t, 0:1]).then_inc(xn_ready, 1)
            ahead(23)
            dve_transposed(dve, ph["t0"] + 1)
            for br in range(3):
                if br == 1:
                    ahead(24)
                dve.wait_ge(sem("gate_sigmoid"), 3 * li + br + 1)
                last_unit = u0 + (23, 25, 26)[br]
                if br == 2:
                    ahead(25)
                dve.wait_ge(unit_used, last_unit + 1)
                for t in range(NT):
                    g_ = gate_or_gain[:, t, br * D:(br + 1) * D]
                    bank = (0, 4, 0)[br] + 2 * t
                    chain_src = ps[:, bank:bank + 2, :].rearrange("p b n -> p (b n)")
                    last = nc.vector.tensor_tensor(g_, chain_src, g_, ALU.mult)
                    if br == 1 and t == 1:
                        last.then_inc(ev("gated_ready", ph)[0], 1)
                    else:
                        last.then_inc(sem("gated"), 1)
            ahead(26)
            for t in range(NT):
                dve.wait_ge(sem("merged_ab"), 2 * li + t + 1)
                dve.wait_ge(sem("gated"), 5 * (li + 1))
                nc.vector.tensor_tensor(xn[:, t, :], xn[:, t, :], gate_or_gain[:, t, 2 * D:3 * D], ALU.add)\
                    .then_inc(xn_ready, 1)
            dve_transposed(dve, ph["t0"] + 2)
            for i in range(27, 31):
                ahead(i)
            dve_post(dve, chain, ph, u0 + 30)


        block = ctx.enter_context(nc.Block())

        @block.sync
        def _(sp):
            sp.dma_start(x[:, :, :], A["x"][0].rearrange("(t p) d -> p t d", p=P)).then_inc(x_loaded, 16)
            for ph in info:
                if ph["kind"] == "ffn":
                    sp_ffn(sp, ph)
                elif ph["kind"] == "mix1":
                    sp_mix1(sp, ph)
                else:
                    sp_mix2(sp, ph)
            for t in range(NT):
                sp.wait_ge(x_ready, n_x + t + 1)
                sp.dma_start(out[0, t * P:(t + 1) * P, :], x[:, t, :]).then_inc(stored, 16)
            sp.wait_ge(stored, 16 * NT)

        @block.gpsimd
        def _(pool):
            chain = Chain(pool, sem("pool_chain"))
            chain(nc.gpsimd.memset(minus_half, -0.5))
            chain.wait()
            n_const = consts.shape[1]
            pool.dma_start(consts[:, :], A["const_table"][:, 0:n_const]).then_inc(const_loaded, 16)
            pool.dma_start(tmp[:, 0:P], A["const_table"][:, n_const:n_const + P]).then_inc(const_loaded, 16)
            pool.dma_start(gains[:, :, :], A["gains"]).then_inc(const_loaded, 16)
            for ph in info:
                if ph["post"]:
                    if ph["post0"] > 0:
                        pool.wait_ge(x_ready, ph["x0"] + 2)
                    pool.dma_start(post_gain, A[ph["post"]][0].partition_broadcast(P))\
                        .then_inc(gain_loaded, 16)
                pool_rstd(pool, chain, ph["ss0"])
                if ph["kind"] == "mix1":
                    pool_mix1(pool, chain, ph)
                if ph["kind"] == "mix2":
                    pool_mix2(pool, chain, ph)
                if ph["post"]:
                    pool_rstd(pool, chain, ph["ss0"] + 2)

        @block.tensor
        def _(pe):
            pe.wait_ge(const_loaded, N_CONST)
            pe.wait_ge(sem("masks_ready"), 1)
            for ph in info:
                if ph["kind"] == "ffn":
                    pe_ffn(pe, ph)
                elif ph["kind"] == "mix1":
                    pe_mix1(pe, ph)
                else:
                    pe_mix2(pe, ph)

        @block.scalar
        def _(act):
            chain = Chain(act, sem("act_chain"))
            split_hi(act, 0, width=width_of(0))
            split_hi(act, 1, width=width_of(1))
            for ph in info:
                if ph["kind"] == "ffn":
                    act_ffn(act, ph)
                elif ph["kind"] == "mix1":
                    act_mix1(act, chain, ph)
                else:
                    act_mix2(act, chain, ph)

        @block.vector
        def _(dve):
            chain = Chain(dve, sem("dve_chain"))
            dve.wait_ge(x_loaded, 16)
            dve.wait_ge(const_loaded, N_CONST)
            nc.vector.tensor_copy(ident_bf, ident)
            nc.vector.tensor_copy(causal_bf, const("causal"))
            nc.vector.tensor_copy(notpast_bf, tmp[:, 0:P]).then_inc(sem("masks_ready"), 1)
            for t in range(NT):
                nc.vector.tensor_copy(stats[:, 93 + t:94 + t], x[:, t, 0:1]).then_inc(x_ready, 1)
            split_lo(dve, 0, width=width_of(0))
            split_lo(dve, 1, width=width_of(1))
            for ph in info:
                if ph["kind"] == "ffn":
                    dve_ffn(dve, chain, ph)
                elif ph["kind"] == "mix1":
                    dve_mix1(dve, chain, ph)
                else:
                    dve_mix2(dve, chain, ph)


FFN = {"kind": "ffn", "gu": None, "post": None, "weight": 0.5}
PLAN = [
    {**FFN, "l": 0, "gate": "ffn1_w_gate", "up": "ffn1_w_up", "down": "ffn1_w_down", "post": "ffn1_post_g",
     "gain": 0},
    {"kind": "mix1", "l": 0, "gain": 1, "post": "mix_post_g", "weight": 1.0},
    {**FFN, "l": 0, "gate": "ffn2_w_gate", "up": "ffn2_w_up", "down": "ffn2_w_down", "post": "ffn2_post_g",
     "gain": 2},
]
GAINS = [("ffn1_pre_g", 0), ("mix_pre_g", 0), ("ffn2_pre_g", 0)]
for _l in range(2):
    PLAN += [
        {**FFN, "l": _l, "gu": "ffn1_w_gu_2", "down": "ffn1_w_down_2", "gain": 3 + 3 * _l},
        {"kind": "mix2", "l": _l, "gain": 4 + 3 * _l, "post": None, "weight": 1.0},
        {**FFN, "l": _l, "gu": "ffn2_w_gu_2", "down": "ffn2_w_down_2", "gain": 5 + 3 * _l},
    ]
    GAINS += [("ffn1_norm_2", _l), ("mix_norm_2", _l), ("ffn2_norm_2", _l)]
NGAIN = len(GAINS)
N_CONST = 16 * 3
UNITS1 = 17
UNITS2 = 31


def kernel(**inputs):
    from concourse import bacc
    from concourse.bass_utils import run_bass_kernel_spmd

    nc = bacc.Bacc("TRN2", target_bir_lowering=False, num_devices=1)
    const_table, place = const_arrays()
    arrays = {k: np.ascontiguousarray(v) for k, v in inputs.items()}
    arrays["gains"] = np.ascontiguousarray(
        np.stack([arrays[name][l].reshape(KC, P) for name, l in GAINS]).transpose(2, 0, 1))
    arrays["cmp_pe"] = np.ascontiguousarray(
        arrays["nsa_cmp_pe_2"].reshape(2, 2, 16, 2, HD).transpose(0, 1, 3, 4, 2).reshape(2, 2, P, 16))
    arrays["const_table"] = const_table
    A = {k: nc.dram_tensor("in_" + k, v.shape, mybir.dt.from_np(v.dtype), kind="ExternalInput").ap()
         for k, v in arrays.items()}
    out = nc.dram_tensor("out_0", (1, S, D), F32, kind="ExternalOutput").ap()
    build(nc, A, place, out)
    r = run_bass_kernel_spmd(nc, [{"in_" + k: v for k, v in arrays.items()}], core_ids=[0])
    return r.results[0]["out_0"]
```

```python
from contextlib import ExitStack

import numpy as np

import concourse.bass as bass
from concourse import mybir

F32 = mybir.dt.float32
F32R = mybir.dt.float32r
BF16 = mybir.dt.bfloat16
ALU = mybir.AluOpType
ACT = mybir.ActivationFunctionType
AX = mybir.AxisListType

P = 128
S = 256
NT = S // P
D = 1024
KC = D // P
DFF = 2816
STEP_F = 256
STEPS = DFF // STEP_F
UNIT = 2048
SLOTS = 3
EPS = 1e-6
NEG = -1.0e30
TAKEN = -3.0e38
HD = 64
SCALE = HD ** -0.5


class Chain:

    def __init__(self, eng, sem):
        self.eng, self.sem, self.n = eng, sem, 0

    def __call__(self, ins):
        ins.then_inc(self.sem, 1)
        self.n += 1

    def wait(self):
        self.eng.wait_ge(self.sem, self.n)


def const_arrays():
    j = np.arange(P)[:, None]
    t = np.arange(P)[None, :]
    cols = {}
    cols["ident"] = np.eye(P)
    cols["cumsum"] = (j <= t) * 1.0
    cols["ones"] = np.ones((P, P))
    cols["ones_neg"] = -np.ones((P, P))
    cols["tail_neg"] = (j >= t) * -1.0
    cols["past"] = (j < t) * 1.0
    cols["causal"] = (t > j) * NEG

    def rope(pos, dim):
        inv = np.float32(500000.0) ** (-np.arange(0, dim, 2, dtype=np.float32) / np.float32(dim))
        ang = pos.astype(np.float32)[:, None] * inv.astype(np.float32)[None, :]
        return np.cos(ang.astype(np.float32)), np.sin(ang.astype(np.float32))

    pos = np.arange(S)
    for name, dim in (("16", 16), ("8", 8)):
        c, s = rope(pos, dim)
        for nm, v in (("cos", c), ("sin", s)):
            cols[nm + name] = v.reshape(NT, P, dim // 2).transpose(1, 0, 2).reshape(P, -1)
    nc_blocks = S // 16 - 1
    c, s = rope(np.arange(nc_blocks) * 16 + 31, 16)
    for nm, v in (("coscmp", c), ("sincmp", s)):
        full = np.zeros((P, 8))
        full[:2 * nc_blocks] = np.tile(v, (2, 1))
        cols[nm] = full
    end = np.arange(nc_blocks) * 16 + 31
    vis = (end[None, None, :] <= (np.arange(NT)[None, :, None] * P + np.arange(P)[:, None, None]))
    cols["cmpvis"] = (vis * 1.0).reshape(P, -1)
    cols["cmpbias"] = ((~vis) * NEG).reshape(P, -1)
    bd = np.zeros((P, 8))
    for h in range(8):
        bd[h * nc_blocks:(h + 1) * nc_blocks, h] = 1.0
    cols["headdiag"] = bd
    place, at = {}, 0
    for name, v in cols.items():
        place[name] = (at, v.shape[1])
        at += v.shape[1]
    table = np.concatenate([v for v in cols.values()] + [(j >= t) * NEG], axis=1).astype(np.float32)
    return table, place


def build(nc, A, place, out):
    with ExitStack() as ctx:
        sems = {}

        def sem(name):
            if name not in sems:
                sems[name] = ctx.enter_context(nc.semaphore(name))
            return sems[name]

        def sb(name, shape, dt=F32):
            return ctx.enter_context(nc.sbuf_tensor(name, shape, dt))

        raw = [sb(f"raw{i}", [P, UNIT]) for i in range(SLOTS)]
        w_hi = [sb(f"w_hi{i}", [P, UNIT], F32R) for i in range(SLOTS)]
        w_lo = [sb(f"w_lo{i}", [P, UNIT], F32R) for i in range(SLOTS)]
        aT_hi = sb("aT_hi", [P, KC, S], F32R)
        aT_lo = sb("aT_lo", [P, KC, S], F32R)
        act_hi = [sb(f"act_hi{i}", [P, 2, S], F32R) for i in range(2)]
        act_lo = [sb(f"act_lo{i}", [P, 2, S], F32R) for i in range(2)]
        x = sb("x", [P, NT, D])
        tmp = sb("tmp", [P, 2304])
        qk_t = sb("qk_t", [P, 17, S])
        consts = sb("consts", [P, max(a + w for a, w in place.values())])
        cbf = sb("cbf", [P, 3 * P], BF16)
        gains = sb("gains", [P, NGAIN, KC])
        stats = sb("stats", [P, 96])
        gate_or_gain = sb("gate_or_gain", [P, NT, 3 * D])
        proj = sb("proj", [P, NT, 3080])
        o_all = sb("o_all", [P, NT, D])
        p_buf = sb("p_buf", [P, 2, 2, 384])
        pt_buf = sb("pt_buf", [P, 2, 2, 384])
        sb_mask = sb("sel_mask", [P, 3 * P], BF16)
        small = sb("small", [P, 700])
        ps = ctx.enter_context(nc.psum_tensor("ps", [P, 8, 512], F32))

        xn = qk_t[:, 0:8, :].rearrange("p a b -> p (a b)").rearrange("p (t d) -> p t d", t=NT)
        post_gain = gate_or_gain[:, 1, 0:D]
        sg = [tmp[:, i * 512:(i + 1) * 512].rearrange("p (f s) -> p f s", f=2) for i in range(2)]
        minus_half = stats[:, 95:96]
        notpast = small[:, 0:P]

        def const(name, rows=P):
            a, w = place[name]
            return consts[0:rows, a:a + w]

        ident = const("ident")
        ident_bf = cbf[:, 0:P]
        causal_bf = cbf[:, P:2 * P]
        notpast_bf = cbf[:, 2 * P:3 * P]

        def acc(t):
            return ps[:, 2 * t:2 * t + 2, :].rearrange("p b n -> p (b n)")

        def gu(par):
            return ps[:, 4 + 2 * par:6 + 2 * par, :].rearrange("p f (g s) -> p f g s", g=2)

        def tp(q):
            return ps[:, 4 + q, :].rearrange("p (c s) -> p c s", c=4)

        def tmp_quarter(q):
            return tmp[:, q * 512:(q + 1) * 512].rearrange("p (c s) -> p c s", c=4)

        def a_quarter(a, q):
            t, c = q // 2, 4 * (q % 2)
            return a[:, c:c + 4, t * P:(t + 1) * P]

        raw_loaded = [sem(f"raw_loaded{i}") for i in range(SLOTS)]
        hi_ready, lo_ready, unit_used = sem("hi_ready"), sem("lo_ready"), sem("unit_used")
        silu_ready, act_ready = sem("silu_ready"), sem("act_ready")
        act_hi_ready, act_lo_ready = sem("act_hi_ready"), sem("act_lo_ready")
        ss_ready, rstd_ready, x_ready = sem("ss_ready"), sem("rstd_ready"), sem("x_ready")
        xn_ready, tp_done, tmp_ready = sem("xn_ready"), sem("tp_done"), sem("tmp_ready")
        out_t0_ready = sem("out_t0_ready")
        aT_hi_ready, aT_ready = sem("aT_hi_ready"), sem("aT_ready")
        first_loaded, const_loaded, gain_loaded, stored = (sem("first_loaded"), sem("const_loaded"),
                                                           sem("gain_loaded"), sem("stored"))
        x_loaded = [sem(f"x_loaded{t}") for t in range(NT)]

        phases = PLAN
        n_units = 0
        n_b = n_item = n_proj = n_mix2 = 0
        n_x = n_t = n_post = steps = 0
        info = []
        for ph in phases:
            ph = dict(ph)
            ph["u0"], ph["t0"], ph["x0"], ph["s0"], ph["post0"] = n_units, n_t, n_x, steps, n_post
            ph["B0"], ph["item0"], ph["proj0"], ph["mix2_before"] = n_b, n_item, n_proj, n_mix2
            kind = ph["kind"]
            n_b += {"ffn": 0, "mix1": 8, "mix2": 10}[kind]
            n_item += {"ffn": 0, "mix1": 16, "mix2": 18}[kind]
            n_proj += {"ffn": 0, "mix1": 13, "mix2": 23}[kind]
            n_mix2 += kind == "mix2"
            ph["index"] = len(info)
            n_units += {"ffn": 3 * STEPS, "mix1": UNITS1, "mix2": UNITS2}[kind]
            n_t += {"ffn": 1, "mix1": 2, "mix2": 3}[kind]
            n_x += 2
            n_post += 1 if ph["post"] else 0
            steps += STEPS if kind == "ffn" else 0
            ph["u_end"] = n_units
            info.append(ph)

        n_ss = 0
        for prev, ph in zip([None] + info, info + [None]):
            for t in range(NT):
                if prev and prev["post"]:
                    prev.setdefault("post_c", []).append(n_ss)
                    n_ss += 1
                if ph:
                    ph.setdefault("pre_c", []).append(n_ss)
                    n_ss += 1

        def raw_count(n):
            return 16 * (n // SLOTS + 1)

        def load(sp, n, src, slot=None):
            k = n % SLOTS if slot is None else slot
            if slot is not None or n >= SLOTS:
                sp.wait_ge(lo_ready, n - (SLOTS - 1))
            width = 1
            for w in src.shape[1:]:
                width *= w
            dst = raw[k][:, 0:width]
            if len(src.shape) == 3:
                dst = dst.rearrange("p (a b) -> p a b", a=src.shape[1])
            sp.dma_start(dst, src).then_inc(raw_loaded[k], 16)

        def split_hi(act, n, width=UNIT, slot=None, loads=None):
            k = n % SLOTS if slot is None else slot
            if slot is None and n >= n_units:
                return
            act.wait_ge(raw_loaded[k], raw_count(n) if loads is None else 16 * loads)
            if slot is not None or n >= SLOTS:
                act.wait_ge(unit_used, n - (SLOTS - 1))
            nc.scalar.activation(w_hi[k][:, 0:width], raw[k][:, 0:width], ACT.Copy).then_inc(hi_ready, 1)

        def split_lo(dve, n, width=UNIT, slot=None):
            k = n % SLOTS if slot is None else slot
            if slot is None and n >= n_units:
                return
            dve.wait_ge(hi_ready, n + 1)
            nc.vector.tensor_tensor(w_lo[k][:, 0:width], raw[k][:, 0:width],
                                    w_hi[k][:, 0:width].bitcast(F32), ALU.subtract).then_inc(lo_ready, 1)

        def act_prenorm(act, ph, t):
            act.wait_ge(x_ready, ph["x0"] + t + 1)
            c = ph["pre_c"][t]
            nc.scalar.activation(xn[:, t, :], x[:, t, :], ACT.Square,
                                 accum_out=stats[:, c:c + 1]).then_inc(ss_ready, 1)

        def pool_rstd(pool, chain, c):
            pool.wait_ge(ss_ready, c + 1)
            chain(nc.gpsimd.tensor_scalar(stats[:, c:c + 1], stats[:, c:c + 1], 1.0 / D, EPS, ALU.mult, ALU.add))
            chain.wait()
            nc.gpsimd.tensor_tensor(stats[:, c:c + 1], stats[:, c:c + 1], minus_half, ALU.pow)\
                .then_inc(rstd_ready, 1)

        def pool_boundary(pool, chain, prev, ph):
            for t in range(NT):
                if prev and prev["post"]:
                    pool_rstd(pool, chain, prev["post_c"][t])
                if ph:
                    pool_rstd(pool, chain, ph["pre_c"][t])

        def dve_prenorm(dve, ph, t):
            c = ph["pre_c"][t]
            dve.wait_ge(rstd_ready, c + 1)
            nc.vector.tensor_scalar(xn[:, t, :], x[:, t, :], stats[:, c:c + 1], None, ALU.mult)\
                .then_inc(xn_ready, 1)

        def pe_transpose(pe, inst, src, t):
            pe.wait_ge(xn_ready, 2 * inst + t + 1)
            for q in (2 * t, 2 * t + 1):
                for c in range(4):
                    k = 4 * (q % 2) + c
                    last = nc.tensor.transpose(tp(q)[:, c, :], src[:, t, k * P:(k + 1) * P], ident)
                last.then_inc(tp_done, 1)

        def pe_wait_aT(pe, inst, t):
            pe.wait_ge(aT_ready, 4 * inst + 2 * t + 2)

        def dve_transposed(dve, inst, t, gain=None):
            for q in (2 * t, 2 * t + 1):
                dve.wait_ge(tp_done, 4 * inst + q + 1)
                if gain is None:
                    nc.vector.tensor_copy(tmp_quarter(q), tp(q)).then_inc(tmp_ready, 1)
                else:
                    c = 4 * (q % 2)
                    nc.vector.tensor_tensor(tmp_quarter(q), tp(q), gains[:, gain, c:c + 4].unsqueeze(2)
                                            .broadcast_to([P, 4, P]), ALU.mult).then_inc(tmp_ready, 1)
            for q in (2 * t, 2 * t + 1):
                dve.wait_ge(aT_hi_ready, 4 * inst + q + 1)
                nc.vector.tensor_tensor(a_quarter(aT_lo, q), tmp_quarter(q), a_quarter(aT_hi, q).bitcast(F32),
                                        ALU.subtract).then_inc(aT_ready, 1)

        def act_transposed(act, inst, t):
            for q in (2 * t, 2 * t + 1):
                act.wait_ge(tmp_ready, 4 * inst + q + 1)
                nc.scalar.activation(a_quarter(aT_hi, q), tmp_quarter(q), ACT.Copy).then_inc(aT_hi_ready, 1)

        def wait_output(eng, ph, t):
            if t == 0:
                eng.wait_ge(out_t0_ready, ph["index"] + 1)
            else:
                eng.wait_ge(unit_used, ph["u_end"])

        def act_post(act, ph, t):
            wait_output(act, ph, t)
            c = ph["post_c"][t]
            nc.scalar.activation(xn[:, t, :], acc(t), ACT.Square, accum_out=stats[:, c:c + 1]).then_inc(ss_ready, 1)

        def dve_post(dve, chain, ph, t):
            wait_output(dve, ph, t)
            src, weight = acc(t), ph["weight"]
            if ph["post"]:
                c = ph["post_c"][t]
                dve.wait_ge(gain_loaded, 16 * (ph["post0"] + 1))
                dve.wait_ge(rstd_ready, c + 1)
                chain(nc.vector.scalar_tensor_tensor(xn[:, t, :], acc(t), stats[:, c:c + 1], post_gain,
                                                     ALU.mult, ALU.mult))
                chain.wait()
                src = xn[:, t, :]
            nc.vector.scalar_tensor_tensor(x[:, t, :], src, weight, x[:, t, :], ALU.mult, ALU.add)\
                .then_inc(x_ready, 1)

        def split_after(ph):
            return 1 if ph and ph["kind"] == "ffn" else 0

        def act_boundary(act, prev, ph):
            for t in range(NT if prev is None else 0):
                act_prenorm(act, ph, t)
            for t in range(NT):
                if prev and prev["post"]:
                    act_post(act, prev, t)
                if ph and prev:
                    act_prenorm(act, ph, t)
                if ph:
                    act_transposed(act, ph["t0"], t)
                if prev and t == split_after(ph):
                    split_hi(act, prev["u_end"] + 1, width=width_of(prev["u_end"] + 1))

            for n in range(2 if prev is None else 0):
                split_hi(act, n, width=width_of(n))

        def dve_boundary(dve, chain, prev, ph):
            for t in range(NT if prev is None else 0):
                dve_prenorm(dve, ph, t)
            for t in range(NT):
                if prev:
                    dve_post(dve, chain, prev, t)
                if ph and prev:
                    dve_prenorm(dve, ph, t)
                if ph:
                    dve_transposed(dve, ph["t0"], t, ph["gain"])
                if prev and t == split_after(ph):
                    split_lo(dve, prev["u_end"] + 1, width=width_of(prev["u_end"] + 1))
            for n in range(2 if prev is None else 0):
                split_lo(dve, n, width=width_of(n))

        def pe_begin(pe, inst, src, part, transposed=()):
            for t in range(NT):
                if t not in transposed:
                    pe_transpose(pe, inst, src, t)
                pe_wait_aT(pe, inst, t)
                part(0, t)
                part(1, t)

        def ffn_src(ph):
            if ph["gu"] is None:
                wg, wu = A[ph["gate"]][ph["l"]], A[ph["up"]][ph["l"]]
            else:
                both = A[ph["gu"]][ph["l"]]
                wg, wu = both[:, 0:DFF], both[:, DFF:2 * DFF]
            return (wg.rearrange("(k p) f -> p k f", p=P), wu.rearrange("(k p) f -> p k f", p=P),
                    A[ph["down"]][ph["l"]].rearrange("(c p) n -> p c n", p=P))

        def sp_ffn(sp, ph):
            wg, wu, wd = ffn_src(ph)
            u0 = ph["u0"]
            load(sp, u0, wg[:, :, 0:STEP_F])
            load(sp, u0 + 1, wu[:, :, 0:STEP_F])
            first = 1
            if u0 == 0:
                load(sp, 2, wg[:, :, STEP_F:2 * STEP_F])
                load(sp, 3, wu[:, :, STEP_F:2 * STEP_F])
                load(sp, 4, wd[:, 0:2, :])
                first = 2
            with sp.Fori(first, STEPS) as s:
                load(sp, 3 * s + (u0 - 1), wg[:, :, bass.ds(s * STEP_F, STEP_F)], slot=(u0 - 1) % SLOTS)
                load(sp, 3 * s + u0, wu[:, :, bass.ds(s * STEP_F, STEP_F)], slot=u0 % SLOTS)
                load(sp, 3 * s + (u0 + 1), wd[:, bass.ds(2 * s - 2, 2), :], slot=(u0 + 1) % SLOTS)
            load(sp, u0 + 3 * STEPS - 1, wd[:, 2 * STEPS - 2:2 * STEPS, :])

        def pe_gate_up_unit(pe, n, slot, par, g):
            pe.wait_ge(lo_ready, n + 1)
            hi = w_hi[slot][:, :].rearrange("p (k f) -> p k f", k=KC)
            lo = w_lo[slot][:, :].rearrange("p (k f) -> p k f", k=KC)
            for f in range(2):
                dst = gu(par)[:, f, g, :]
                for k in range(KC):
                    cols = slice(f * P, (f + 1) * P)
                    nc.tensor.matmul(dst, hi[:, k, cols], aT_hi[:, k, :], start=k == 0, stop=False)
                    nc.tensor.matmul(dst, hi[:, k, cols], aT_lo[:, k, :], start=False, stop=False)
                    last = nc.tensor.matmul(dst, lo[:, k, cols], aT_hi[:, k, :], start=False, stop=k == KC - 1)
            return last

        def pe_gate_up(pe, ph, s, par, in_loop=False):
            u0 = ph["u0"]
            if in_loop or ph["s0"] + s >= 2:
                pe.wait_ge(act_ready, s + (ph["s0"] - 1))
            for g in range(2):
                pe_gate_up_unit(pe, 3 * s + (u0 - 1 + g), (u0 - 1 + g) % SLOTS, par, g).then_inc(unit_used, 1)

        def pe_rows(pe, n, slot, hi_a, lo_a, banks, first, last, tiles=(0, 1), between=None):
            pe.wait_ge(lo_ready, n + 1)
            hi = w_hi[slot][:, :].rearrange("p (c n) -> p c n", c=2)
            lo = w_lo[slot][:, :].rearrange("p (c n) -> p c n", c=2)
            for t in tiles:
                toks = slice(t * P, (t + 1) * P)
                for h in range(2):
                    if h == 1 and between is not None:
                        between()
                    dst = ps[:, banks + 2 * t + h, :]
                    cols = slice(h * 512, (h + 1) * 512)
                    for c in range(2):
                        nc.tensor.matmul(dst, hi_a[:, c, toks], hi[:, c, cols], start=first and c == 0, stop=False)
                        nc.tensor.matmul(dst, hi_a[:, c, toks], lo[:, c, cols], start=False, stop=False)
                        mm = nc.tensor.matmul(dst, lo_a[:, c, toks], hi[:, c, cols], start=False,
                                              stop=last and c == 1)
            return mm

        def pe_down(pe, ph, s, par, first=False):
            n = 3 * s + (ph["u0"] + 1)
            pe.wait_ge(act_lo_ready, s + ph["s0"])
            pe_rows(pe, n, (ph["u0"] + 1) % SLOTS, act_hi[par], act_lo[par], 0, first, False)\
                .then_inc(unit_used, 1)

        def pe_last_rows(pe, ph, parts):
            n = ph["u_end"] - 2

            def transpose_next():
                if ph["index"] + 1 < len(info):
                    pe_transpose(pe, info[ph["index"] + 1]["t0"], xn, 0)
            for t in range(NT):
                for i, (wait_, hi_a, lo_a) in enumerate(parts):
                    if wait_ is not None and t == 0:
                        pe.wait_ge(*wait_)
                    mm = pe_rows(pe, n + i, (n + i) % SLOTS, hi_a, lo_a, 0, False, i == 1, (t,),
                                 transpose_next if t == 1 and i == 1 else None)
                    if t == 1:
                        mm.then_inc(unit_used, 1)
                    elif i == 1:
                        mm.then_inc(out_t0_ready, 1)

        def issued(ph):
            return (0,) if ph["index"] > 0 else ()

        def pe_ffn(pe, ph):
            u0 = ph["u0"]
            if ph["s0"] > 0:
                pe.wait_ge(act_ready, ph["s0"])

            for t in range(NT):
                if t not in issued(ph):
                    pe_transpose(pe, ph["t0"], xn, t)
            pe_wait_aT(pe, ph["t0"], NT - 1)
            for g in range(2):
                pe_gate_up_unit(pe, u0 + g, (u0 + g) % SLOTS, 0, g).then_inc(unit_used, 1)
            pe_gate_up(pe, ph, 1, 1)
            pe_down(pe, ph, 1, 0, first=True)
            with pe.Fori(2, STEPS - 1, 2) as s:
                for j in range(2):
                    pe_gate_up(pe, ph, s + j, j, in_loop=True)
                    pe_down(pe, ph, s + j, 1 - j)
            pe_gate_up(pe, ph, STEPS - 1, 0)
            pe_last_rows(pe, ph, [((act_lo_ready, STEPS - 1 + ph["s0"]), act_hi[1], act_lo[1]),
                                  ((act_lo_ready, STEPS + ph["s0"]), act_hi[0], act_lo[0])])

        def act_step(act, ph, s, par, in_loop=False, last=False):
            u0, s0 = ph["u0"], ph["s0"]

            def split(d):
                n = 3 * s + (u0 + d)
                if in_loop:
                    slot = (u0 + d) % SLOTS
                    split_hi(act, n, slot=slot, loads=s + (u0 + d - slot) // SLOTS + 1)
                else:
                    split_hi(act, n, width=width_of(n))
            split(2)
            act.wait_ge(unit_used, (3 * s + u0 + 1) if in_loop or s > 0 else u0 + 2)
            if in_loop or s0 + s >= 2:
                act.wait_ge(act_lo_ready, s + (s0 - 1))
            nc.scalar.activation(sg[par], gu(par)[:, :, 0, :], ACT.Silu).then_inc(silu_ready, 1)
            split(3)
            act.wait_ge(act_ready, s + (s0 + 1))
            nc.scalar.activation(act_hi[par][:, :, :], sg[par], ACT.Copy).then_inc(act_hi_ready, 1)
            if not last:
                split(4)

        def dve_step(dve, ph, s, par, in_loop=False, last=False):
            u0, s0 = ph["u0"], ph["s0"]

            def split(d):
                n = 3 * s + (u0 + d)
                if in_loop:
                    split_lo(dve, n, slot=(u0 + d) % SLOTS)
                else:
                    split_lo(dve, n, width=width_of(n))
            split(2)
            dve.wait_ge(silu_ready, s + (s0 + 1))
            nc.vector.tensor_tensor(sg[par], sg[par], gu(par)[:, :, 1, :], ALU.mult).then_inc(act_ready, 1)
            dve.wait_ge(act_hi_ready, s + (s0 + 1))
            nc.vector.tensor_tensor(act_lo[par][:, :, :], sg[par], act_hi[par][:, :, :].bitcast(F32),
                                    ALU.subtract).then_inc(act_lo_ready, 1)
            split(3)
            if not last:
                split(4)

        def run_steps(eng, ph, step):
            step(eng, ph, 0, 0)
            step(eng, ph, 1, 1)
            with eng.Fori(2, STEPS - 1, 2) as s:
                for j in range(2):
                    step(eng, ph, s + j, j, in_loop=True)
            step(eng, ph, STEPS - 1, 0, last=True)

        widths = {}

        for ph in info:
            if ph["kind"] == "mix1":
                widths[ph["u0"] + 2] = KC * 8

        def width_of(n):
            return widths.get(n, UNIT)

        proj_evac, items_done = sem("proj_evac"), sem("items_done")
        item_act, item_dve = sem("item_act"), sem("item_dve")
        att_scores, att_max, att_exp, att_pt = sem("att_scores"), sem("att_max"), sem("att_exp"), sem("att_pt")
        att_pt_act, att_pt_dve, att_pv, att_out = (sem("att_pt_act"), sem("att_pt_dve"), sem("att_pv"),
                                                   sem("att_out"))
        FILL_BANK, O_BANK = 7, 6

        def proj_psum(bank, w):
            return ps[:, bank, 0:2 * w].rearrange("p (t n) -> p t n", t=NT)

        def sp_cols(sp, n, w_ap, c0, w):
            load(sp, n, w_ap.rearrange("(k p) f -> p k f", p=P)[:, :, c0:c0 + w])

        def sp_rows(sp, n, w_ap, i):
            load(sp, n, w_ap.rearrange("(c p) n -> p c n", p=P)[:, 2 * i:2 * i + 2, :])

        def pe_cols(pe, n, w, bank, evacuated, tiles=(0, 1), between=None):
            if evacuated > 0 and tiles[0] == 0:
                pe.wait_ge(proj_evac, evacuated)
            pe.wait_ge(lo_ready, n + 1)
            hi = w_hi[n % SLOTS][:, 0:KC * w].rearrange("p (k f) -> p k f", k=KC)
            lo = w_lo[n % SLOTS][:, 0:KC * w].rearrange("p (k f) -> p k f", k=KC)
            for t in tiles:
                dst, toks = proj_psum(bank, w)[:, t, :], slice(t * P, (t + 1) * P)
                for k in range(KC):
                    nc.tensor.matmul(dst, aT_hi[:, k, toks], hi[:, k, :], start=k == 0, stop=False)
                    nc.tensor.matmul(dst, aT_hi[:, k, toks], lo[:, k, :], start=False, stop=False)
                    last = nc.tensor.matmul(dst, aT_lo[:, k, toks], hi[:, k, :], start=False, stop=k == KC - 1)
                    if between is not None:
                        between(k)
            if tiles[-1] == NT - 1:
                last.then_inc(unit_used, 1)

        def a_chunks(i):
            return aT_hi[:, 2 * i:2 * i + 2, :], aT_lo[:, 2 * i:2 * i + 2, :]

        def pe_out(pe, ph, inst, src, transposed=()):
            n = ph["u_end"] - 4

            def part(i, t):
                mm = pe_rows(pe, n + i, (n + i) % SLOTS, *a_chunks(i), 0, i == 0, False, (t,))
                if t == NT - 1:
                    mm.then_inc(unit_used, 1)
            pe_begin(pe, inst, src, part, transposed)
            pe_last_rows(pe, ph, [(None, *a_chunks(2)), (None, *a_chunks(3))])

        def act_evac(act, n, dst, w, bank, scale=1.0, skip=0):
            act.wait_ge(unit_used, n + 1)
            src = proj_psum(bank, w)[:, :, skip:]
            if len(dst.shape) == 4:
                src = src.rearrange("p t (h d) -> p t h d", d=dst.shape[3])
            nc.scalar.activation(dst, src, ACT.Copy, scale=scale).then_inc(proj_evac, 1)

        def pe_items(pe, st, items):
            first = st["item"]
            for i, (srcs, dst, _) in enumerate(items):
                m = first + i - 3
                if i >= 4:
                    pe.wait_ge(item_act, (m + 1) // 2)
                    pe.wait_ge(item_dve, m // 2)
                rows = dst.shape[0]
                for j, src in enumerate(srcs):
                    for t in range(NT):
                        c = (j * NT + t) * P
                        last = nc.tensor.transpose(ps[0:rows, i % 4, c:c + P], src[t], ident)
                last.then_inc(items_done, 1)
            st["item"] += len(items)

        def pe_items_left(pe, st):
            pe.wait_ge(item_act, (st["item"] + 1) // 2)
            pe.wait_ge(item_dve, st["item"] // 2)

        def evac_items(eng, st, items, parity):
            for i, (srcs, dst, scale) in enumerate(items):
                m = st["item"] + i
                if m % 2 != parity:
                    continue
                eng.wait_ge(items_done, m + 1)
                rows, n = dst.shape[0], len(srcs)
                src = ps[0:rows, i % 4, 0:n * S].rearrange("p (h s) -> p h s", h=n)
                if parity == 0:
                    nc.scalar.activation(dst, src, ACT.Copy, scale=scale).then_inc(item_act, 1)
                else:
                    nc.vector.tensor_scalar(dst, src, scale, None, ALU.mult).then_inc(item_dve, 1)
            st["item"] += len(items)

        def score_banks(B):
            return ps[:, 2 * (B % 2):2 * (B % 2) + 2, :]

        neg_max = [small[:, 0 + 4 * i:4 + 4 * i] for i in range(2)]
        row_sum = [small[:, 8 + 4 * i:12 + 4 * i] for i in range(2)]
        row_inv = small[:, 16:20]

        def pe_scores(pe, att, b):
            B = att["B0"] + b
            if B >= 2:
                pe.wait_ge(att_exp, 4 * (B - 1))
            if b == att.get("masked_from"):
                pe.wait_ge(*att["mask_ready"])
            for hh in range(2):
                q, k, dst = att["q"](b, hh), att["k"](b, hh), score_banks(B)[:, hh, :]
                mask = att["mask"] if b >= att.get("masked_from", att["n"]) else None
                nc.tensor.matmul(dst[:, 0:P], q[:, 0:P], k[:, 0:P], start=True, stop=False)
                nc.tensor.matmul(dst[:, 0:P], ident_bf, causal_bf if mask is None else mask[:, 0:P],
                                 start=False, stop=True)
                nc.tensor.matmul(dst[:, P:3 * P], q[:, P:S], k, start=True, stop=False)
                if mask is None:
                    last = nc.tensor.matmul(dst[:, 2 * P:3 * P], ident_bf, causal_bf, start=False, stop=True)
                else:
                    last = nc.tensor.matmul(dst[:, P:3 * P], ident_bf, mask[:, P:3 * P], start=False, stop=True)
            last.then_inc(att_scores, 1)

        def dve_max(dve, att, b):
            B = att["B0"] + b
            dve.wait_ge(att_scores, B + 1)
            nm = neg_max[B % 2]
            nc.vector.tensor_reduce(nm[:, 0:2], score_banks(B)[:, :, 0:P], AX.X, ALU.max, negate=True)
            nc.vector.tensor_reduce(nm[:, 2:4], score_banks(B)[:, :, P:3 * P], AX.X, ALU.max, negate=True)\
                .then_inc(att_max, 1)

        def act_exp(act, att, b):
            B = att["B0"] + b
            act.wait_ge(att_max, B + 1)
            if B >= 2:
                act.wait_ge(att_pt, 2 * (B - 1))
                act.wait_ge(att_out, B - 1)
            for t in range(NT):
                cols = slice(0, P) if t == 0 else slice(P, 3 * P)
                for hh in range(2):
                    j = 2 * t + hh
                    nc.scalar.activation(p_buf[:, B % 2, hh, cols], score_banks(B)[:, hh, cols], ACT.Exp,
                                         bias=neg_max[B % 2][:, j:j + 1],
                                         accum_out=row_sum[B % 2][:, j:j + 1]).then_inc(att_exp, 1)

        def pe_pt(pe, att, b):
            B = att["B0"] + b
            pe.wait_ge(att_exp, 4 * (B + 1))
            for hh in range(2):
                if B >= 1:
                    pe.wait_ge(att_pt_dve if hh else att_pt_act, B)
                for i in range(3):
                    last = nc.tensor.transpose(ps[:, 4 + hh, i * P:(i + 1) * P],
                                               p_buf[:, B % 2, hh, i * P:(i + 1) * P], ident)
                last.then_inc(att_pt, 1)

        def evac_pt(eng, att, b, hh):
            B = att["B0"] + b
            eng.wait_ge(att_pt, 2 * B + 1 + hh)
            if B >= 2:
                eng.wait_ge(att_pv, B - 1)
            src, dst = ps[:, 4 + hh, 0:3 * P], pt_buf[:, B % 2, hh, :]
            if hh == 0:
                nc.scalar.activation(dst, src, ACT.Copy).then_inc(att_pt_act, 1)
            else:
                nc.vector.tensor_copy(dst, src).then_inc(att_pt_dve, 1)

        att_psum = ps[:, O_BANK, :].rearrange("p (t h d) -> p t h d", t=NT, h=2)

        def att_own(lo0, lo1):
            v = ps[:, O_BANK, :].rearrange("p (t x d) -> p t x d", t=NT, d=HD)
            return v[:, :, lo0 // HD:3 + lo1 // HD:2 + (lo1 - lo0) // HD, :]

        def pe_pv(pe, att, b):
            B = att["B0"] + b
            pe.wait_ge(att_pt_act, B + 1)
            pe.wait_ge(att_pt_dve, B + 1)
            if B >= 1:
                pe.wait_ge(att_out, B)
            for hh in range(2):
                pt = pt_buf[:, B % 2, hh, :]
                dst = att_psum
                nc.tensor.matmul(dst[:, 0, hh, :], pt[:, 0:P], att["v"](b, hh, 0), start=True, stop=True)
                nc.tensor.matmul(dst[:, 1, hh, :], pt[:, P:2 * P], att["v"](b, hh, 0), start=True, stop=False)
                last = nc.tensor.matmul(dst[:, 1, hh, :], pt[:, 2 * P:3 * P], att["v"](b, hh, 1), start=False,
                                        stop=True)
            last.then_inc(att_pv, 1)

        def dve_norm(dve, chain, att, b):
            B = att["B0"] + b
            dve.wait_ge(att_pv, B + 1)
            chain(nc.vector.reciprocal(row_inv, row_sum[B % 2]))
            chain.wait()
            att["finish"](dve, chain, b)

        def pe_attention(pe, att, fill=None):
            pe_scores(pe, att, 0)
            pe_scores(pe, att, 1)
            for b in range(att["n"]):
                if fill:
                    fill(b, 0)
                pe_pt(pe, att, b)
                if b + 2 < att["n"]:
                    pe_scores(pe, att, b + 2)
                if fill:
                    fill(b, 1)
                pe_pv(pe, att, b)

        def act_attention(act, att, fill=None):
            act_exp(act, att, 0)
            for b in range(att["n"]):
                if b + 1 < att["n"]:
                    act_exp(act, att, b + 1)
                evac_pt(act, att, b, 0)
                if fill:
                    fill(b)

        def dve_attention(dve, chain, att, fill=None):
            dve_max(dve, att, 0)
            for b in range(att["n"]):
                if b + 1 < att["n"]:
                    dve_max(dve, att, b + 1)
                evac_pt(dve, att, b, 1)
                if fill:
                    fill(b)
                dve_norm(dve, chain, att, b)

        def inv_bc(dv):
            return row_inv.rearrange("p (t h) -> p t h", t=NT).unsqueeze(3).broadcast_to([P, NT, 2, dv])

        def rope(dve, chain, view, n, half, cos, sin, scratch, ready):
            shape = [P, NT, n, half]
            c = cos.rearrange("p (t i) -> p t i", t=NT).unsqueeze(2).broadcast_to(shape)
            s = sin.rearrange("p (t i) -> p t i", t=NT).unsqueeze(2).broadcast_to(shape)
            x1, x2 = view[:, :, :, 0:half], view[:, :, :, half:2 * half]
            size = NT * n * half
            a, b, e, f = (scratch[:, i * size:(i + 1) * size].rearrange("p (t h i) -> p t h i", t=NT, h=n)
                          for i in range(4))
            chain(nc.vector.tensor_tensor(a, x1, c, ALU.mult))
            chain(nc.vector.tensor_tensor(b, x2, s, ALU.mult))
            chain(nc.vector.tensor_tensor(e, x2, c, ALU.mult))
            chain(nc.vector.tensor_tensor(f, x1, s, ALU.mult))
            chain.wait()
            nc.vector.tensor_tensor(x1, a, b, ALU.subtract)
            nc.vector.tensor_tensor(x2, e, f, ALU.add).then_inc(ready, 1)

        FH, DH, DV = 8, 4, 128
        GATE0, DIFF0 = 3 * FH * HD, 3 * FH * HD + FH
        cols1 = [(0, 256), (256, 256), (GATE0, FH)] + [(i * 256, 256) for i in range(2, 6)] + [(DIFF0 + i * 256, 256) for i in range(6)]
        LAM_INIT = 0.8 - 0.6 * float(np.exp(-0.3 * 0))
        AUG = HD + 2
        q_aug = tmp[:, 0:NT * FH * AUG].rearrange("p (t h d) -> p t h d", t=NT, h=FH)
        k_aug = tmp[:, NT * FH * AUG:2 * NT * FH * AUG].rearrange("p (t h d) -> p t h d", t=NT, h=FH)

        def tiny(at, shape):
            n = 1
            for w in shape:
                n *= w
            v = small[:, at:at + n]
            return v if len(shape) == 1 else v.rearrange("p (a b) -> p a b", a=shape[0])

        gate_z, gate_e = tiny(20, [NT, FH]), tiny(36, [NT, FH])
        log_f, forget_b = tiny(52, [NT, FH]), tiny(68, [FH])
        lam_in, lam_prod = tiny(76, [4, HD]), tiny(332, [2, HD])
        lam_sum, neg_lam = tiny(460, [2]), tiny(462, [1])
        sub_gain, diff_ss = tiny(463, [DV]), tiny(591, [NT, DH])
        diff_nat = o_all[:, :, FH * HD:D]
        c_psum = ps[:, FILL_BANK, 0:NT * FH].rearrange("p (t h) -> p t h", t=NT)

        def fox_finish(dve, chain, b):
            dst = o_all[:, :, 2 * b * HD:2 * (b + 1) * HD].rearrange("p t (h d) -> p t h d", h=2)
            nc.vector.tensor_tensor(dst, att_own(0, HD), inv_bc(HD), ALU.mult).then_inc(att_out, 1)

        def diff_finish(dve, chain, b):
            both = tmp[:, 1024:1536].rearrange("p (t h d) -> p t h d", t=NT, h=2)
            nc.vector.tensor_tensor(both, att_psum, inv_bc(DV), ALU.mult).then_inc(att_out, 1)
            dve.wait_ge(att_out, fox["n"] + b + 1)
            chain(nc.vector.scalar_tensor_tensor(diff_nat[:, :, b * DV:(b + 1) * DV], both[:, :, 1, :], neg_lam,
                                                 both[:, :, 0, :], ALU.mult, ALU.add))
            chain.wait()

        fox = {"B0": 0, "n": FH // 2, "finish": fox_finish,
               "q": lambda b, hh: qk_t[0:AUG, 2 * b + hh, :], "k": lambda b, hh: qk_t[0:AUG, 8 + 2 * b + hh, :],
               "v": lambda b, hh, kt: proj[:, kt, 1024 + 2 * b * HD:1024 + 2 * (b + 1) * HD]}
        diff = {"B0": FH // 2, "n": DH, "finish": diff_finish,
                "q": lambda b, hh: qk_t[0:HD, 2 * b + hh, :], "k": lambda b, hh: qk_t[0:HD, 8 + 2 * b + hh, :],
                "v": lambda b, hh, kt: proj[:, kt, DIFF0 + 1024 + b * DV:DIFF0 + 1024 + (b + 1) * DV]}
        diff_qk = proj[:, :, DIFF0:DIFF0 + 1024].rearrange("p t (h d) -> p t h d", d=HD)
        fox_items, diff_items = [], []
        for _b in range(4):
            for _k, _aug in ((0, q_aug), (1, k_aug)):
                fox_items.append(([[_aug[:, t, h, :] for t in range(NT)] for h in (2 * _b, 2 * _b + 1)],
                                  qk_t[0:AUG, 8 * _k + 2 * _b:8 * _k + 2 * _b + 2, :], 1.0))
                diff_items.append(([[diff_qk[:, t, 8 * _k + h, :] for t in range(NT)]
                                    for h in (2 * _b, 2 * _b + 1)],
                                   qk_t[0:HD, 8 * _k + 2 * _b:8 * _k + 2 * _b + 2, :], 1.0))

        def evac1(act, u0, i, bank):
            if i == 2:
                dst, scale = gate_z, 1.0
            elif i < 2:
                dst, scale = q_aug[:, :, 4 * i:4 * (i + 1), 0:HD], SCALE
            elif i <= 4:
                dst, scale = k_aug[:, :, 4 * (i - 3):4 * (i - 2), 0:HD], 1.0
            else:
                c0 = cols1[i][0]
                dst, scale = proj[:, :, c0:c0 + 256], SCALE if i in (7, 8) else 1.0
            act_evac(act, u0 + i, dst, cols1[i][1], bank, scale)

        def sp_mix1(sp, ph):
            w_in, w_out = A["w_in"][0], A["w_out"][0]
            for i, (c0, w) in enumerate(cols1):
                sp_cols(sp, ph["u0"] + i, w_in, c0, w)
            for i in range(4):
                sp_rows(sp, ph["u0"] + 13 + i, w_out, i)

        def pool_mix1(pool, chain, ph):
            pool.dma_start(forget_b, A["fox_forget_b"][0].partition_broadcast(P)).then_inc(sem("mix1_loaded"), 16)
            for i, nm in enumerate(("q1", "q2", "k1", "k2")):
                pool.dma_start(lam_in[:, i, :], A["diff_lambda_" + nm][0].partition_broadcast(P))\
                    .then_inc(sem("mix1_loaded"), 16)
            pool.dma_start(sub_gain, A["diff_subln_g"][0].partition_broadcast(P)).then_inc(sem("mix1_loaded"), 16)
            pool.wait_ge(aT_ready, 4 * (ph["t0"] + 1))
            nc.gpsimd.memset(q_aug[:, :, :, HD + 1:HD + 2], 1.0).then_inc(sem("aug_ones"), 1)
            nc.gpsimd.memset(k_aug[:, :, :, HD:HD + 1], 1.0).then_inc(sem("aug_ones"), 1)
            pool.wait_ge(sem("diff_ss_ready"), 1)
            chain(nc.gpsimd.tensor_scalar(diff_ss, diff_ss, 1.0 / DV, EPS, ALU.mult, ALU.add))
            chain.wait()
            nc.gpsimd.tensor_tensor(diff_ss, diff_ss, minus_half.unsqueeze(2).broadcast_to([P, NT, DH]), ALU.pow)\
                .then_inc(sem("diff_rstd_ready"), 1)

        def pe_mix1(pe, ph):
            st, u0 = {"item": 0}, ph["u0"]
            pe_begin(pe, ph["t0"], xn, lambda i, t: pe_cols(pe, u0 + i, 256, i, 0, (t,)),
                     transposed=issued(ph))
            for i in range(2, 7):
                pe_cols(pe, u0 + i, cols1[i][1], i % 4, i - 3)
            pe_cols(pe, u0 + 7, 256, FILL_BANK, 0)
            pe.wait_ge(sem("logf_ready"), 1)
            pe.wait_ge(proj_evac, 8)
            nc.tensor.matmul(c_psum[:, 0, :], const("cumsum"), log_f[:, 0, :], start=True, stop=True)
            nc.tensor.matmul(c_psum[:, 1, :], const("cumsum"), log_f[:, 1, :], start=True, stop=False)
            nc.tensor.matmul(c_psum[:, 1, :], const("ones"), log_f[:, 0, :], start=False, stop=True)\
                .then_inc(sem("decay_ready"), 1)
            pe.wait_ge(sem("aug_ready"), 2)
            pe.wait_ge(sem("aug_ones"), 2)
            pe_items(pe, st, fox_items)
            pe_cols(pe, u0 + 8, 256, FILL_BANK, 0)
            pe_items_left(pe, st)
            pe_attention(pe, fox, lambda b, t: pe_cols(pe, u0 + 9 + b, 256, FILL_BANK, 9 + b, (t,)))
            pe.wait_ge(proj_evac, 13)
            pe.wait_ge(sem("diff_rope_ready"), 1)
            pe.wait_ge(att_exp, 4 * fox["n"])
            pe_items(pe, st, diff_items)
            pe_items_left(pe, st)
            pe_attention(pe, diff)
            pe_out(pe, ph, ph["t0"] + 1, o_all)

        def act_mix1(act, chain, ph):
            st, u0 = {"item": 0}, ph["u0"]

            def ahead(i):
                split_hi(act, u0 + i + 2, width=width_of(u0 + i + 2))
            for i in range(7):
                ahead(i)
                evac1(act, u0, i, i % 4)
                if i == 3:
                    act.wait_ge(sem("gate_abs_ready"), 1)
                    chain(nc.scalar.activation(gate_e, gate_e, ACT.Exp))
                    chain.wait()
                    nc.scalar.activation(gate_e, gate_e, ACT.Ln, bias=1.0).then_inc(sem("gate_ln_ready"), 1)
            ahead(7)
            evac1(act, u0, 7, FILL_BANK)
            ahead(8)
            evac_items(act, st, fox_items, 0)
            evac1(act, u0, 8, FILL_BANK)
            act.wait_ge(sem("lam_sum_ready"), 1)
            nc.scalar.activation(lam_sum, lam_sum, ACT.Exp).then_inc(sem("lam_exp_ready"), 1)

            def fill(b):
                ahead(9 + b)
                evac1(act, u0, 9 + b, FILL_BANK)
            act_attention(act, fox, fill)
            ahead(13)
            evac_items(act, st, diff_items, 0)
            act_attention(act, diff)
            act_transposed(act, ph["t0"] + 1, 0)
            act_transposed(act, ph["t0"] + 1, 1)
            ahead(14)
            ahead(15)

        def dve_mix1(dve, chain, ph):
            st, u0 = {"item": 0}, ph["u0"]

            def ahead(i):
                split_lo(dve, u0 + i + 2, width=width_of(u0 + i + 2))
            ahead(0)
            ahead(1)
            ahead(2)
            dve.wait_ge(sem("mix1_loaded"), 16 * 6)
            dve.wait_ge(proj_evac, 3)
            chain(nc.vector.tensor_tensor(gate_z, gate_z, forget_b.unsqueeze(1).broadcast_to([P, NT, FH]), ALU.add))
            chain.wait()
            nc.vector.scalar_tensor_tensor(gate_e, gate_z, -1.0, gate_z, ALU.mult, ALU.min)\
                .then_inc(sem("gate_abs_ready"), 1)
            ahead(3)
            dve.wait_ge(sem("gate_ln_ready"), 1)
            nc.vector.scalar_tensor_tensor(log_f, gate_z, 0.0, gate_e, ALU.min, ALU.subtract)\
                .then_inc(sem("logf_ready"), 1)
            chain(nc.vector.tensor_tensor(lam_prod, lam_in[:, 0:2, :], lam_in[:, 2:4, :], ALU.mult))
            chain(nc.vector.tensor_scalar(sub_gain, sub_gain, 1.0 - LAM_INIT, None, ALU.mult))
            chain.wait()
            nc.vector.tensor_reduce(lam_sum, lam_prod, AX.X, ALU.add).then_inc(sem("lam_sum_ready"), 1)
            for i in range(4, 9):
                ahead(i)
            dve.wait_ge(sem("decay_ready"), 1)
            nc.vector.tensor_copy(q_aug[:, :, :, HD:HD + 1], c_psum.unsqueeze(3)).then_inc(sem("aug_ready"), 1)
            nc.vector.tensor_scalar(k_aug[:, :, :, HD + 1:HD + 2], c_psum.unsqueeze(3), -1.0, None, ALU.mult)\
                .then_inc(sem("aug_ready"), 1)
            evac_items(dve, st, fox_items, 1)
            dve.wait_ge(sem("lam_exp_ready"), 1)
            chain(nc.vector.tensor_tensor(neg_lam, lam_sum[:, 1:2], lam_sum[:, 0:1], ALU.subtract))
            chain.wait()
            chain(nc.vector.tensor_scalar(neg_lam, neg_lam, -LAM_INIT, None, ALU.add))
            chain.wait()
            dve_attention(dve, chain, fox, lambda b: ahead(9 + b))
            ahead(13)
            dve.wait_ge(proj_evac, 13)
            rope(dve, chain, diff_qk, 16, 8, const("cos16"), const("sin16"), tmp, sem("diff_rope_ready"))
            evac_items(dve, st, diff_items, 1)
            dve_attention(dve, chain, diff)
            square = tmp[:, 0:1024].rearrange("p (t h d) -> p t h d", t=NT, h=DH)
            heads = diff_nat.rearrange("p t (h d) -> p t h d", h=DH)
            chain(nc.vector.tensor_tensor(square, heads, heads, ALU.mult))
            chain.wait()
            nc.vector.tensor_reduce(diff_ss, square, AX.X, ALU.add).then_inc(sem("diff_ss_ready"), 1)
            dve.wait_ge(sem("diff_rstd_ready"), 1)
            for t in range(NT):
                chain(nc.vector.tensor_tensor(heads[:, t], heads[:, t],
                                              diff_ss[:, t, :].unsqueeze(2).broadcast_to([P, DH, DV]), ALU.mult))
                chain.wait()
                nc.vector.tensor_tensor(heads[:, t], heads[:, t],
                                        sub_gain.unsqueeze(1).broadcast_to([P, DH, DV]), ALU.mult)\
                    .then_inc(xn_ready, 1)
            dve_transposed(dve, ph["t0"] + 1, 0)
            dve_transposed(dve, ph["t0"] + 1, 1)
            ahead(14)
            ahead(15)

        DIN = 2752
        cols2 = [(i * 256, 256) for i in range(10)] + [(DIN - 256, 256)]
        N_IN, N_GATE = len(cols2), 3 * D // 256
        SBH, NH, NG, DSH, IXH, IXD = 4, 8, 2, 4, 8, 32
        NQ, NKC, NKS, NVS, NKW, NVW, GATES, DQ, DV0, IQ, IW = (768, 1280, 1536, 1664, 1792, 1920, 2048, 2072,
                                                               2392, 2456, 2744)
        NB = S // 16 - 1
        TOPK = min(256, S // 4)
        NQK = NH + 2 * NG + DSH + 1
        qk_nat = tmp[:, 0:NT * NQK * HD].rearrange("p (t h d) -> p t h d", t=NT, h=NQK)
        qk_groups = [(0, NH, NQ, 0), (NH, NG, NKS, 1), (NH + NG, NG, NKW, 2), (NH + 2 * NG, DSH, DQ, 3),
                     (NH + 2 * NG + DSH, 1, DQ + DSH * HD, 4)]
        qk_load = [qk_groups[0], qk_groups[1], qk_groups[2], (NH + 2 * NG, DSH + 1, DQ, 3)]
        head_gain = proj[:, 0, DIN:DIN + 5 * HD].rearrange("p (g d) -> p g d", g=5)
        cmp_gain = proj[:, 1, DIN:DIN + HD]
        cmp_w2 = proj[:, 1, DIN + HD:DIN + 3 * HD].rearrange("p (a d) -> p a d", a=2)
        cmp_pe = proj[:, 1, DIN + 3 * HD:DIN + 3 * HD + 32].rearrange("p (a j) -> p a j", a=2)
        cmp_w1 = qk_t[:, 0:16, :].rearrange("p a b -> p (a b)").rearrange("p (a j n) -> p a j n", a=2, j=16)
        pb = p_buf[:, :, :, :].rearrange("p a b c -> p (a b c)")
        ptb = pt_buf[:, :, :, :].rearrange("p a b c -> p (a b c)")
        cmp_in = pb[:, 0:960].rearrange("p (a j c) -> p a j c", a=2, j=16)
        sb_t = o_all[:, :, :].rearrange("p t d -> p (t d)").rearrange("p (h s) -> p h s", h=8)
        cmp_hid, cmp_sig = tiny(20, [2, 2 * NB]), tiny(80, [2, 2 * NB])
        vc_in = small[:, 140:140 + NH * NB]
        kc = small[0:2 * NB, 260:324]
        kc_sq = small[0:2 * NB, 324:388]
        kc_ss = small[0:2 * NB, 388:389]
        kc_t = small[0:HD, 390:390 + 2 * NB]
        kc_rot = small[0:2 * NB, 420:452]
        nsa_gate = tiny(452, [NT, 3 * NH])
        gates = nsa_gate.rearrange("p t (h c) -> p t h c", c=3)
        qk_ss = tiny(500, [NT, NQK])
        cmp_max, cmp_den, cmp_zero = tiny(534, [NT, NH]), tiny(550, [NT, NH]), tiny(566, [NT, NH])
        row_gate = small[:, 582:586]
        top8 = [small[:, 586 + 8 * i:594 + 8 * i] for i in range(2)]
        ix_w = tiny(602, [NT, IXH])
        v_diag = ptb[0:NH * NB, 0:512].rearrange("p (h d) -> p h d", h=NH)
        cmp_s = pb[:, 0:NT * NH * NB].rearrange("p (t h c) -> p t h c", t=NT, h=NH)
        cmp_p_t = pb[0:NH * NB, 240:240 + S]
        ix_relu = [pb[:, 500:884], ptb[:, 512:896]]
        ix_score, ix_val = gate_or_gain[:, 0, 2560:2944], gate_or_gain[:, 1, 2560:2944]
        sel_mask = sb_mask
        CMP_BANK = 4

        def ev(name, ph):
            return sem(name), ph["mix2_before"] + 1

        def wait(eng, name, ph, times=1):
            s_, v_ = ev(name, ph)
            eng.wait_ge(s_, v_ * times)

        def nsa_finish(ph, dve, chain, b):
            pair, branch = b % 4, b // 4 + 1
            g = pair // 2
            chain(nc.vector.tensor_tensor(row_gate.rearrange("p (t h) -> p t h", t=NT),
                                          row_inv.rearrange("p (t h) -> p t h", t=NT),
                                          gates[:, :, 2 * pair:2 * pair + 2, branch], ALU.mult))
            chain.wait()
            part = tmp[:, 0:256].rearrange("p (t h d) -> p t h d", t=NT, h=2)
            nc.vector.tensor_tensor(part, att_own(g * HD, g * HD), row_gate.rearrange("p (t h) -> p t h", t=NT)
                                    .unsqueeze(3).broadcast_to([P, NT, 2, HD]), ALU.mult).then_inc(att_out, 1)
            dve.wait_ge(att_out, ph["B0"] + b + 1)
            dst = o_all[:, :, 256 + 2 * pair * HD:256 + 2 * (pair + 1) * HD]\
                .rearrange("p t (h d) -> p t h d", h=2)
            chain(nc.vector.tensor_tensor(dst, dst, part, ALU.add))
            chain.wait()

        def dsa_finish(dve, chain, b):
            dst = o_all[:, :, 768 + 2 * b * HD:768 + 2 * (b + 1) * HD].rearrange("p t (h d) -> p t h d", h=2)
            nc.vector.tensor_tensor(dst, att_own(HD, HD), inv_bc(HD), ALU.mult).then_inc(att_out, 1)

        def attentions(ph):
            def finish(dve, chain, b):
                if b < 8:
                    nsa_finish(ph, dve, chain, b)
                else:
                    dsa_finish(dve, chain, b - 8)
            return {"B0": ph["B0"], "n": 10, "finish": finish,
                    "masked_from": 8, "mask": sel_mask, "mask_ready": ev("mask_ready", ph),
                    "q": lambda b, hh: qk_t[0:HD, 2 * (b % 4) + hh + (0 if b < 8 else NH + 2 * NG), :],
                    "k": lambda b, hh: qk_t[0:HD, NH + NG * (b // 4) + b % 4 // 2 if b < 8 else NQK - 1, :],
                    "v": lambda b, hh, kt: (proj[:, kt, (NVS, NVW)[b // 4]:(NVS, NVW)[b // 4] + NG * HD] if b < 8
                                            else proj[:, kt, DV0 - HD:DV0 + HD])}

        mix2_halves = [(1, 1), (1, 1), (0, 1), (1, 1), (0, 1), (0, 1), (0, 1), (0, 1), (0, 1), (0, 0)]
        mix2_fills = {}
        for _b, _pair in enumerate(mix2_halves):
            _n = sum(map(sum, mix2_halves[:_b + 1]))
            if _n // 2 > sum(map(sum, mix2_halves[:_b])) // 2:
                mix2_fills[_b] = 6 + _n // 2 - 1

        def mix2_beside(fill, b, place):
            if mix2_halves[b][place]:
                n = sum(map(sum, mix2_halves[:b])) + (mix2_halves[b][0] if place else 0)
                fill(6 + n // 2, (n % 2,))

        def nat(src, c0, w):
            return [src[:, t, c0:c0 + w] for t in range(NT)]

        sb_items, qk_items, ix_items = [], [], []
        for _i in range(2):
            for _k in range(2):
                sb_items.append(([nat(proj, 256 * _k + (2 * _i + j) * HD, HD) for j in range(2)],
                                 sb_t[0:HD, 4 * _k + 2 * _i:4 * _k + 2 * _i + 2, :], 1.0))
        for _i in range(0, NQK, 2):
            _n = min(2, NQK - _i)
            is_q = _i < NH or NH + 2 * NG <= _i < NQK - 1
            qk_items.append(([[qk_nat[:, t, _i + j, :] for t in range(NT)] for j in range(_n)],
                             qk_t[0:HD, _i:_i + _n, :], SCALE if is_q else 1.0))
        ix_t = tmp[0:IXD, 0:(IXH + 1) * S].rearrange("p (h s) -> p h s", h=IXH + 1)
        for _i in range(0, IXH + 1, 2):
            _n = min(2, IXH + 1 - _i)
            ix_items.append(([nat(proj, IQ + (_i + j) * IXD, IXD) for j in range(_n)],
                             ix_t[:, _i:_i + _n, :], 1.0))

        def sb_bank(h):
            return ps[:, h, 0:3 * P]

        def sb_view(buf, half):
            return buf[:, half * 768:(half + 1) * 768].rearrange("p (h c) -> p h c", h=2)

        def sb_diag(buf, half):
            v = sb_view(buf, half).rearrange("p h (b c) -> p h b c", b=3)
            return [v[:, h, 0:3:2, :] for h in range(2)]

        def pe_sb_z(pe, h, start, stop):
            q, k, dst = sb_t[0:HD, h, :], sb_t[0:HD, 4 + h, :], sb_bank(h)
            nc.tensor.matmul(dst[:, 0:S], k[:, 0:P], q, start=start, stop=stop)
            return dst, q, k

        def pe_sb_scores(pe, half, ph):
            for h in (2 * half, 2 * half + 1):
                dst, q, k = pe_sb_z(pe, h, True, True)
                last = nc.tensor.matmul(dst[:, S:3 * P], k[:, P:S], q[:, P:S], start=True, stop=True)
            last.then_inc(ev("sb_z_ready", ph)[0], 1)

        def pe_sb_logw(pe, half, ph):
            sp_ = sb_view(ptb, half)
            for h in (2 * half, 2 * half + 1):
                dst, q, k = pe_sb_z(pe, h, True, False)
                own = sp_[:, h % 2, :]
                nc.tensor.matmul(dst[:, 0:S], const("tail_neg"), own[:, 0:S], start=False, stop=False)
                nc.tensor.matmul(dst[:, P:S], const("ones_neg"), own[:, S:3 * P], start=False, stop=False)
                nc.tensor.matmul(dst[:, 0:P], ident_bf, notpast_bf, start=False, stop=True)
                nc.tensor.matmul(dst[:, S:3 * P], k[:, P:S], q[:, P:S], start=True, stop=False)
                nc.tensor.matmul(dst[:, S:3 * P], const("tail_neg"), own[:, S:3 * P], start=False, stop=False)
                last = nc.tensor.matmul(dst[:, S:3 * P], ident_bf, notpast_bf, start=False, stop=True)
            last.then_inc(ev("sb_logw_ready", ph)[0], 1)

        def sp_mix2(sp, ph):
            l, u0 = ph["l"], ph["u0"]
            for i, (c0, w) in enumerate(cols2):
                sp_cols(sp, u0 + i, A["w_in_2"][l], c0, w)
            for i in range(N_GATE):
                sp_cols(sp, u0 + N_IN + i, A["w_gate_2"][l], i * 256, 256)
            sp_rows(sp, u0 + 23, A["w_br_a_2"][l], 0)
            sp_rows(sp, u0 + 24, A["w_br_b_2"][l], 0)
            sp_rows(sp, u0 + 25, A["w_br_b_2"][l], 1)
            sp_rows(sp, u0 + 26, A["w_br_c_2"][l], 0)
            for i in range(4):
                sp_rows(sp, u0 + 27 + i, A["w_out_2"][l], i)

        def pool_mix2(pool, chain, ph):
            l = ph["l"]
            loaded = ev("mix2_loaded", ph)[0]
            pool.wait_ge(tp_done, 4 * (ph["t0"] + 1))
            for a in range(2):
                pool.dma_start(cmp_w1[:, a], A["nsa_cmp_w1_2"][l, a].rearrange("(j p) n -> p j n", p=P))\
                    .then_inc(loaded, 16)
                pool.dma_start(cmp_w2[:, a, :], A["nsa_cmp_w2_2"][l, a]).then_inc(loaded, 16)
                pool.dma_start(cmp_pe[:, a, :], A["cmp_pe"][l, a]).then_inc(loaded, 16)
            for i, src in enumerate((A["nsa_q_norm_2"][l], A["nsa_k_norm_2"][l, 1], A["nsa_k_norm_2"][l, 2],
                                     A["dsa_q_norm_2"][l], A["dsa_k_norm_2"][l])):
                pool.dma_start(head_gain[:, i, :], src.partition_broadcast(P)).then_inc(loaded, 16)
            pool.dma_start(cmp_gain, A["nsa_k_norm_2"][l, 0].partition_broadcast(P)).then_inc(loaded, 16)
            wait(pool, "qk_ss_ready", ph)
            chain(nc.gpsimd.tensor_scalar(qk_ss, qk_ss, 1.0 / HD, EPS, ALU.mult, ALU.add))
            chain.wait()
            nc.gpsimd.tensor_tensor(qk_ss, qk_ss, minus_half.unsqueeze(2).broadcast_to([P, NT, NQK]), ALU.pow)\
                .then_inc(ev("qk_rstd_ready", ph)[0], 1)
            wait(pool, "kc_ss_ready", ph)
            chain(nc.gpsimd.tensor_scalar(kc_ss, kc_ss, 1.0 / HD, EPS, ALU.mult, ALU.add))
            chain.wait()
            nc.gpsimd.tensor_tensor(kc_ss, kc_ss, minus_half[0:2 * NB], ALU.pow)\
                .then_inc(ev("kc_rstd_ready", ph)[0], 1)
            for t in range(NT):
                pool.wait_ge(sem("gated_b"), 2 * (ev("", ph)[1] - 1) + t + 1)
                nc.gpsimd.tensor_tensor(xn[:, t, :], gate_or_gain[:, t, 0:D], gate_or_gain[:, t, D:2 * D], ALU.add)\
                    .then_inc(ev("merged_ab", ph)[0], 1)

        def pe_mix2(pe, ph):
            st, u0 = {"item": ph["item0"]}, ph["u0"]
            pj0 = ph["proj0"]

            def fill(k, tiles=(0, 1), between=None):
                pe_cols(pe, u0 + N_IN + k, 256, FILL_BANK, pj0 + N_IN + k, tiles, between)
            pe_begin(pe, ph["t0"], xn, lambda i, t: pe_cols(pe, u0 + i, 256, i, 0, (t,)),
                     transposed=issued(ph))
            for i in range(2, N_IN):
                pe_cols(pe, u0 + i, cols2[i][1], i % 4, pj0 + i - 3 if i > 3 else 0)
            pe.wait_ge(proj_evac, pj0 + N_IN)
            pe_items(pe, st, sb_items)
            for a in range(2):
                for g in range(NG):
                    for t in range(NT):
                        for par in range(2):
                            c = (a * NG + g) * P + t * HD
                            last = nc.tensor.matmul(ps[par * HD:(par + 1) * HD, O_BANK, c:c + HD],
                                                    proj[:, t, NKC + (a * NG + g) * HD:NKC + (a * NG + g + 1) * HD],
                                                    ident[:, par::2], start=True, stop=True)
            last.then_inc(ev("pairs_ready", ph)[0], 1)
            fill(0, tiles=(0,))
            wait(pe, "cmp_in_ready", ph)

            def hidden(k):
                for i in range(4 * k, 4 * k + 4):
                    a, j = i // 16, i % 16
                    mm = nc.tensor.matmul(ps[:, CMP_BANK, a * 2 * NB:(a + 1) * 2 * NB], cmp_w1[:, a, j, :],
                                          cmp_in[:, a, j, :], start=j == 0, stop=j == 15)
                if k == KC - 1:
                    mm.then_inc(ev("hidden_ready", ph)[0], 1)
            fill(0, tiles=(1,), between=hidden)
            pe_items_left(pe, st)
            pe_sb_scores(pe, 0, ph)
            pe_sb_scores(pe, 1, ph)
            fill(1)
            for half in range(2):
                pe.wait_ge(ev("sb_sp_ready", ph)[0], 2 * (ev("", ph)[1] - 1) + half + 1)
                pe_sb_logw(pe, half, ph)
            fill(2)
            for half in range(2):
                pe.wait_ge(ev("sb_w_ready", ph)[0], 2 * (ev("", ph)[1] - 1) + half + 1)
            o_sb = ps[:, O_BANK, :].rearrange("p (t h d) -> p t h d", t=NT, h=SBH)
            for h in range(SBH):
                w = sb_view(pb, h // 2)[:, h % 2, :]
                v = [proj[:, t, 512 + h * HD:512 + (h + 1) * HD] for t in range(NT)]
                nc.tensor.matmul(o_sb[:, 0, h, :], w[:, 0:P], v[0], start=True, stop=True)
                nc.tensor.matmul(o_sb[:, 1, h, :], w[:, P:S], v[0], start=True, stop=False)
                last = nc.tensor.matmul(o_sb[:, 1, h, :], w[:, S:3 * P], v[1], start=False, stop=True)
            last.then_inc(ev("sb_out_ready", ph)[0], 1)
            wait(pe, "hid_ready", ph)
            nc.tensor.matmul(ps[0:2 * NB, CMP_BANK, 128:128 + HD], cmp_hid[:, 0, :], cmp_w2[:, 0, :],
                             start=True, stop=True)
            nc.tensor.matmul(ps[0:NH * NB, CMP_BANK + 1, 0:HD], vc_in, cmp_w2[:, 1, :], start=True, stop=True)\
                .then_inc(ev("kcvc_ready", ph)[0], 1)
            fill(3)
            wait(pe, "qk_ready", ph)
            pe_items(pe, st, qk_items)
            wait(pe, "kc_ready", ph)
            nc.tensor.transpose(ps[0:HD, CMP_BANK, 256:256 + 2 * NB], kc, ident[0:2 * NB, 0:2 * NB])\
                .then_inc(ev("kcT_psum", ph)[0], 1)
            pe_items_left(pe, st)
            wait(pe, "kcT_ready", ph)
            for t in range(NT):
                for h in range(NH):
                    g = h // (NH // NG)
                    c = (t * NH + h) * NB
                    last = nc.tensor.matmul(ps[:, CMP_BANK, c:c + NB], qk_t[0:HD, h, t * P:(t + 1) * P],
                                            kc_t[:, g * NB:(g + 1) * NB], start=True, stop=True)
            last.then_inc(ev("cmp_scores", ph)[0], 1)
            fill(4)
            wait(pe, "ix_rope_ready", ph)
            pe_items(pe, st, ix_items)
            wait(pe, "cmp_p_ready", ph)
            for t in range(NT):
                last = nc.tensor.transpose(ps[0:NH * NB, CMP_BANK + 1, t * P:(t + 1) * P],
                                           cmp_s[:, t].rearrange("p h c -> p (h c)"), ident)
            last.then_inc(ev("cmp_pt", ph)[0], 1)
            wait(pe, "cmp_pt_ready", ph)
            for t in range(NT):
                last = nc.tensor.matmul(ps[:, CMP_BANK + t, :], cmp_p_t[:, t * P:(t + 1) * P],
                                        v_diag.rearrange("p h d -> p (h d)"), start=True, stop=True)
            last.then_inc(ev("cmp_out_ready", ph)[0], 1)
            fill(5)
            pe_items_left(pe, st)
            r0 = IXH * (ev("", ph)[1] - 1)
            for h in range(IXH):
                if h >= 4:
                    pe.wait_ge(sem("ix_relu_ready"), r0 + h - 3)
                nc.tensor.matmul(ps[:, h % 4, 0:P], ix_t[:, h, 0:P], ix_t[:, IXH, 0:P], start=True, stop=True)
                nc.tensor.matmul(ps[:, h % 4, P:3 * P], ix_t[:, h, P:S], ix_t[:, IXH, :], start=True, stop=True)\
                    .then_inc(sem("ix_logits"), 1)
            pe.wait_ge(sem("ix_relu_ready"), r0 + IXH)
            pe_attention(pe, attentions(ph), lambda b, place: mix2_beside(fill, b, place))
            li = ev("", ph)[1] - 1
            for t in range(NT):
                pe_transpose(pe, ph["t0"] + 1, o_all, t)
            for t in range(NT):
                pe_wait_aT(pe, ph["t0"] + 1, t)
                mm = pe_rows(pe, u0 + 23, (u0 + 23) % SLOTS, *a_chunks(0), 0, True, True, (t,))
            mm.then_inc(unit_used, 1)
            for t in range(NT):
                for i, (bank, first, last) in enumerate(((4, True, False), (4, False, True), (0, True, True))):
                    n = u0 + 24 + i
                    if i == 2:
                        if t == 1:
                            pe_transpose(pe, ph["t0"] + 2, xn, 0)
                        pe.wait_ge(sem("gated_a"), 2 * li + t + 1)
                    mm = pe_rows(pe, n, n % SLOTS, *a_chunks(1 + i), bank, first, last, (t,))
                    if t == 1:
                        mm.then_inc(unit_used, 1)
                    elif i == 2:
                        mm.then_inc(sem("branches_t0_ready"), 1)
            pe_out(pe, ph, ph["t0"] + 2, xn, transposed=(0,))

        def act_mix2(act, chain, ph):
            st, u0 = {"item": ph["item0"]}, ph["u0"]
            li = ev("", ph)[1] - 1

            def ahead(i):
                split_hi(act, u0 + i + 2, width=width_of(u0 + i + 2))

            def fill(k):
                ahead(N_IN + k)
                if k == 10:
                    wait(act, "mask_ready", ph)
                act_evac(act, u0 + N_IN + k, gate_or_gain[:, :, k * 256:(k + 1) * 256], 256, FILL_BANK)
            for i, (c0, w) in enumerate(cols2):
                ahead(i)
                skip = 256 * i - c0
                act_evac(act, u0 + i, proj[:, :, c0 + skip:c0 + w], w, i % 4, SCALE if i == 0 else 1.0, skip)
            act.wait_ge(proj_evac, ph["proj0"] + N_IN)
            act.wait_ge(aT_ready, 4 * (ph["t0"] + 1))
            for h0, n, c0, _ in qk_load:
                last = nc.scalar.activation(qk_nat[:, :, h0:h0 + n, :].rearrange("p t h d -> p t (h d)"),
                                            proj[:, :, c0:c0 + n * HD], ACT.Square)
            last.then_inc(ev("qk_sq_ready", ph)[0], 1)
            evac_items(act, st, sb_items, 0)
            fill(0)
            wait(act, "gates_clamped", ph)
            nc.scalar.activation(nsa_gate, nsa_gate, ACT.Exp, scale=-1.0).then_inc(ev("gates_exp", ph)[0], 1)
            wait(act, "hid_clamped", ph)
            nc.scalar.activation(cmp_sig, cmp_sig, ACT.Exp, scale=-1.0).then_inc(ev("hid_exp", ph)[0], 1)
            for half in range(2):
                act.wait_ge(sem("sb_z_ready"), 2 * li + half + 1)
                z, buf = ps[:, 2 * half:2 * half + 2, 0:3 * P], sb_view(pb, half)
                chain(nc.scalar.activation(buf, z, ACT.Abs))
                chain.wait()
                chain(nc.scalar.activation(buf, buf, ACT.Exp, scale=-1.0))
                chain.wait()
                nc.scalar.activation(buf, buf, ACT.Ln, bias=1.0).then_inc(sem("sb_ln_ready"), 1)
            fill(1)
            for half in range(2):
                act.wait_ge(sem("sb_logw_ready"), 2 * li + half + 1)
                nc.scalar.activation(sb_view(pb, half), ps[:, 2 * half:2 * half + 2, 0:3 * P], ACT.Exp)\
                    .then_inc(sem("sb_w_ready"), 1)
            fill(2)
            fill(3)
            evac_items(act, st, qk_items, 0)
            wait(act, "kcT_psum", ph)
            nc.scalar.activation(kc_t, ps[0:HD, CMP_BANK, 256:256 + 2 * NB], ACT.Copy)\
                .then_inc(ev("kcT_ready", ph)[0], 1)
            wait(act, "cmp_shifted", ph)
            nc.scalar.activation(cmp_s, cmp_s, ACT.Exp).then_inc(ev("cmp_exp", ph)[0], 1)
            fill(4)
            evac_items(act, st, ix_items, 0)
            wait(act, "cmp_pt", ph)
            nc.scalar.activation(cmp_p_t, ps[0:NH * NB, CMP_BANK + 1, 0:S], ACT.Copy)\
                .then_inc(ev("cmp_pt_ready", ph)[0], 1)
            fill(5)
            for h in range(IXH):
                act.wait_ge(sem("ix_logits"), IXH * li + h + 1)
                if h >= 2:
                    act.wait_ge(sem("ix_added"), IXH * li + h - 1)
                nc.scalar.activation(ix_relu[h % 2], ps[:, h % 4, 0:3 * P], ACT.Relu)\
                    .then_inc(sem("ix_relu_ready"), 1)
            act_attention(act, attentions(ph), lambda b: fill(mix2_fills[b]) if b in mix2_fills else None)
            ahead(23)
            for br in range(3):
                g_ = gate_or_gain[:, :, br * D:(br + 1) * D]
                nc.scalar.activation(g_, g_, ACT.Sigmoid).then_inc(sem("gate_sigmoid"), 1)
                if br == 0:
                    act_transposed(act, ph["t0"] + 1, 0)
                    act_transposed(act, ph["t0"] + 1, 1)
            ahead(24)
            ahead(25)
            act_transposed(act, ph["t0"] + 2, 0)
            ahead(26)
            act_transposed(act, ph["t0"] + 2, 1)
            ahead(27)
            ahead(28)
            ahead(29)

        def dve_mix2(dve, chain, ph):
            st, u0 = {"item": ph["item0"]}, ph["u0"]
            li = ev("", ph)[1] - 1

            def ahead(i):
                split_lo(dve, u0 + i + 2, width=width_of(u0 + i + 2))

            def fill(k):
                ahead(N_IN + k)
            for i in range(N_IN):
                ahead(i)
            dve.wait_ge(proj_evac, ph["proj0"] + N_IN)
            evac_items(dve, st, sb_items, 1)
            dve.wait_ge(sem("mix2_loaded"), 16 * 12 * (li + 1))
            wait(dve, "pairs_ready", ph)
            for a in range(2):
                for g in range(NG):
                    c = (a * NG + g) * P
                    pairs = ps[:, O_BANK, c:c + P].rearrange("p (m j) -> p m j", j=8)
                    for jh in range(2):
                        last = nc.vector.tensor_tensor(
                            cmp_in[:, a, 8 * jh:8 * jh + 8, g * NB:(g + 1) * NB].rearrange("p j c -> p c j"),
                            pairs[:, jh:jh + NB, :],
                            cmp_pe[:, a, 8 * jh:8 * jh + 8].unsqueeze(1).broadcast_to([P, NB, 8]), ALU.add)
            last.then_inc(ev("cmp_in_ready", ph)[0], 1)
            fill(0)
            nc.vector.tensor_scalar(nsa_gate, proj[:, :, GATES:GATES + 3 * NH], -80.0, None, ALU.max)\
                .then_inc(ev("gates_clamped", ph)[0], 1)
            wait(dve, "qk_sq_ready", ph)
            nc.vector.tensor_reduce(qk_ss, qk_nat, AX.X, ALU.add).then_inc(ev("qk_ss_ready", ph)[0], 1)
            wait(dve, "hidden_ready", ph)
            hid = ps[:, CMP_BANK, 0:4 * NB].rearrange("p (a c) -> p a c", a=2)
            nc.vector.tensor_scalar(cmp_sig, hid, -80.0, None, ALU.max).then_inc(ev("hid_clamped", ph)[0], 1)
            wait(dve, "gates_exp", ph)
            chain(nc.vector.tensor_scalar(nsa_gate, nsa_gate, 1.0, None, ALU.add))
            wait(dve, "hid_exp", ph)
            chain(nc.vector.tensor_scalar(cmp_sig, cmp_sig, 1.0, None, ALU.add))
            chain.wait()
            chain(nc.vector.reciprocal(nsa_gate, nsa_gate))
            chain(nc.vector.reciprocal(cmp_sig, cmp_sig))
            chain.wait()
            chain(nc.vector.tensor_tensor(cmp_hid, hid, cmp_sig, ALU.mult))
            chain.wait()
            nc.vector.tensor_copy(vc_in.rearrange("p (g r c) -> p g r c", g=NG, c=NB),
                                  cmp_hid[:, 1, :].rearrange("p (g c) -> p g c", g=NG).unsqueeze(2)
                                  .broadcast_to([P, NG, NH // NG, NB])).then_inc(ev("hid_ready", ph)[0], 1)
            for half in range(2):
                dve.wait_ge(sem("sb_ln_ready"), 2 * li + half + 1)
                out_ = sb_view(ptb, half)
                for h in range(2):
                    chain(nc.vector.scalar_tensor_tensor(out_[:, h], ps[:, 2 * half + h, 0:3 * P], 0.0,
                                                         sb_view(pb, half)[:, h], ALU.max, ALU.add))
                chain.wait()
                for h in range(2):
                    d_ = sb_diag(ptb, half)[h]
                    last = nc.vector.tensor_tensor(d_, d_, const("past").unsqueeze(1).broadcast_to([P, 2, P]),
                                                   ALU.mult)
                last.then_inc(sem("sb_sp_ready"), 1)
            fill(1)
            wait(dve, "qk_rstd_ready", ph)
            for h0, n, c0, _ in qk_load:
                chain(nc.vector.tensor_tensor(qk_nat[:, :, h0:h0 + n, :],
                                              proj[:, :, c0:c0 + n * HD].rearrange("p t (h d) -> p t h d", d=HD),
                                              qk_ss[:, :, h0:h0 + n].unsqueeze(3).broadcast_to([P, NT, n, HD]),
                                              ALU.mult))
            chain.wait()
            for h0, n, _, g in qk_groups:
                v = qk_nat[:, :, h0:h0 + n, :]
                chain(nc.vector.tensor_tensor(v, v, head_gain[:, g, :].unsqueeze(1).unsqueeze(1)
                                              .broadcast_to([P, NT, n, HD]), ALU.mult))
            chain.wait()
            fill(2)
            wait(dve, "sb_out_ready", ph)
            chain(nc.vector.tensor_copy(o_all[:, :, 0:256],
                                        ps[:, O_BANK, :].rearrange("p (t n) -> p t n", t=NT)))
            rope(dve, chain, qk_nat, NQK, 8, const("cos16"), const("sin16"), pb, ev("qk_ready", ph)[0])
            wait(dve, "qk_ready", ph)
            wait(dve, "kcvc_ready", ph)
            chain(nc.vector.tensor_copy(kc, ps[0:2 * NB, CMP_BANK, 128:128 + HD]))
            chain(nc.vector.tensor_tensor(v_diag, ps[0:NH * NB, CMP_BANK + 1, 0:HD].unsqueeze(1)
                                          .broadcast_to([NH * NB, NH, HD]),
                                          const("headdiag", NH * NB).unsqueeze(2)
                                          .broadcast_to([NH * NB, NH, HD]), ALU.mult))
            chain.wait()
            chain(nc.vector.tensor_tensor(kc_sq, kc, kc, ALU.mult))
            chain.wait()
            nc.vector.tensor_reduce(kc_ss, kc_sq, AX.X, ALU.add).then_inc(ev("kc_ss_ready", ph)[0], 1)
            fill(3)
            wait(dve, "kc_rstd_ready", ph)
            chain(nc.vector.scalar_tensor_tensor(kc, kc, kc_ss, cmp_gain[0:2 * NB], ALU.mult, ALU.mult))
            chain.wait()
            cs, sn = const("coscmp", 2 * NB), const("sincmp", 2 * NB)
            for i, (half_, tab) in enumerate(((0, cs), (1, sn), (1, cs), (0, sn))):
                chain(nc.vector.tensor_tensor(kc_rot[:, 8 * i:8 * i + 8], kc[:, 8 * half_:8 * half_ + 8], tab,
                                              ALU.mult))
            chain.wait()
            nc.vector.tensor_tensor(kc[:, 0:8], kc_rot[:, 0:8], kc_rot[:, 8:16], ALU.subtract)
            nc.vector.tensor_tensor(kc[:, 8:16], kc_rot[:, 16:24], kc_rot[:, 24:32], ALU.add)\
                .then_inc(ev("kc_ready", ph)[0], 1)
            evac_items(dve, st, qk_items, 1)
            rope(dve, chain, proj[:, :, IQ:IW].rearrange("p t (h d) -> p t h d", d=IXD), IXH + 1, 4,
                 const("cos8"), const("sin8"), pb[:, 884:1268],
                 ev("ix_rope_ready", ph)[0])
            chain(nc.vector.tensor_scalar(ix_w, proj[:, :, IW:IW + IXH], IXH ** -0.5, IXD ** -0.5,
                                          ALU.mult, ALU.mult))
            wait(dve, "cmp_scores", ph)
            shape = [P, NT, NH, NB]
            vis = const("cmpvis").rearrange("p (t c) -> p t c", t=NT).unsqueeze(2).broadcast_to(shape)
            bias = const("cmpbias").rearrange("p (t c) -> p t c", t=NT).unsqueeze(2).broadcast_to(shape)
            sc = ps[:, CMP_BANK, 0:NT * NH * NB].rearrange("p (t h c) -> p t h c", t=NT, h=NH)
            chain(nc.vector.tensor_tensor(cmp_s, sc, bias, ALU.add))
            chain.wait()
            chain(nc.vector.tensor_reduce(cmp_max, cmp_s, AX.X, ALU.max))
            chain.wait()
            nc.vector.tensor_tensor(cmp_s, cmp_s, cmp_max.unsqueeze(3).broadcast_to(shape), ALU.subtract)\
                .then_inc(ev("cmp_shifted", ph)[0], 1)
            wait(dve, "cmp_exp", ph)
            chain(nc.vector.tensor_tensor(cmp_s, cmp_s, vis, ALU.mult))
            chain.wait()
            chain(nc.vector.tensor_reduce(cmp_den, cmp_s, AX.X, ALU.add))
            chain.wait()
            chain(nc.vector.tensor_scalar(cmp_zero, cmp_den, 0.0, None, ALU.is_equal))
            chain.wait()
            chain(nc.vector.tensor_tensor(cmp_den, cmp_den, cmp_zero, ALU.add))
            chain.wait()
            chain(nc.vector.reciprocal(cmp_den, cmp_den))
            chain.wait()
            nc.vector.tensor_tensor(cmp_s, cmp_s, cmp_den.unsqueeze(3).broadcast_to(shape), ALU.mult)\
                .then_inc(ev("cmp_p_ready", ph)[0], 1)
            fill(4)
            evac_items(dve, st, ix_items, 1)
            wait(dve, "cmp_out_ready", ph)
            for t in range(NT):
                chain(nc.vector.tensor_tensor(o_all[:, t, 256:768].rearrange("p (h d) -> p h d", h=NH),
                                              ps[:, CMP_BANK + t, :].rearrange("p (h d) -> p h d", h=NH),
                                              gates[:, t, :, 0].unsqueeze(2).broadcast_to([P, NH, HD]), ALU.mult))
            fill(5)
            tiles = (slice(0, P), slice(P, 3 * P))
            for h in range(IXH):
                dve.wait_ge(sem("ix_relu_ready"), IXH * li + h + 1)
                for t in range(NT):
                    r, w_ = ix_relu[h % 2][:, tiles[t]], ix_w[:, t, h:h + 1]
                    dst = ix_score[:, tiles[t]]
                    if h == 0:
                        last = nc.vector.tensor_scalar(dst, r, w_, None, ALU.mult)
                    else:
                        last = nc.vector.scalar_tensor_tensor(dst, r, w_, dst, ALU.mult, ALU.add)
                last.then_inc(sem("ix_added"), 1)
                dve.wait_ge(sem("ix_added"), IXH * li + h + 1)
            for c in (0, 2 * P):
                chain(nc.vector.tensor_tensor(ix_score[:, c:c + P], ix_score[:, c:c + P], const("causal"), ALU.add))
            chain.wait()
            def top_k_round(r):
                src = ix_score if r == 0 else ix_val
                for t in range(NT):
                    chain(nc.vector.max(top8[t], src[:, tiles[t]]))
                chain.wait()
                for t in range(NT):
                    chain(nc.vector.match_replace(ix_val[:, tiles[t]], top8[t], src[:, tiles[t]], TAKEN))
                chain.wait()

            def mask_from_taken():
                chain(nc.vector.tensor_scalar(ix_val, ix_val, TAKEN, -1.0, ALU.is_equal, ALU.add))
                chain.wait()
                chain(nc.vector.tensor_scalar(ix_val, ix_val, -NEG, None, ALU.mult))
                chain.wait()
                for c in (0, 2 * P):
                    chain(nc.vector.tensor_tensor(sel_mask[:, c:c + P], ix_val[:, c:c + P], const("causal"),
                                                  ALU.add))
                nc.vector.tensor_copy(sel_mask[:, P:2 * P], ix_val[:, P:2 * P])\
                    .then_inc(ev("mask_ready", ph)[0], 1)

            rounds_by = [0, 2, 4, 5, 7] + [TOPK // 8] * 6

            def beside(b):
                if b in mix2_fills:
                    fill(mix2_fills[b])
                for r in range(rounds_by[b], rounds_by[b + 1]):
                    top_k_round(r)
                if b > 0 and rounds_by[b] == TOPK // 8 and rounds_by[b - 1] < TOPK // 8:
                    mask_from_taken()
            dve_attention(dve, chain, attentions(ph), beside)
            dve.wait_ge(att_out, ph["B0"] + 10)
            for t in range(NT):
                nc.vector.tensor_copy(stats[:, 91 + t:92 + t], o_all[:, t, 0:1]).then_inc(xn_ready, 1)
            ahead(23)
            dve_transposed(dve, ph["t0"] + 1, 0)
            dve_transposed(dve, ph["t0"] + 1, 1)

            def gated(br, t):
                g_ = gate_or_gain[:, t, br * D:(br + 1) * D]
                bank = (0, 4, 0)[br] + 2 * t
                return nc.vector.tensor_tensor(g_, ps[:, bank:bank + 2, :].rearrange("p b n -> p (b n)"), g_, ALU.mult)
            dve.wait_ge(unit_used, u0 + 24)
            dve.wait_ge(sem("gate_sigmoid"), 3 * li + 1)
            for t in range(NT):
                gated(0, t).then_inc(sem("gated_a"), 1)
                if t == 0:
                    ahead(24)
            dve.wait_ge(sem("gate_sigmoid"), 3 * li + 3)
            for t in range(NT):
                if t == 0:
                    dve.wait_ge(sem("branches_t0_ready"), li + 1)
                else:
                    dve.wait_ge(unit_used, u0 + 27)
                gated(1, t).then_inc(sem("gated_b"), 1)
                gated(2, t).then_inc(sem("gated_c"), 1)
                dve.wait_ge(sem("gated_c"), 2 * li + t + 1)
                dve.wait_ge(sem("merged_ab"), 2 * li + t + 1)
                nc.vector.tensor_tensor(xn[:, t, :], xn[:, t, :], gate_or_gain[:, t, 2 * D:3 * D], ALU.add)\
                    .then_inc(xn_ready, 1)
                if t == 0:
                    ahead(25)
                dve_transposed(dve, ph["t0"] + 2, t)
                if t == 0:
                    ahead(26)
            ahead(27)
            ahead(28)
            ahead(29)

        block = ctx.enter_context(nc.Block())

        @block.sync
        def _(sp):
            for t in range(NT):
                sp.dma_start(x[:, t, :], A["x"][0, t * P:(t + 1) * P, :]).then_inc(x_loaded[t], 16)
                if t == 0:
                    sp.dma_start(ident, A["const_table"][:, 0:P]).then_inc(first_loaded, 16)
                    sp.dma_start(gains[:, :, :], A["gains"]).then_inc(first_loaded, 16)
            for ph in info:
                if ph["kind"] == "ffn":
                    sp_ffn(sp, ph)
                elif ph["kind"] == "mix1":
                    sp_mix1(sp, ph)
                else:
                    sp_mix2(sp, ph)
            for t in range(NT):
                sp.wait_ge(x_ready, n_x + t + 1)
                sp.dma_start(out[0, t * P:(t + 1) * P, :], x[:, t, :]).then_inc(stored, 16)
            sp.wait_ge(stored, 16 * NT)

        @block.gpsimd
        def _(pool):
            chain = Chain(pool, sem("pool_chain"))
            chain(nc.gpsimd.memset(minus_half, -0.5))
            chain.wait()
            n_const = consts.shape[1]
            pool.dma_start(consts[:, P:n_const], A["const_table"][:, P:n_const]).then_inc(const_loaded, 16)
            pool.dma_start(notpast, A["const_table"][:, n_const:n_const + P]).then_inc(const_loaded, 16)
            for prev, ph in zip([None] + info, info + [None]):
                pool_boundary(pool, chain, prev, ph)
                if ph is None:
                    break
                if ph["post"]:
                    if ph["post0"] > 0:
                        pool.wait_ge(x_ready, ph["x0"] + 2)
                    pool.dma_start(post_gain, A[ph["post"]][0].partition_broadcast(P))\
                        .then_inc(gain_loaded, 16)
                if ph["kind"] == "mix1":
                    pool_mix1(pool, chain, ph)
                if ph["kind"] == "mix2":
                    pool_mix2(pool, chain, ph)

        @block.tensor
        def _(pe):
            pe.wait_ge(first_loaded, 16 * 2)
            for ph in info:
                if ph["kind"] != "ffn":
                    pe.wait_ge(const_loaded, 16 * 2)
                    pe.wait_ge(sem("masks_ready"), 1)
                if ph["kind"] == "ffn":
                    pe_ffn(pe, ph)
                elif ph["kind"] == "mix1":
                    pe_mix1(pe, ph)
                else:
                    pe_mix2(pe, ph)

        @block.scalar
        def _(act):
            chain = Chain(act, sem("act_chain"))
            for prev, ph in zip([None] + info, info + [None]):
                act_boundary(act, prev, ph)
                if ph is None:
                    break
                if ph["kind"] == "ffn":
                    run_steps(act, ph, act_step)
                elif ph["kind"] == "mix1":
                    act_mix1(act, chain, ph)
                else:
                    act_mix2(act, chain, ph)

        @block.vector
        def _(dve):
            chain = Chain(dve, sem("dve_chain"))
            for t in range(NT):
                dve.wait_ge(x_loaded[t], 16)
                nc.vector.tensor_copy(stats[:, 93 + t:94 + t], x[:, t, 0:1]).then_inc(x_ready, 1)
            dve.wait_ge(first_loaded, 16 * 2)
            for prev, ph in zip([None] + info, info + [None]):
                dve_boundary(dve, chain, prev, ph)
                if ph is None:
                    break
                if prev is None:
                    dve.wait_ge(const_loaded, 16 * 2)
                    nc.vector.tensor_copy(ident_bf, ident)
                    nc.vector.tensor_copy(causal_bf, const("causal"))
                    nc.vector.tensor_copy(notpast_bf, notpast).then_inc(sem("masks_ready"), 1)
                if ph["kind"] == "ffn":
                    run_steps(dve, ph, dve_step)
                elif ph["kind"] == "mix1":
                    dve_mix1(dve, chain, ph)
                else:
                    dve_mix2(dve, chain, ph)


FFN = {"kind": "ffn", "gu": None, "post": None, "weight": 0.5}
PLAN = [
    {**FFN, "l": 0, "gate": "ffn1_w_gate", "up": "ffn1_w_up", "down": "ffn1_w_down", "post": "ffn1_post_g",
     "gain": 0},
    {"kind": "mix1", "l": 0, "gain": 1, "post": "mix_post_g", "weight": 1.0},
    {**FFN, "l": 0, "gate": "ffn2_w_gate", "up": "ffn2_w_up", "down": "ffn2_w_down", "post": "ffn2_post_g",
     "gain": 2},
]
GAINS = [("ffn1_pre_g", 0), ("mix_pre_g", 0), ("ffn2_pre_g", 0)]
for _l in range(2):
    PLAN += [
        {**FFN, "l": _l, "gu": "ffn1_w_gu_2", "down": "ffn1_w_down_2", "gain": 3 + 3 * _l},
        {"kind": "mix2", "l": _l, "gain": 4 + 3 * _l, "post": None, "weight": 1.0},
        {**FFN, "l": _l, "gu": "ffn2_w_gu_2", "down": "ffn2_w_down_2", "gain": 5 + 3 * _l},
    ]
    GAINS += [("ffn1_norm_2", _l), ("mix_norm_2", _l), ("ffn2_norm_2", _l)]
NGAIN = len(GAINS)
UNITS1 = 17
UNITS2 = 31


def kernel(**inputs):
    from concourse import bacc
    from concourse.bass_utils import run_bass_kernel_spmd

    nc = bacc.Bacc("TRN2", target_bir_lowering=False, num_devices=1)
    const_table, place = const_arrays()
    arrays = {k: np.ascontiguousarray(v) for k, v in inputs.items()}
    arrays["gains"] = np.ascontiguousarray(
        np.stack([arrays[name][l].reshape(KC, P) for name, l in GAINS]).transpose(2, 0, 1))
    arrays["cmp_pe"] = np.ascontiguousarray(
        arrays["nsa_cmp_pe_2"].reshape(2, 2, 16, 2, HD).transpose(0, 1, 3, 4, 2).reshape(2, 2, P, 16))
    arrays["const_table"] = const_table
    A = {k: nc.dram_tensor("in_" + k, v.shape, mybir.dt.from_np(v.dtype), kind="ExternalInput").ap()
         for k, v in arrays.items()}
    out = nc.dram_tensor("out_0", (1, S, D), F32, kind="ExternalOutput").ap()
    build(nc, A, place, out)
    r = run_bass_kernel_spmd(nc, [{"in_" + k: v for k, v in arrays.items()}], core_ids=[0])
    return r.results[0]["out_0"]
```
